# Optimizing a Trainium2 kernel written in Bass

```python
import jax, jax.numpy as jnp
from jax import lax
import numpy as np

D_MODEL = 1024
BATCH = 1
SEQ = 256
DEPTH = 1
DEC_BATCH = 8
DEC_SEQ = 16
PAST_LEN = 256

CHUNK = 64
D_MIX = D_MODEL
GDN_HEADS = 4
GDN_HEAD_DIM = 128
GDN_WIDTH = GDN_HEADS * GDN_HEAD_DIM
QKV_CONV_WIDTH = 4
CONF_WIDTH = D_MIX - GDN_WIDTH
DW_CONV_WIDTH = 31
N_EXPERTS = 32
TOP_K = 4
D_EXPERT = 1024
SWIGLU_LIMIT = 7.0
SWIGLU_ALPHA = 1.702
MOE_BLOCK = 128
RMS_EPS = 1e-6
LN_EPS = 1e-5
L2_EPS = 1e-6
QKV_COLS = 3 * GDN_WIDTH
Z_COLS = GDN_WIDTH
BETA_COLS = GDN_HEADS
DECAY_COLS = GDN_HEADS
GLU_COLS = 2 * CONF_WIDTH
D_IN_PROJ = QKV_COLS + Z_COLS + BETA_COLS + DECAY_COLS + GLU_COLS
SPLITS = (QKV_COLS, QKV_COLS + Z_COLS, QKV_COLS + Z_COLS + BETA_COLS,
          QKV_COLS + Z_COLS + BETA_COLS + DECAY_COLS)

kernel_name = "hymba_gdn_conformer_moe_stream_step"

def rms_norm(x, g):
    xf = x.astype(jnp.float32)
    y = xf * lax.rsqrt(jnp.mean(xf * xf, axis=-1, keepdims=True) + RMS_EPS)
    return (y * g.astype(jnp.float32)).astype(x.dtype)

def layer_norm(x, g, b):
    xf = x.astype(jnp.float32)
    xc = xf - jnp.mean(xf, axis=-1, keepdims=True)
    y = xc * lax.rsqrt(jnp.mean(xc * xc, axis=-1, keepdims=True) + LN_EPS)
    return (y * g.astype(jnp.float32) + b.astype(jnp.float32)).astype(x.dtype)

def l2_normalize(x):
    xf = x.astype(jnp.float32)
    return (xf * lax.rsqrt(jnp.sum(xf * xf, axis=-1, keepdims=True) + L2_EPS)).astype(x.dtype)

def causal_dwconv(x_ext, w):
    c = w.shape[1]
    return lax.conv_general_dilated(
        x_ext, w[:, None, :].astype(x_ext.dtype), window_strides=(1,), padding='VALID',
        dimension_numbers=('NWC', 'WIO', 'NWC'), feature_group_count=c)

def gated_delta_chunked(q, k, v, g, beta, s0, chunk):
    bsz, t, nh, dk = q.shape
    dv = v.shape[-1]
    n = t // chunk
    f32 = jnp.float32

    def to_chunks(a):
        a = a.astype(f32).reshape((bsz, n, chunk, nh) + a.shape[3:])
        return jnp.moveaxis(a, (1, 3), (0, 2))

    qc, kc, vc, bc = to_chunks(q), to_chunks(k), to_chunks(v), to_chunks(beta)
    gc = jnp.cumsum(to_chunks(g), axis=-1)
    pos = jnp.arange(chunk)
    causal = pos[:, None] >= pos[None, :]
    decay = jnp.exp(jnp.where(causal, gc[..., :, None] - gc[..., None, :], -jnp.inf))
    kb = kc * bc[..., None]
    m = jnp.einsum('nbhik,nbhjk->nbhij', kb, kc) * jnp.where(pos[:, None] > pos[None, :], decay, 0.0)
    lhs = jnp.eye(chunk, dtype=f32) + m
    rhs = jnp.concatenate([vc * bc[..., None], kb * jnp.exp(gc)[..., None]], axis=-1)
    sol = lax.linalg.triangular_solve(lhs, rhs, left_side=True, lower=True, unit_diagonal=True)
    u, w = sol[..., :dv], sol[..., dv:]

    def step(s, inp):
        q_i, k_i, u_i, w_i, g_i, d_i = inp
        v_new = u_i - jnp.einsum('bhck,bhkv->bhcv', w_i, s)
        o_i = (jnp.einsum('bhck,bhkv->bhcv', q_i * jnp.exp(g_i)[..., None], s)
               + jnp.einsum('bhij,bhjv->bhiv', jnp.einsum('bhik,bhjk->bhij', q_i, k_i) * d_i, v_new))
        g_last = g_i[..., -1:]
        s = (s * jnp.exp(g_last)[..., None]
             + jnp.einsum('bhck,bhcv->bhkv', k_i * jnp.exp(g_last - g_i)[..., None], v_new))
        return s, o_i

    s_fin, o = lax.scan(step, s0.astype(f32), (qc, kc, u, w, gc, decay))
    o = jnp.moveaxis(o, (0, 2), (1, 3)).reshape(bsz, t, nh, dv)
    return o.astype(q.dtype), s_fin.astype(s0.dtype)

def token_mixers(h, qkv_hist, s0, glu_hist, w_in, w_conv_qkv, a_log, dt_bias, w_onorm,
                 b_glu, w_dw, b_dw, ln_g, ln_b, w_out, chunk):
    bsz, t, _ = h.shape
    proj = jnp.einsum('btd,de->bte', h, w_in)
    qkv, z, b_beta, a_dec, glu = jnp.split(proj, SPLITS, axis=-1)

    qkv_ext = jnp.concatenate([qkv_hist.astype(qkv.dtype), qkv], axis=1)
    new_qkv_hist = qkv_ext[:, -(QKV_CONV_WIDTH - 1):]
    qkv = jax.nn.silu(causal_dwconv(qkv_ext, w_conv_qkv))
    q, k, v = jnp.split(qkv, 3, axis=-1)
    q = l2_normalize(q.reshape(bsz, t, GDN_HEADS, GDN_HEAD_DIM)) * (GDN_HEAD_DIM ** -0.5)
    k = l2_normalize(k.reshape(bsz, t, GDN_HEADS, GDN_HEAD_DIM))
    v = v.reshape(bsz, t, GDN_HEADS, GDN_HEAD_DIM)
    beta = jax.nn.sigmoid(b_beta.astype(jnp.float32))
    g = -jnp.exp(a_log.astype(jnp.float32)) * jax.nn.softplus(
        a_dec.astype(jnp.float32) + dt_bias.astype(jnp.float32))
    o, s_new = gated_delta_chunked(q, k, v, g, beta, s0, chunk)
    o = rms_norm(o, w_onorm) * jax.nn.silu(z.reshape(bsz, t, GDN_HEADS, GDN_HEAD_DIM))
    o = o.reshape(bsz, t, GDN_WIDTH)

    glu = glu + b_glu
    ga, gb = jnp.split(glu, 2, axis=-1)
    uu = ga * jax.nn.sigmoid(gb)
    u_ext = jnp.concatenate([glu_hist.astype(uu.dtype), uu], axis=1)
    new_glu_hist = u_ext[:, -(DW_CONV_WIDTH - 1):]
    c = causal_dwconv(u_ext, w_dw) + b_dw
    c = jax.nn.silu(layer_norm(c, ln_g, ln_b))

    out = jnp.einsum('bte,ed->btd', jnp.concatenate([o, c], axis=-1), w_out)
    return out, s_new, new_qkv_hist, new_glu_hist

def moe_ffn(h, w_router, b_router, w_gate_up, b_gate_up, w_down, b_down):
    n_tok, d = h.shape
    logits = jnp.dot(h.astype(jnp.float32), w_router.astype(jnp.float32)) + b_router.astype(jnp.float32)
    top_val, top_idx = lax.top_k(logits, TOP_K)
    gates = jax.nn.softmax(top_val, axis=-1).astype(h.dtype)
    n_assign = n_tok * TOP_K
    flat_e = top_idx.reshape(-1).astype(jnp.int32)
    flat_tok = jnp.arange(n_assign, dtype=jnp.int32) // TOP_K
    order = jnp.argsort(flat_e)
    sorted_e = flat_e[order]
    counts = jnp.bincount(flat_e, length=N_EXPERTS).astype(jnp.int32)
    padded = (counts + MOE_BLOCK - 1) // MOE_BLOCK * MOE_BLOCK
    padded_end = jnp.cumsum(padded)
    padded_start = padded_end - padded
    start = jnp.cumsum(counts) - counts
    dest = padded_start[sorted_e] + jnp.arange(n_assign, dtype=jnp.int32) - start[sorted_e]
    n_blocks = -(-n_assign // MOE_BLOCK) + N_EXPERTS
    n_rows = n_blocks * MOE_BLOCK
    row_tok = jnp.full((n_rows,), n_tok, jnp.int32).at[dest].set(flat_tok[order])
    row_gate = jnp.zeros((n_rows,), h.dtype).at[dest].set(gates.reshape(-1)[order])
    block_expert = jnp.minimum(
        jnp.searchsorted(padded_end, jnp.arange(n_blocks, dtype=jnp.int32) * MOE_BLOCK, side='right'),
        N_EXPERTS - 1)
    h_pad = jnp.concatenate([h, jnp.zeros((1, d), h.dtype)], axis=0)
    xb = h_pad[row_tok].reshape(n_blocks, MOE_BLOCK, d)

    def expert_block(args):
        xblk, e = args
        gu = xblk @ w_gate_up[e] + b_gate_up[e]
        x_glu, x_lin = jnp.split(gu, 2, axis=-1)
        x_glu = jnp.minimum(x_glu, SWIGLU_LIMIT)
        x_lin = jnp.clip(x_lin, -SWIGLU_LIMIT, SWIGLU_LIMIT)
        act = x_glu * jax.nn.sigmoid(SWIGLU_ALPHA * x_glu) * (x_lin + 1.0)
        return act @ w_down[e] + b_down[e]

    yb = lax.map(expert_block, (xb, block_expert))
    y = jnp.zeros((n_tok + 1, d), h.dtype).at[row_tok].add(yb.reshape(n_rows, d) * row_gate[:, None])
    return y[:n_tok]

def encoder_layer(x, qkv_hist, s0, glu_hist, norm_mix_g, w_in, w_conv_qkv, a_log, dt_bias, w_onorm,
                  b_glu, w_dw, b_dw, ln_g, ln_b, w_out, norm_ffn_g, w_router, b_router,
                  w_gate_up, b_gate_up, w_down, b_down, chunk):
    h = rms_norm(x, norm_mix_g)
    mix, s_new, qkv_new, glu_new = token_mixers(h, qkv_hist, s0, glu_hist, w_in, w_conv_qkv, a_log,
                                                dt_bias, w_onorm, b_glu, w_dw, b_dw, ln_g, ln_b,
                                                w_out, chunk)
    x = x + mix
    h = rms_norm(x, norm_ffn_g)
    ff = moe_ffn(h.reshape(-1, h.shape[-1]), w_router, b_router, w_gate_up, b_gate_up, w_down, b_down)
    x = x + ff.reshape(x.shape)
    return x, s_new, qkv_new, glu_new

def setup_inputs(seed: int = 0) -> dict:
    key = jax.random.key(seed)
    ks = jax.random.split(key, 32)
    f32 = jnp.float32
    nrm = lambda k, shape, s: jax.random.normal(k, shape, f32) * s
    dt = jnp.exp(jax.random.uniform(ks[10], (DEPTH, GDN_HEADS), f32, np.log(1e-3), np.log(1e-1)))
    return {
        "x_prompt": nrm(ks[0], (BATCH, SEQ, D_MODEL), 1.0),
        "x_sample": nrm(ks[1], (DEC_BATCH, DEC_SEQ, D_MODEL), 1.0),
        "state_gdn": nrm(ks[2], (DEPTH, DEC_BATCH, GDN_HEADS, GDN_HEAD_DIM, GDN_HEAD_DIM), 0.1),
        "state_qkv_conv": nrm(ks[3], (DEPTH, DEC_BATCH, QKV_CONV_WIDTH - 1, QKV_COLS), 1.0),
        "state_dwconv": nrm(ks[4], (DEPTH, DEC_BATCH, DW_CONV_WIDTH - 1, CONF_WIDTH), 0.5),
        "norm_mix_g": 1.0 + nrm(ks[5], (DEPTH, D_MODEL), 0.02),
        "w_in": nrm(ks[6], (DEPTH, D_MODEL, D_IN_PROJ), D_MODEL ** -0.5),
        "w_conv_qkv": nrm(ks[7], (DEPTH, QKV_CONV_WIDTH, QKV_COLS), QKV_CONV_WIDTH ** -0.5),
        "a_log": jnp.log(jax.random.uniform(ks[8], (DEPTH, GDN_HEADS), f32, 1.0, 16.0)),
        "dt_bias": dt + jnp.log(-jnp.expm1(-dt)),
        "w_onorm": 1.0 + nrm(ks[9], (DEPTH, GDN_HEAD_DIM), 0.02),
        "b_glu": nrm(ks[11], (DEPTH, GLU_COLS), 0.02),
        "w_dw": nrm(ks[12], (DEPTH, DW_CONV_WIDTH, CONF_WIDTH), DW_CONV_WIDTH ** -0.5),
        "b_dw": nrm(ks[13], (DEPTH, CONF_WIDTH), 0.02),
        "ln_g": 1.0 + nrm(ks[14], (DEPTH, CONF_WIDTH), 0.02),
        "ln_b": nrm(ks[15], (DEPTH, CONF_WIDTH), 0.02),
        "w_out": nrm(ks[16], (DEPTH, D_MIX, D_MODEL), D_MIX ** -0.5),
        "norm_ffn_g": 1.0 + nrm(ks[17], (DEPTH, D_MODEL), 0.02),
        "w_router": nrm(ks[18], (DEPTH, D_MODEL, N_EXPERTS), D_MODEL ** -0.5),
        "b_router": nrm(ks[19], (DEPTH, N_EXPERTS), 0.01),
        "w_gate_up": nrm(ks[20], (DEPTH, N_EXPERTS, D_MODEL, 2 * D_EXPERT), D_MODEL ** -0.5),
        "b_gate_up": nrm(ks[21], (DEPTH, N_EXPERTS, 2 * D_EXPERT), 0.01),
        "w_down": nrm(ks[22], (DEPTH, N_EXPERTS, D_EXPERT, D_MODEL), D_EXPERT ** -0.5),
        "b_down": nrm(ks[23], (DEPTH, N_EXPERTS, D_MODEL), 0.01),
        "norm_final_g": 1.0 + nrm(ks[24], (D_MODEL,), 0.02),
    }

def reference(x_prompt, x_sample, state_gdn, state_qkv_conv, state_dwconv, norm_mix_g, w_in,
              w_conv_qkv, a_log, dt_bias, w_onorm, b_glu, w_dw, b_dw, ln_g, ln_b, w_out,
              norm_ffn_g, w_router, b_router, w_gate_up, b_gate_up, w_down, b_down, norm_final_g):
    bp = x_prompt.shape[0]
    xp, xs = x_prompt, x_sample
    sp_l, qp_l, gp_l, ss_l, qs_l, gs_l = [], [], [], [], [], []
    for l in range(DEPTH):
        lw = (norm_mix_g[l], w_in[l], w_conv_qkv[l], a_log[l], dt_bias[l], w_onorm[l], b_glu[l],
              w_dw[l], b_dw[l], ln_g[l], ln_b[l], w_out[l], norm_ffn_g[l], w_router[l], b_router[l],
              w_gate_up[l], b_gate_up[l], w_down[l], b_down[l])
        zero_qkv = jnp.zeros((bp, QKV_CONV_WIDTH - 1, QKV_COLS), xp.dtype)
        zero_s = jnp.zeros((bp, GDN_HEADS, GDN_HEAD_DIM, GDN_HEAD_DIM), state_gdn.dtype)
        zero_glu = jnp.zeros((bp, DW_CONV_WIDTH - 1, CONF_WIDTH), xp.dtype)
        xp, sp, qp, gp = encoder_layer(xp, zero_qkv, zero_s, zero_glu, *lw, chunk=CHUNK)
        xs, ss, qs, gs = encoder_layer(xs, state_qkv_conv[l], state_gdn[l], state_dwconv[l], *lw,
                                       chunk=xs.shape[1])
        sp_l.append(sp); qp_l.append(qp); gp_l.append(gp)
        ss_l.append(ss); qs_l.append(qs); gs_l.append(gs)
    y_prompt = rms_norm(xp, norm_final_g)
    y_sample = rms_norm(xs, norm_final_g)
    return (y_prompt, y_sample, jnp.stack(sp_l), jnp.stack(qp_l), jnp.stack(gp_l),
            jnp.stack(ss_l), jnp.stack(qs_l), jnp.stack(gs_l))


_drawn_inputs = setup_inputs


def setup_inputs(seed=0):
    import zlib

    import numpy as np

    out = dict(_drawn_inputs(seed))
    spreads = {}
    factors = {'b_gate_up': 8.0, 'b_down': 8.0, 'norm_final_g': 2.842}
    for name, (base, spread) in spreads.items():
        noise = np.random.default_rng([zlib.crc32(name.encode()), seed]).standard_normal(out[name].shape)
        drawn = base * np.exp(spread * noise) if base else spread * noise
        out[name] = __import__('jax').numpy.asarray(drawn.astype(out[name].dtype))
    for name, factor in factors.items():
        out[name] = (out[name] * factor).astype(out[name].dtype)
    return out
```

```python
from contextlib import ExitStack

import numpy as np

import concourse.bass as bass
from concourse import mybir

F32 = mybir.dt.float32
BF16 = mybir.dt.bfloat16
I32 = mybir.dt.int32
U32 = mybir.dt.uint32
ALU = mybir.AluOpType
ACT = mybir.ActivationFunctionType
AX_X = mybir.AxisListType.X

P = 128
D = 1024
KD = D // P
NT = 3
T = NT * P
TP = 256
NB, TS = 8, 16
H = 4
QW, DW = 4, 31
QC, CC = 12, 4
QE = QW - 1 + TP + NB * (QW - 1 + TS)
UE = DW - 1 + TP + NB * (DW - 1 + TS)
QS, US = QW - 1 + TP, DW - 1 + TP
NE, TOPK = 32, 4
F = 1024
BLK = 64
NX = (T * TOPK) // (BLK + 1)
NSLOT = 12
SLOT = 2 * F
RMS_EPS, LN_EPS, L2_EPS = 1e-6, 1e-5, 1e-6
LIMIT, ALPHA = 7.0, 1.702
NPAIR = NE // 2
LEVELS = 7
S_LEVELS = 4

C_Z, C_BA, C_GA, C_GB = 1536, 2048, 2056, 2568
CHUNKS = (C_GA, C_GB, 0, 512, 1024, C_Z)

MATS = ["ident", "ones", "incl_p", "incl_s", "later_p", "later_s", "strict"] + [f"level{l}" for l in range(LEVELS)]
M = {name: i for i, name in enumerate(MATS)}
X_IOTA, X_BLK, X_SEL = 0, 64, 64 + NB
NXC = 64 + NB + NE + 1
PARAMS, _at = {}, 0
for _name, _n in (("g_mix", KD), ("conv", QW * QC), ("dw", DW * CC), ("b_glu", 2 * CC), ("b_dw", CC), ("ln_g", CC),
                  ("ln_b", CC), ("onorm", 1), ("a_log", H), ("dt", H), ("b_router", NE)):
    PARAMS[_name] = _at
    _at += _n
NPARAM = _at


class Count:

    def __init__(self, sem):
        self.sem, self.n = sem, 0

    def inc(self, ins):
        self.n += 1
        ins.then_inc(self.sem, 1)
        return self.n


def stream_step(nc, xT, x_prompt, x_sample, state_gdn, hist_q, hist_u, params, consts, w_in, w_out, g_ffn,
                g_final, w_router, w_gate_up, b_gate_up, w_down, b_down,
                y_out, sp_out, ss_out, q_state_out, u_state_out):
    h2_dram = nc.dram_tensor("h2_rows", (T, D), F32, kind="Internal").ap()
    y_dram = nc.dram_tensor("expert_rows", ((NE + NX) * BLK, D), F32, kind="Internal").ap()

    with ExitStack() as ctx:
        def sb(name, shape, dt=F32):
            return ctx.enter_context(nc.sbuf_tensor(name, shape, dt))

        def sem(name):
            return ctx.enter_context(nc.semaphore(name))

        ring = sb("ring", [P, NSLOT * SLOT])
        mats = sb("mats", [P, len(MATS) * P])
        cst = sb("cst", [P, NXC])
        par = sb("par", [P, NPARAM])
        win = sb("win", [P, 2 * KD * 512])
        hT = sb("hT", [P, KD * T])
        xt = sb("xt", [P, NT * D])
        qkvc = sb("qkvc", [P, QC * T])
        zs = sb("zs", [P, CC * T])
        cb = sb("cb", [P, CC * T])
        oT = sb("oT", [P, CC * T])
        qst = sb("qst", [P, QC * 9 * 3])
        ust = sb("ust", [P, CC * 9 * 30])
        gff = sb("gff", [P, D])
        gates_t = sb("gates_t", [P, 12 * 12])
        epst = sb("epst", [P, 12])
        bank = [ctx.enter_context(nc.psum_tensor(f"bank{i}", [P, 512], F32))[:, :] for i in range(8)]

        def mat(name):
            return mats[:, M[name] * P:(M[name] + 1) * P]

        def mat4(name):
            return mat(name).unsqueeze(1).to_broadcast([P, H, P])

        def col(name, i=0, n=1):
            return par[:, PARAMS[name] + i:PARAMS[name] + i + n]

        at = [0]

        def scratch(n):
            at[0] += n
            assert at[0] <= NSLOT * SLOT
            return ring[:, at[0] - n:at[0]]

        qx = scratch(QE * QC)
        s_smp = scratch(NB * H * P)
        gB_ = scratch(T * H)
        eg_ = scratch(T * H)
        d_ = scratch(T * H)
        e_ = scratch(T * H)
        x_ = scratch(T * H)
        lt_ = scratch(T * H)
        mt_ = scratch(T * H)
        at_ = scratch(T * H)
        s_prm = scratch(H * P)
        vnew = scratch(H * P)
        onrm = scratch(H * P)
        qx3 = qx.rearrange("p (c e) -> p c e", c=QC)
        ux3 = ring[:, QE * QC + NB * H * P + 2 * T * H:][:, 0:UE * CC].rearrange("p (c e) -> p c e", c=CC)
        base_lt = QE * QC + NB * H * P + 5 * T * H
        sq3 = ring[:, base_lt:base_lt + KD * T].rearrange("p (k t) -> p k t", k=KD)
        rB = at_[:, 0:T]
        base_gB = QE * QC + NB * H * P
        rn3 = ring[:, base_gB:base_gB + KD * T].rearrange("p (k t) -> p k t", k=KD)
        vb_, kbe_, kd_ = qx[:, 0:T * H], qx[:, T * H:2 * T * H], qx[:, 2 * T * H:3 * T * H]

        def tile4(x, n):
            return x[:, n * 512:(n + 1) * 512].rearrange("p (h t) -> p h t", h=H)

        def flat(x, n):
            return x[:, n * 512:(n + 1) * 512]

        hT3 = hT[:].rearrange("p (k t) -> p k t", k=KD)
        qkv3 = qkvc[:].rearrange("p (c t) -> p c t", c=QC)
        zs3 = zs[:].rearrange("p (c t) -> p c t", c=CC)
        cb3 = cb[:].rearrange("p (c t) -> p c t", c=CC)
        oT3 = oT[:].rearrange("p (c t) -> p c t", c=CC)
        win4 = win[:].rearrange("p (b k n) -> p b k n", b=2, k=KD)
        hu = cb[:, 0:CC * NB * 30].rearrange("p (c b j) -> p c b j", c=CC, b=NB)
        hq = cb[:, CC * NB * 30:CC * NB * 30 + QC * NB * 3].rearrange("p (c b j) -> p c b j", c=QC, b=NB)
        xt3 = xt[:].rearrange("p (n d) -> p n d", n=NT)
        gcol = [gates_t[:, 12 * i:12 * i + 12] for i in range(12)]
        (y_, ab_, e1_, l1_, bl_, beta, g_, gc, ec, bec, ed, ea) = gcol

        h2 = qkvc[:, 0:NT * D]
        h23 = h2.rearrange("p (n d) -> p n d", n=NT)
        xg = qkvc[:, NT * D:NT * D + D]
        actT = qkvc[:, NT * D + D:NT * D + D + 512]
        at2 = [0]

        def wscratch(n):
            at2[0] += n
            assert at2[0] <= 2 * KD * 512
            return win[:, at2[0] - n:at2[0]]

        hitf = wscratch(NT * NE * BLK // 2)
        hit = hitf.bitcast(BF16).rearrange("p (n e s) -> p n e s", n=NT, e=NE)
        xTe = wscratch(KD * P).rearrange("p (k s) -> p k s", k=KD)
        g_s, l_s, sg_b, t_s, a_s = (wscratch(512) for _ in range(5))
        y_s = [wscratch(512) for _ in range(2)]
        hito = wscratch(NT * BLK // 2).bitcast(BF16).rearrange("p (n s) -> p n s", n=NT)
        bparts = zs[:, 0:3 * F // 2].bitcast(BF16)
        small = oT[:, :]
        sm = [0]

        def srow(n):
            sm[0] += n
            assert sm[0] <= CC * T
            return small[:, sm[0] - n:sm[0]]

        wr = ust[:, 0:KD * NE].rearrange("p (k e) -> p k e", k=KD)
        lg = srow(NT * NE).rearrange("p (n e) -> p n e", n=NT)
        v8 = srow(NT * 8).rearrange("p (n j) -> p n j", n=NT)
        i8 = srow(NT * 8).rearrange("p (n j) -> p n j", n=NT)
        if8 = srow(NT * 8).rearrange("p (n j) -> p n j", n=NT)
        gate = srow(NT * TOPK).rearrange("p (n j) -> p n j", n=NT)
        gsum = srow(NT)
        nv0 = srow(NT)
        mall = srow(NT * NE).rearrange("p (n e) -> p n e", n=NT)
        pos = srow(NE * NT).rearrange("p (e n) -> p e n", n=NT)
        posj = srow(NT * TOPK).rearrange("p (n j) -> p n j", n=NT)
        rowi = srow(NT * TOPK).bitcast(I32).rearrange("p (n j) -> p n j", n=NT)
        cntB = srow(NE)
        nxb = srow(NE)
        cumA, cumB = srow(NE), srow(NE)
        cmpx = cb[:, 0:NX * NE].rearrange("p (i e) -> p i e", i=NX)
        ex = srow(NX)
        stx = srow(NX)
        movej = srow(NT * TOPK).rearrange("p (n j) -> p n j", n=NT)
        pick, pick2 = (x.rearrange("p (n j e) -> p n j e", n=NT, j=TOPK) for x in (
            cb[:, NX * NE:NX * NE + NT * TOPK * NE], hT[:, 0:NT * TOPK * NE]))
        off64 = srow(NX)
        tab = srow(NX + 1).bitcast(I32)
        idxf = srow(NPAIR)
        idx = srow(NPAIR).bitcast(I32)
        idx_cur = srow(1).bitcast(I32)
        idxof = srow(1)
        idxo = srow(1).bitcast(I32)
        pcur = srow(NT)
        ssq = epst[:, 4:4 + NT]
        tokf = srow(NT)
        sel_sb = srow(BLK).bitcast(BF16).rearrange("p (x s) -> p x s", x=2)
        tok2 = srow(NT).bitcast(BF16).rearrange("p (n c) -> p n c", n=NT)
        rr = epst[:, 8:8 + NT]

        s_xT, s_cst, s_par, s_hist, s_state = (sem(x) for x in ("xT_in", "consts_in", "params_in", "hist_in", "state_in"))
        s_win = [sem(f"win_in{i}") for i in range(2)]
        s_ba_in, s_xt, s_gff, s_wr = sem("ba_in"), sem("x_in"), sem("gffn_in"), sem("router_in")
        s_bias, s_gfin = sem("bias_in"), sem("gfinal_in")
        s_ext = sem("histories_placed")
        s_eps = sem("eps_set")
        s_sq, s_ssum, s_rt, s_h = sem("x_squared"), sem("x_sum"), sem("x_root"), sem("hT_ready")
        s_proj, s_evac = sem("proj_ready"), sem("proj_taken")
        s_ba, s_bag, s_bae, s_gates = sem("ba_ready"), sem("ba_taken"), sem("ba_scalar"), sem("g_ready")
        s_cs, s_cse, s_bec = sem("cumsum_ready"), sem("cumsum_exp"), sem("beta_exp_ready")
        s_u, s_cv, s_dwc = sem("u_ready"), sem("qkv_conv"), sem("dw_conv")
        s_silu = sem("qkv_silu")
        s_n, s_nroot, s_nrm = sem("norm_sums"), sem("norm_roots"), sem("qk_normed")
        s_st = sem("conv_states_staged")
        s_ln, s_xc, s_lsq, s_ln2, s_lroot, s_lnd, s_conf = (sem(x) for x in (
            "ln_sum", "ln_centred", "ln_squared", "ln_sum2", "ln_root", "ln_scaled", "conformer_ready"))
        s_a1, s_gBc, s_dif, s_dT, s_a1d = (sem(x) for x in ("gram_ready", "decay_rows", "decay_diff", "decay_exp", "gram_taken"))
        s_lt, s_e1, s_tr, s_d1 = sem("level_rows"), sem("inverse_start"), sem("inverse_T"), sem("inverse_T_taken")
        s_x, s_xs, s_pq, s_de = sem("level_x"), sem("level_x_taken"), sem("level_pq"), sem("level_done")
        s_vk, s_vke = sem("vk_turned"), sem("vk_taken")
        s_wt, s_wte, s_v, s_ve = sem("w_ready"), sem("w_taken"), sem("vnew_ready"), sem("vnew_taken")
        s_qg, s_t1, s_t1e = sem("q_decayed"), sem("stream_terms"), sem("stream_terms_taken")
        s_o, s_osq, s_ort, s_on = sem("o_ready"), sem("o_squared"), sem("o_root"), sem("o_normed")
        s_ot, s_oTd = sem("o_turned"), sem("oT_ready")
        s_s, s_sd, s_km = sem("state_ready"), sem("state_taken"), sem("k_masked")
        s_mix, s_x2, s_x2q, s_x2r, s_h2, s_h2st = (sem(x) for x in (
            "mix_ready", "x2_ready", "x2_squared", "x2_root", "h2_ready", "h2_stored"))
        s_h2t, s_h2te = sem("h2_turned"), sem("h2T_ready")
        s_lg, s_gx, s_ge = sem("logits_ready"), sem("gate_max"), sem("gate_exp")
        s_m, s_pp, s_tok, s_hit, s_id, s_idx = (sem(x) for x in (
            "mask_ready", "places_ready", "token_ids", "hits_ready", "index_sums", "index_ready"))
        s_tabs = sem("tables_ready")
        s_w = [sem(f"w_landed{i}") for i in range(NSLOT)]
        s_wu = sem("w_used")
        s_icur, s_gat, s_xgt, s_xte = sem("index_cur"), sem("gathered"), sem("rows_turned"), sem("rowsT_ready")
        s_sel, s_gu, s_g, s_sig, s_act = (sem(x) for x in ("sel_ready", "gu_ready", "gate_clamped", "sig_ready", "act_ready"))
        s_att, s_atr, s_dn, s_yc = sem("act_turned"), sem("actT_ready"), sem("down_ready"), sem("y_copied")
        s_ys = [sem(f"y_stored{i}") for i in range(2)]
        s_hito, s_ido, s_idxo = sem("hits_extra"), sem("index_sums_extra"), sem("index_extra")
        s_xdone = sem("extra_done")
        s_yg, s_acc = [sem(f"y_gathered{i}") for i in range(NT)], sem("y_ready")
        s_fin = sem("final_squared")
        s_frt = sem("final_root")
        s_stq = sem("states_out")
        s_yout = sem("y_out_stored")
        s_zero, s_zeroed, s_row = sem("zeros_set"), sem("zero_rows_stored"), sem("rows_known")
        s_xrows, s_go = sem("extra_rows_stored"), sem("gather_may_go")
        s_lin, s_pc, s_ix1 = sem("linear_ready"), sem("places_extra"), sem("index_part")
        s_dve, s_act_o, s_pool = sem("vector_order"), sem("scalar_order"), sem("pool_order")
        s_scr = sem("scratch_free")
        s_sout, s_ssout = sem("prompt_state_out"), sem("sample_state_out")

        JOBS = [("ga", c) for c in range(CC)] + [("gb", c) for c in range(CC)] + \
               [("qkv", c) for c in range(QC)] + [("z", c) for c in range(CC)]
        NJ = len(JOBS)
        NN = 2 * H
        TILES = range(NT)

        def levels():
            for l in range(1, LEVELS):
                yield l, [n for n in TILES if n < 2 or l < S_LEVELS]

        LT_AT, DE_AT, k_, x2_ = {}, {}, 0, 0
        for l_, ns_ in levels():
            for n_ in ns_:
                k_ += 1
                LT_AT[l_, n_] = k_
        N_STEPS = k_

        block = ctx.enter_context(nc.Block())

        @block.sync
        def _(sp):
            sp.dma_start(hT3, xT.rearrange("(k p) t -> p k t", p=P)).then_inc(s_xT, 16)

            def load_win(i):
                c = CHUNKS[i]
                if i >= 2:
                    sp.wait_ge(s_proj, 4 * (i - 1))
                sp.dma_start(win4[:, i % 2], w_in[:, c:c + 512].rearrange("(k p) n -> p k n", p=P))\
                  .then_inc(s_win[i % 2], 16)

            load_win(0)
            sp.dma_start(gff[:, 0:KD * 8].rearrange("p (k n) -> p k n", k=KD),
                         w_in[:, C_BA:C_BA + 8].rearrange("(k p) n -> p k n", p=P),
                         allow_slow_non_contiguous=True).then_inc(s_ba_in, 16)
            for i in range(1, len(CHUNKS)):
                load_win(i)
            for i in range(2):
                sp.wait_ge(s_proj, 4 * (len(CHUNKS) - 1 + i))
                sp.dma_start(win4[:, i], w_out[:, 512 * i:512 * i + 512].rearrange("(k p) n -> p k n", p=P))\
                  .then_inc(s_win[i], 16)
            sp.wait_ge(s_proj, NJ)
            for j in range(3):
                rows = hT[NE * j:NE * (j + 1), :]
                sp.dma_start(rows[:, 0:2 * F], b_gate_up).then_inc(s_bias, 16)
                sp.dma_start(rows[:, 2 * F:3 * F], b_down).then_inc(s_bias, 16)
            sp.wait_ge(s_ba, 1)
            sp.dma_start(gff[:, :], g_ffn.partition_broadcast(P)).then_inc(s_gff, 16)
            sp.wait_ge(s_conf, CC)
            sp.wait_ge(s_sout, 16)
            sp.wait_ge(s_stq, 32)
            sp.wait_ge(s_ssout, 16)
            sp.wait_ge(s_scr, 1)

            def load_expert(ld, e, value):
                for s in range(NSLOT):
                    if value:
                        ld.wait_ge(s_wu, value(s))
                    dst = ring[:, s * SLOT:(s + 1) * SLOT]
                    if s < KD:
                        src = w_gate_up[bass.ds(e, 1), s * P:(s + 1) * P, :].rearrange("a p n -> (a p) n")
                        ld.dma_start(dst, src).then_inc(s_w[s], 16)
                    else:
                        r = (s - KD) * 2 * P
                        src = w_down[bass.ds(e, 1), r:r + 2 * P, :].rearrange("a (k p) n -> (a p) k n", p=P)
                        ld.dma_start(dst.rearrange("p (k n) -> p k n", k=2), src).then_inc(s_w[s], 16)

            load_expert(sp, 0, None)
            with sp.Fori(1, NE) as e:
                load_expert(sp, e, lambda s: e * NSLOT + (s + 1 - NSLOT))
            sp.wait_ge(s_tabs, 1)
            n_extra = sp.value_load(tab[0:1, NX:NX + 1], min_val=0, max_val=NX)
            with sp.Fori(0, NX) as i:
                with sp.If(i < n_extra):
                    ei = sp.value_load(tab[0:1, bass.ds(i, 1)], min_val=0, max_val=NE - 1)
                    load_expert(sp, ei, lambda s: i * NSLOT + (NE - 1) * NSLOT + s + 1)
            for n in TILES:
                sp.wait_ge(s_acc, 2 * n + 2)
                sp.dma_start(y_out[n * P:(n + 1) * P, :], xt3[:, n, :]).then_inc(s_yout, 16)
            sp.wait_ge(s_yout, 16 * NT)

        @block.gpsimd
        def _(pool):
            order = Count(s_pool)

            def link(ins):
                pool.wait_ge(s_pool, order.inc(ins))

            pool.memset(zs[:, 0:D], 0.0).then_inc(s_zero, 1)
            pool.wait_ge(s_zero, 1)
            for i in range(0, NX * BLK, P):
                m = min(P, NX * BLK - i)
                pool.dma_start(y_dram[NE * BLK + i:NE * BLK + i + m, :], zs[0:m, 0:D]).then_inc(s_zeroed, 16)
            pool.memset(epst[:, 0:1], RMS_EPS).then_inc(s_eps, 1)
            pool.memset(epst[:, 1:2], LN_EPS).then_inc(s_eps, 1)
            pool.memset(epst[:, 2:3], L2_EPS).then_inc(s_eps, 1)
            pool.memset(ux3[:, :, 0:DW - 1], 0.0).then_inc(s_ext, 1)
            pool.memset(qx3[:, :, 0:QW - 1], 0.0).then_inc(s_ext, 1)
            pool.wait_ge(s_hist, 32)
            for c in range(CC):
                pool.tensor_copy(ux3[:, c, US:].rearrange("p (b e) -> p b e", b=NB)[:, :, 0:DW - 1],
                                 hu[:, c]).then_inc(s_ext, 1)
            for c in range(QC):
                pool.tensor_copy(qx3[:, c, QS:].rearrange("p (b e) -> p b e", b=NB)[:, :, 0:QW - 1],
                                 hq[:, c]).then_inc(s_ext, 1)
            ust4 = ust[:].rearrange("p (c b j) -> p c b j", c=CC, b=9)
            qst4 = qst[:].rearrange("p (c b j) -> p c b j", c=QC, b=9)
            pool.wait_ge(s_u, 2 * CC)
            pool.wait_ge(s_ext, 2 + CC + QC)
            for c in range(CC):
                pool.tensor_copy(ust4[:, c, 0, :], ux3[:, c, TP:US]).then_inc(s_st, 1)
                pool.tensor_copy(ust4[:, c, 1:9, :],
                                 ux3[:, c, US:].rearrange("p (b e) -> p b e", b=NB)[:, :, TS:]).then_inc(s_st, 1)
            for c in range(QC):
                pool.wait_ge(s_evac, 2 * CC + 2 * (c + 1))
                pool.tensor_copy(qst4[:, c, 0, :], qx3[:, c, TP:QS]).then_inc(s_st, 1)
                pool.tensor_copy(qst4[:, c, 1:9, :],
                                 qx3[:, c, QS:].rearrange("p (b e) -> p b e", b=NB)[:, :, TS:]).then_inc(s_st, 1)
            pool.wait_ge(s_st, 2 * (CC + QC))
            pool.dma_start(q_state_out, qst[:]).then_inc(s_stq, 16)
            pool.dma_start(u_state_out, ust[:]).then_inc(s_stq, 16)
            for l, ns in levels():
                for n in ns:
                    pool.wait_ge(s_a1d, n + 1)
                    if l == 1:
                        pool.wait_ge(s_e1, n + 1)
                    else:
                        pool.wait_ge(s_x, LT_AT[l - 1, n])
                    pool.tensor_tensor(tile4(lt_, n), tile4(mt_, n), mat4(f"level{l}"), ALU.mult).then_inc(s_lt, 1)
            pool.wait_ge(s_sd, 2)
            pool.dma_start(sp_out.rearrange("h k v -> k h v"), s_prm.rearrange("p (h v) -> p h v", h=H)).then_inc(s_sout, 16)
            pool.wait_ge(s_sd, NB + 2)
            pool.dma_start(ss_out.rearrange("b h k v -> k (b h) v"),
                           s_smp.rearrange("p (b v) -> p b v", v=P)).then_inc(s_ssout, 16)
            for n in TILES:
                pool.wait_ge(s_h2, n + 1)
                pool.dma_start(h2_dram[n * P:(n + 1) * P, :], h23[:, n, :]).then_inc(s_h2st, 16)
            pool.wait_ge(s_h2st, 16 * NT)
            pool.wait_ge(s_idx, 1)

            def gather(p, first):
                if not first:
                    pool.wait_ge(s_xgt, p)
                pool.tensor_copy(idx_cur, idx[:, bass.ds(p, 1)]).then_inc(s_icur, 1)
                pool.wait_ge(s_icur, p + 1)
                pool.sem_inc(s_go, 1)
                pool.indirect_dma_start(xg, None, h2_dram, bass.IndirectOffsetOnAxis(idx_cur, 0)).then_inc(s_gat, 16)

            gather(0, True)
            with pool.Fori(1, NPAIR) as p:
                gather(p, False)
            pool.wait_ge(s_tabs, 1)
            n_extra = pool.value_load(tab[0:1, NX:NX + 1], min_val=0, max_val=NX)
            with pool.Fori(0, NX) as i:
                with pool.If(i < n_extra):
                    pool.wait_ge(s_xgt, i + NPAIR)
                    pool.wait_ge(s_idxo, i + 1)
                    pool.sem_inc(s_go, 1)
                    pool.indirect_dma_start(xg[0:BLK], None, h2_dram,
                                            bass.IndirectOffsetOnAxis(idxo[0:BLK], 0)).then_inc(s_gat, 16)
            pool.wait_ge(s_xdone, 1)
            pool.wait_ge(s_row, 1)
            for n in TILES:
                for j in range(TOPK):
                    pool.indirect_dma_start(ring[:, (n * TOPK + j) * D:(n * TOPK + j + 1) * D], None, y_dram,
                                            bass.IndirectOffsetOnAxis(rowi[:, n, j:j + 1], 0)).then_inc(s_yg[n], 16)

        @block.scalar
        def _(act):
            act.dma_start(par[:], params).then_inc(s_par, 16)
            act.dma_start(mats[:], consts[:, 0:len(MATS) * P]).then_inc(s_cst, 16)
            act.dma_start(cst[:], consts[:, len(MATS) * P:]).then_inc(s_cst, 16)
            act.dma_start(cb[:, 0:CC * NB * 30], hist_u).then_inc(s_hist, 16)
            act.dma_start(cb[:, CC * NB * 30:CC * NB * 30 + QC * NB * 3], hist_q).then_inc(s_hist, 16)
            act.dma_start(s_smp.rearrange("p (b v) -> p b v", v=P),
                          state_gdn.rearrange("b h k v -> k (b h) v")).then_inc(s_state, 16)
            for n in TILES:
                src = x_prompt[n * P:(n + 1) * P, :] if n < 2 else x_sample
                act.dma_start(xt3[:, n, :], src).then_inc(s_xt, 16)
            act.wait_ge(s_zeroed, 16 * (-(-NX * BLK // P)))
            act.wait_ge(s_xT, 16)
            for k in range(KD):
                act.activation(sq3[:, k], hT3[:, k], ACT.Square).then_inc(s_sq, 1)
            act.wait_ge(s_eps, 3)
            act.wait_ge(s_ssum, 1)
            act.activation(rB, bank[4][:, 0:T], ACT.Sqrt, bias=epst[:, 0:1], scale=1.0 / D).then_inc(s_rt, 1)
            act.wait_ge(s_par, 16)

            def evac(j):
                kind, c = JOBS[j]
                ps = bank[j % 4][:, 0:T]
                act.wait_ge(s_proj, j + 1)
                if kind == "ga":
                    act.activation(zs3[:, c], ps, ACT.Identity, bias=col("b_glu", c)).then_inc(s_evac, 1)
                elif kind == "gb":
                    act.activation(oT3[:, c], ps, ACT.Sigmoid, bias=col("b_glu", CC + c)).then_inc(s_evac, 1)
                elif kind == "qkv":
                    act.activation(qx3[:, c, QW - 1:QS], ps[:, 0:TP], ACT.Copy).then_inc(s_evac, 1)
                    act.activation(qx3[:, c, QS:].rearrange("p (b e) -> p b e", b=NB)[:, :, QW - 1:],
                                   ps[:, TP:T].rearrange("p (b t) -> p b t", b=NB), ACT.Copy).then_inc(s_evac, 1)
                else:
                    if c == 0:
                        act.wait_ge(s_u, 2 * CC)
                    act.activation(zs3[:, c], ps, ACT.Silu).then_inc(s_evac, 1)

            for j in range(2 * CC):
                evac(j)
            act.wait_ge(s_bag, 3)
            act.activation(e1_, ab_, ACT.Exp, scale=-1.0).then_inc(s_bae, 1)
            act.activation(ea[:, 0:H], col("a_log", 0, H), ACT.Exp).then_inc(s_bae, 1)
            act.wait_ge(s_bag, 4)
            act.activation(l1_, e1_, ACT.Ln).then_inc(s_bae, 1)
            act.activation(beta, bl_, ACT.Sigmoid).then_inc(s_bae, 1)
            for j in range(2 * CC, 2 * CC + QC):
                evac(j)
            act.wait_ge(s_cs, 1)
            act.activation(ec, bank[5][:, 32:44], ACT.Exp).then_inc(s_cse, 1)
            act.activation(ed, bank[5][:, 64:76], ACT.Exp).then_inc(s_cse, 1)
            act.activation(gc, bank[5][:, 32:44], ACT.Copy).then_inc(s_cse, 1)
            for c in range(QC):
                act.wait_ge(s_cv, 2 * (c + 1))
                act.activation(qkv3[:, c], qkv3[:, c], ACT.Silu).then_inc(s_silu, 1)
                if c % 3 == 2:
                    evac(2 * CC + QC + c // 3)
            for c in range(CC):
                act.wait_ge(s_xc, c + 1)
                act.activation(sq3[:, c], cb3[:, c], ACT.Square).then_inc(s_lsq, 1)
            act.wait_ge(s_ln2, 1)
            act.activation(rB, bank[7][:, 0:T], ACT.Sqrt, bias=epst[:, 1:2], scale=1.0 / (CC * P)).then_inc(s_lroot, 1)
            act.wait_ge(s_silu, QC)
            for c in range(NN):
                act.activation(sq3[:, c], qkv3[:, c], ACT.Square).then_inc(s_silu, 1)
            for c in range(NN):
                act.wait_ge(s_n, c + 1)
                act.activation(rn3[:, c], bank[c % 4][:, 0:T], ACT.Sqrt, bias=epst[:, 2:3]).then_inc(s_nroot, 1)
            for c in range(CC):
                act.wait_ge(s_lnd, c + 1)
                act.activation(cb3[:, c], cb3[:, c], ACT.Silu, bias=col("ln_b", c), scale=col("ln_g", c))\
                   .then_inc(s_conf, 1)

            def copy_heads(dst, src, cols, n):
                for h in range(H):
                    act.activation(dst[:, h], src[:, h * P:(h + 1) * P], ACT.Copy, scale=cols[:, H * n + h:H * n + h + 1])\
                       .then_inc(s_vke, 1)

            act.wait_ge(s_nrm, NN)
            for n in TILES:
                act.wait_ge(s_a1, n + 1)
                act.activation(flat(gB_, n), bank[4], ACT.Copy).then_inc(s_gBc, 1)
                act.activation(flat(eg_, n), bank[4], ACT.Exp).then_inc(s_gBc, 1)
                act.wait_ge(s_dif, H * (n + 1))
                act.activation(flat(x_, n), flat(x_, n), ACT.Exp).then_inc(s_dT, 1)
            act.wait_ge(s_bec, 1)
            for n in TILES:
                act.wait_ge(s_vk, n + 1)
                if n == 0:
                    act.wait_ge(s_st, 2 * (CC + QC))
                copy_heads(tile4(vb_, n), bank[6], beta, n)
                copy_heads(tile4(kbe_, n), bank[7], bec, n)
                copy_heads(tile4(kd_, n), bank[7], ed, n)
            for n in TILES:
                act.wait_ge(s_tr, n + 1)
                act.activation(flat(d_, n), bank[2 * n], ACT.Copy).then_inc(s_d1, 1)
            for l, ns in levels():
                for n in ns:
                    act.wait_ge(s_x, LT_AT[l, n])
                    act.activation(flat(x_, n), bank[2 * n], ACT.Copy).then_inc(s_xs, 1)
            for n in TILES:
                if n >= 1:
                    act.wait_ge(s_wt, n)
                    act.activation(flat(x_, n), bank[0], ACT.Copy, scale=-1.0).then_inc(s_wte, 1)
                if n == 2:
                    for i, dst in ((0, lt_), (1, mt_)):
                        act.wait_ge(s_t1, i + 1)
                        act.activation(flat(dst, 0), bank[4 + i], ACT.Copy).then_inc(s_t1e, 1)
                act.wait_ge(s_v, n + 1)
                if n >= 1:
                    act.wait_ge(s_s, n)
                act.activation(vnew, bank[1], ACT.Copy).then_inc(s_ve, 1)
                act.wait_ge(s_o, n + 1)
                if n >= 1:
                    act.wait_ge(s_ot, n)
                for h in range(H):
                    act.activation(onrm[:, h * P:(h + 1) * P], bank[2][:, h * P:(h + 1) * P], ACT.Square,
                                   accum_out=ea[:, 4 + h:5 + h]).then_inc(s_osq, 1)
                act.wait_ge(s_osq, H * (n + 1))
                act.activation(y_[:, 0:H], ea[:, 4:8], ACT.Sqrt, bias=epst[:, 0:1], scale=1.0 / P).then_inc(s_ort, 1)
            act.wait_ge(s_stq, 32)
            act.dma_start(wr, w_router.rearrange("(k p) e -> p k e", p=P)).then_inc(s_wr, 16)
            for n in TILES:
                act.wait_ge(s_x2, 2 * (n + 1))
                act.activation(h23[:, n], xt3[:, n], ACT.Square, accum_out=ssq[:, n:n + 1]).then_inc(s_x2q, 1)
                act.wait_ge(s_x2q, n + 1)
                act.activation(rr[:, n:n + 1], ssq[:, n:n + 1], ACT.Sqrt, bias=epst[:, 0:1], scale=1.0 / D).then_inc(s_x2r, 1)
            for n in TILES:
                act.wait_ge(s_h2t, 2 * n + 1)
                act.activation(hT3[:, 0:4, n * P:(n + 1) * P], bank[6].rearrange("p (k t) -> p k t", k=4),
                               ACT.Copy).then_inc(s_h2te, 1)
            act.wait_ge(s_h2, NT)
            act.dma_start(gff[:, :], g_final.partition_broadcast(P)).then_inc(s_gfin, 16)
            act.wait_ge(s_gx, NT)
            for n in TILES:
                act.activation(gate[:, n], v8[:, n, 0:TOPK], ACT.Exp, bias=nv0[:, n:n + 1],
                               accum_out=gsum[:, n:n + 1]).then_inc(s_ge, 1)

            def rows_t(turned):
                act.wait_ge(s_xgt, turned)
                act.activation(xTe[:, 4:8, :], bank[5].rearrange("p (k s) -> p k s", k=4), ACT.Copy).then_inc(s_xte, 1)

            def sigmoid(item):
                act.wait_ge(s_g, item + 1)
                act.activation(sg_b, g_s, ACT.Sigmoid, scale=ALPHA).then_inc(s_sig, 1)

            def rows_out(item, x, row):
                act.wait_ge(s_dn, item + 1)
                act.activation(y_s[x], bank[7], ACT.Copy).then_inc(s_yc, 1)
                act.wait_ge(s_yc, item + 1)
                for a in range(2):
                    act.dma_start(y_dram[bass.ds(row, BLK), a * 512:(a + 1) * 512],
                                  y_s[x][a * BLK:(a + 1) * BLK]).then_inc(s_ys[x], 16)

            def pair(p, first):
                rows_t(p + 1)
                for x in range(2):
                    sigmoid(2 * p + x)
                    if not first:
                        act.wait_ge(s_ys[x], 32 * p)
                    rows_out(2 * p + x, x, p * (2 * BLK) + x * BLK)

            pair(0, True)
            with act.Fori(1, NPAIR) as p:
                pair(p, False)
            act.wait_ge(s_ys[0], 32 * NPAIR)
            act.wait_ge(s_ys[1], 32 * NPAIR)
            act.wait_ge(s_tabs, 1)
            n_extra = act.value_load(tab[0:1, NX:NX + 1], min_val=0, max_val=NX)
            with act.Fori(0, NX) as i:
                with act.If(i < n_extra):
                    rows_t(i + (NPAIR + 1))
                    sigmoid(i + NE)
                    rows_out(i + NE, 0, i * BLK + NE * BLK)
                    act.wait_ge(s_ys[0], i * 32 + 32 * (NPAIR + 1))
                    act.sem_inc(s_xrows, 1)
            act.sem_inc(s_xdone, 1)
            for n in TILES:
                act.wait_ge(s_acc, 2 * n + 1)
                act.activation(h23[:, n], xt3[:, n], ACT.Square, accum_out=ssq[:, n:n + 1]).then_inc(s_fin, 1)
                act.wait_ge(s_fin, n + 1)
                act.activation(rr[:, n:n + 1], ssq[:, n:n + 1], ACT.Sqrt, bias=epst[:, 0:1], scale=1.0 / D).then_inc(s_frt, 1)

        @block.vector
        def _(dve):
            order = Count(s_dve)

            def link(ins):
                dve.wait_ge(s_dve, order.inc(ins))

            dve.wait_ge(s_rt, 1)
            link(dve.reciprocal(rB, rB))
            dve.wait_ge(s_par, 16)
            for k in range(KD):
                dve.scalar_tensor_tensor(hT3[:, k], hT3[:, k], col("g_mix", k), rB, ALU.mult, ALU.mult).then_inc(s_h, 1)
            dve.wait_ge(s_evac, 2 * CC)
            for c in range(CC):
                dve.tensor_tensor(ux3[:, c, DW - 1:US], zs3[:, c, 0:TP], oT3[:, c, 0:TP], ALU.mult).then_inc(s_u, 1)
                dve.tensor_tensor(ux3[:, c, US:].rearrange("p (b e) -> p b e", b=NB)[:, :, DW - 1:],
                                  zs3[:, c, TP:].rearrange("p (b t) -> p b t", b=NB),
                                  oT3[:, c, TP:].rearrange("p (b t) -> p b t", b=NB), ALU.mult).then_inc(s_u, 1)
            ba = bank[5][:, 0:NT * 8].rearrange("p (n c) -> p n c", n=NT)

            def by_tile(x):
                return x.rearrange("p (n h) -> p n h", n=NT)

            dve.wait_ge(s_ba, 1)
            dve.tensor_tensor(by_tile(y_), ba[:, :, H:2 * H], col("dt", 0, H).unsqueeze(1).to_broadcast([P, NT, H]),
                              ALU.add).then_inc(s_bag, 1)
            dve.tensor_copy(by_tile(bl_), ba[:, :, 0:H]).then_inc(s_bag, 1)
            dve.wait_ge(s_bag, 2)
            dve.scalar_tensor_tensor(ab_, y_, -1.0, y_, ALU.mult, ALU.max).then_inc(s_bag, 1)
            dve.wait_ge(s_bae, 2)
            dve.tensor_scalar(e1_, e1_, 1.0, None, ALU.add).then_inc(s_bag, 1)
            dve.wait_ge(s_bae, 4)
            link(dve.scalar_tensor_tensor(g_, y_, 0.0, l1_, ALU.max, ALU.add))
            dve.scalar_tensor_tensor(by_tile(g_), by_tile(g_), -1.0, ea[:, 0:H].unsqueeze(1).to_broadcast([P, NT, H]),
                                     ALU.mult, ALU.mult).then_inc(s_gates, 1)

            def conv(src, wide, dst, c, taps, w, bias, last):
                start = wide - TP
                parts = ((lambda j: src[:, c, j:j + TP], dst[:, c, 0:TP]),
                         (lambda j: src[:, c, start + TP:].rearrange("p (b e) -> p b e", b=NB)[:, :, j:j + TS],
                          dst[:, c, TP:].rearrange("p (b t) -> p b t", b=NB)))
                for j in range(taps):
                    marks = []
                    if j:
                        dve.wait_ge(s_dve, order.n)
                    for at_tap, out in parts:
                        if j == 0:
                            ins = dve.tensor_scalar(out, at_tap(0), w(0), bias, ALU.mult,
                                                    ALU.bypass if bias is None else ALU.add)
                        else:
                            ins = dve.scalar_tensor_tensor(out, at_tap(j), w(j), out, ALU.mult, ALU.add)
                        if j == taps - 1:
                            ins.then_inc(last, 1)
                        else:
                            order.inc(ins)

            dve.wait_ge(s_ext, 2 + CC + QC)
            dve.wait_ge(s_u, 2 * CC)
            for c in range(CC):
                conv(ux3, US, cb3, c, DW, lambda j: col("dw", j * CC + c), col("b_dw", c), s_dwc)
            for c in range(QC):
                dve.wait_ge(s_evac, 2 * CC + 2 * (c + 1))
                conv(qx3, QS, qkv3, c, QW, lambda j: col("conv", j * QC + c), None, s_cv)
            dve.wait_ge(s_cse, 3)
            dve.tensor_tensor(bec, beta, ec, ALU.mult).then_inc(s_bec, 1)
            dve.wait_ge(s_ln, 1)
            for c in range(CC):
                dve.scalar_tensor_tensor(cb3[:, c], bank[6][:, 0:T], -1.0 / (CC * P), cb3[:, c], ALU.mult, ALU.add)\
                   .then_inc(s_xc, 1)
            dve.wait_ge(s_lroot, 1)
            dve.wait_ge(s_xc, CC)
            link(dve.reciprocal(rB, rB))
            for c in range(CC):
                dve.tensor_tensor(cb3[:, c], cb3[:, c], rB, ALU.mult).then_inc(s_lnd, 1)
            for c in range(NN):
                dve.wait_ge(s_nroot, c + 1)
                link(dve.reciprocal(rn3[:, c], rn3[:, c]))
                dve.scalar_tensor_tensor(qkv3[:, c], qkv3[:, c], float(P) ** -0.5 if c < H else 1.0, rn3[:, c],
                                         ALU.mult, ALU.mult).then_inc(s_nrm, 1)
            dve.wait_ge(s_cst, 32)
            dve.wait_ge(s_st, 2 * (CC + QC))
            dve.wait_ge(s_bec, 1)
            for n in TILES:
                incl = mat4("incl_p" if n < 2 else "incl_s")
                dve.wait_ge(s_gBc, 2 * n + 1)
                for h in range(H):
                    dve.tensor_scalar(tile4(x_, n)[:, h], tile4(gB_, n)[:, h], gc[:, H * n + h:H * n + h + 1], 0.0,
                                      ALU.subtract, ALU.min).then_inc(s_dif, 1)
                dve.wait_ge(s_dT, n + 1)
                link(dve.tensor_tensor(flat(mt_, n), bank[6], flat(x_, n), ALU.mult))
                link(dve.tensor_tensor(flat(at_, n), bank[7], flat(x_, n), ALU.mult))
                dve.tensor_tensor(flat(mt_, n), flat(mt_, n), bank[5], ALU.mult).then_inc(s_a1d, 1)
                link(dve.tensor_tensor(tile4(at_, n), tile4(at_, n), incl, ALU.mult))
                dve.wait_ge(s_a1d, n + 1)
                link(dve.tensor_tensor(tile4(e_, n), tile4(mt_, n), mat4("level0"), ALU.mult))
                dve.tensor_tensor(tile4(e_, n), mat4("ident"), tile4(e_, n), ALU.subtract).then_inc(s_e1, 1)
            for l, ns in levels():
                for n in ns:
                    dve.wait_ge(s_pq, LT_AT[l, n])
                    if l < LEVELS - 1:
                        dve.tensor_tensor(flat(d_, n), flat(d_, n), bank[2 * n], ALU.subtract).then_inc(s_de, 1)
                    else:
                        dve.nop().then_inc(s_de, 1)
                    dve.tensor_tensor(flat(e_, n), flat(e_, n), bank[2 * n + 1], ALU.subtract).then_inc(s_de, 1)
            for n in (1, 2):
                dve.wait_ge(s_de, 2 * N_STEPS)
                dve.tensor_tensor(tile4(d_, n), qkv3[:, 0:H, n * P:(n + 1) * P], tile4(eg_, n), ALU.mult).then_inc(s_qg, 1)

            def outputs(n):
                dve.wait_ge(s_ort, n + 1)
                link(dve.reciprocal(y_[:, 4:8], y_[:, 0:4]))
                for h in range(H):
                    dve.tensor_scalar(onrm[:, h * P:(h + 1) * P], bank[2][:, h * P:(h + 1) * P], y_[:, 4 + h:5 + h],
                                      None, ALU.mult).then_inc(s_on, 1)
                dve.wait_ge(s_ot, n + 1)
                dve.scalar_tensor_tensor(oT3[:, :, n * P:(n + 1) * P], bank[7].rearrange("p (h t) -> p h t", h=H),
                                         col("onorm"), zs3[:, :, n * P:(n + 1) * P], ALU.mult, ALU.mult).then_inc(s_oTd, 1)

            for n in TILES:
                outputs(n)
                if n == 0:
                    dve.wait_ge(s_s, 1)
                    dve.tensor_copy(s_prm, bank[3]).then_inc(s_sd, 1)
                elif n == 1:
                    dve.wait_ge(s_s, 2)
                    for h in range(H):
                        last = dve.scalar_tensor_tensor(s_prm[:, h * P:(h + 1) * P], s_prm[:, h * P:(h + 1) * P],
                                                        tile4(eg_, 1)[:, h, P - 1:P], bank[3][:, h * P:(h + 1) * P],
                                                        ALU.mult, ALU.add)
                        if h < H - 1:
                            order.inc(last)
                    last.then_inc(s_sd, 1)
                    for b in range(2):
                        dve.tensor_scalar(flat(vb_, b), flat(kd_, 2), cst[:, X_BLK + b:X_BLK + b + 1], None,
                                          ALU.mult).then_inc(s_km, 1)
            smp4 = s_smp.rearrange("p (b h v) -> p b h v", b=NB, h=H)
            for b in range(NB):
                ps = bank[3 + b % 2]
                dve.wait_ge(s_s, 3 + b)
                for h in range(H):
                    last = dve.scalar_tensor_tensor(smp4[:, b, h], smp4[:, b, h],
                                                    tile4(eg_, 2)[:, h, TS * b + TS - 1:TS * b + TS],
                                                    ps[:, h * P:(h + 1) * P], ALU.mult, ALU.add)
                    if h < H - 1:
                        order.inc(last)
                last.then_inc(s_sd, 1)
                if b + 2 < NB:
                    dve.tensor_scalar(flat(vb_, b % 2), flat(kd_, 2), cst[:, X_BLK + b + 2:X_BLK + b + 3], None,
                                      ALU.mult).then_inc(s_km, 1)
            dve.wait_ge(s_bias, 96)
            link(dve.tensor_copy(bparts[0:3 * NE], hT[0:3 * NE, :]))
            link(dve.tensor_tensor(hT[0:3 * NE, :], hT[0:3 * NE, :], bparts[0:3 * NE], ALU.subtract))
            for j in (1, 2):
                link(dve.tensor_copy(bparts[NE * j:NE * (j + 1)], hT[NE * j:NE * (j + 1), :]))
            link(dve.tensor_tensor(hT[2 * NE:3 * NE, :], hT[2 * NE:3 * NE, :], bparts[2 * NE:3 * NE], ALU.subtract))
            link(dve.tensor_copy(bparts[2 * NE:3 * NE], hT[2 * NE:3 * NE, :]))
            dve.wait_ge(s_xt, 16 * NT)
            dve.wait_ge(s_gff, 16)
            for n in TILES:
                for a in range(2):
                    dve.wait_ge(s_mix, 2 * n + a + 1)
                    dve.tensor_tensor(xt3[:, n, a * 512:(a + 1) * 512], xt3[:, n, a * 512:(a + 1) * 512],
                                      bank[2 * n + a], ALU.add).then_inc(s_x2, 1)
            for n in TILES:
                dve.wait_ge(s_x2r, n + 1)
                link(dve.reciprocal(rr[:, n:n + 1], rr[:, n:n + 1]))
                dve.scalar_tensor_tensor(h23[:, n], xt3[:, n], rr[:, n:n + 1], gff[:, :], ALU.mult, ALU.mult)\
                   .then_inc(s_h2, 1)
            for n in TILES:
                dve.wait_ge(s_h2t, 2 * n + 2)
                dve.tensor_copy(hT3[:, 4:8, n * P:(n + 1) * P], bank[7].rearrange("p (k t) -> p k t", k=4))\
                   .then_inc(s_h2te, 1)
            iota = cst[:, X_IOTA:X_IOTA + BLK]
            for n in TILES:
                dve.wait_ge(s_lg, n + 1)
                link(dve.tensor_tensor(lg[:, n], bank[n][:, 0:NE], col("b_router", 0, NE), ALU.add))
                link(dve.max(v8[:, n], lg[:, n]))
                dve.tensor_scalar(nv0[:, n:n + 1], v8[:, n, 0:1], -1.0, None, ALU.mult).then_inc(s_gx, 1)
                link(dve.max_index(i8[:, n].bitcast(U32), v8[:, n], lg[:, n]))
                link(dve.tensor_copy(if8[:, n], i8[:, n].bitcast(U32)))
                link(dve.tensor_scalar(mall[:, n], iota[:, 0:NE], if8[:, n, 0:1], None, ALU.is_equal))
                for j in range(1, TOPK):
                    link(dve.scalar_tensor_tensor(mall[:, n], iota[:, 0:NE], if8[:, n, j:j + 1], mall[:, n],
                                                  ALU.is_equal, ALU.add))
                dve.nop().then_inc(s_m, 1)
            for n in TILES:
                link(dve.memset(tok2[:, n, 0:1], float(P * n)))
                link(dve.tensor_copy(tok2[:, n, 1:2], cst[:, X_SEL + NE:X_SEL + NE + 1]))
            dve.wait_ge(s_pp, 1)
            link(dve.tensor_copy(cntB, bank[3][:, 3 * NE:4 * NE]))
            for n in TILES:
                link(dve.scalar_tensor_tensor(pos[:, :, n], bank[3][:, n * NE:(n + 1) * NE], 1.0, mall[:, n],
                                              ALU.add, ALU.mult))
                link(dve.tensor_scalar(pos[:, :, n], pos[:, :, n], -1.0, None, ALU.add))
                dve.tensor_tensor(hit[:, n], pos[:, :, n].unsqueeze(2).to_broadcast([P, NE, BLK]),
                                  iota.unsqueeze(1).to_broadcast([P, NE, BLK]), ALU.is_equal).then_inc(s_hit, 1)
            dve.wait_ge(s_id, 1)
            ids = bank[6][:, 0:2 * NPAIR].rearrange("p (q c) -> p q c", c=2)
            link(dve.tensor_copy(idxf, ids[:, :, 0]))
            dve.tensor_tensor(idx, idxf, ids[:, :, 1], ALU.add).then_inc(s_idx, 1)

            def tables():
                dve.wait_ge(s_ge, NT)
                link(dve.reciprocal(gsum, gsum))
                for n in TILES:
                    link(dve.tensor_scalar(gate[:, n], gate[:, n], gsum[:, n:n + 1], None, ALU.mult))
                link(dve.tensor_scalar(nxb, cntB, float(BLK), None, ALU.is_gt))
                for b in range(2, T // BLK):
                    link(dve.scalar_tensor_tensor(nxb, cntB, float(BLK * b), nxb, ALU.is_gt, ALU.add))
                link(dve.tensor_copy(cumA, nxb))
                a, b, s = cumA, cumB, 1
                while s < NE:
                    link(dve.tensor_copy(b[:, 0:s], a[:, 0:s]))
                    link(dve.tensor_tensor(b[:, s:], a[:, s:], a[:, 0:NE - s], ALU.add))
                    a, b, s = b, a, 2 * s
                link(dve.tensor_tensor(cmpx, a.unsqueeze(1).to_broadcast([P, NX, NE]),
                                       iota[:, 0:NX].unsqueeze(2).to_broadcast([P, NX, NE]), ALU.is_le))
                link(dve.tensor_reduce(ex, cmpx, AX_X, ALU.add))
                link(dve.tensor_scalar(ex, ex, float(NE - 1), None, ALU.min))
                link(dve.tensor_tensor(cmpx, cmpx, nxb.unsqueeze(1).to_broadcast([P, NX, NE]), ALU.mult))
                link(dve.tensor_reduce(stx, cmpx, AX_X, ALU.add))
                link(dve.tensor_tensor(off64, iota[:, 0:NX], stx, ALU.subtract))
                link(dve.tensor_scalar(off64, off64, 1.0, float(BLK), ALU.add, ALU.mult))
                link(dve.tensor_copy(tab[:, 0:NX], ex))
                dve.tensor_copy(tab[:, NX:NX + 1], a[:, NE - 1:NE]).then_inc(s_tabs, 1)
                link(dve.tensor_tensor(b, a, nxb, ALU.subtract))
                link(dve.tensor_tensor(b, b, iota[:, 0:NE], ALU.subtract))
                link(dve.tensor_scalar(b, b, float(NE - 1), float(BLK), ALU.add, ALU.mult))
                four = [P, NT, TOPK, NE]
                link(dve.tensor_tensor(pick, iota[:, 0:NE].unsqueeze(1).unsqueeze(1).to_broadcast(four),
                                       if8[:, :, 0:TOPK].unsqueeze(3).to_broadcast(four), ALU.is_equal))
                link(dve.tensor_tensor(pick2, pick, pos.rearrange("p e n -> p n e").unsqueeze(2).to_broadcast(four),
                                       ALU.mult))
                link(dve.tensor_reduce(posj, pick2, AX_X, ALU.add))
                link(dve.tensor_tensor(pick2, pick, b.unsqueeze(1).unsqueeze(1).to_broadcast(four), ALU.mult))
                link(dve.tensor_reduce(movej, pick2, AX_X, ALU.add))
                link(dve.scalar_tensor_tensor(movej, posj, float(BLK), movej, ALU.is_ge, ALU.mult))
                link(dve.tensor_tensor(posj, posj, movej, ALU.add))
                dve.scalar_tensor_tensor(rowi, if8[:, :, 0:TOPK], float(BLK), posj, ALU.mult, ALU.add).then_inc(s_row, 1)

            def rows_t(turned):
                dve.wait_ge(s_xgt, turned)
                dve.tensor_copy(xTe[:, 0:4, :], bank[4].rearrange("p (k s) -> p k s", k=4)).then_inc(s_xte, 1)

            def select(x, e):
                dve.tensor_scalar(sel_sb[0:3 * NE, x], mat("ones")[0:3 * NE, 0:BLK],
                                  cst[0:3 * NE, bass.ds(e + X_SEL, 1)], None, ALU.mult).then_inc(s_sel, 1)

            def expert(item):
                dve.wait_ge(s_gu, item + 1)
                dve.tensor_scalar(g_s, bank[0], LIMIT, None, ALU.min).then_inc(s_g, 1)
                dve.tensor_scalar(l_s, bank[1], -LIMIT, LIMIT, ALU.max, ALU.min).then_inc(s_lin, 1)
                dve.wait_ge(s_sig, item + 1)
                dve.wait_ge(s_g, item + 1)
                dve.tensor_tensor(t_s, g_s, sg_b, ALU.mult).then_inc(s_lin, 1)
                dve.wait_ge(s_lin, item * 2 + 2)
                dve.scalar_tensor_tensor(a_s, l_s, 1.0, t_s, ALU.add, ALU.mult).then_inc(s_act, 1)
                dve.wait_ge(s_att, item + 1)
                dve.tensor_copy(actT, bank[6]).then_inc(s_atr, 1)

            def pair(p):
                rows_t(p + 1)
                for x in range(2):
                    select(x, 2 * p + x)
                    expert(2 * p + x)

            pair(0)
            tables()
            with dve.Fori(1, NPAIR) as p:
                pair(p)
            n_extra = dve.value_load(tab[0:1, NX:NX + 1], min_val=0, max_val=NX)
            with dve.Fori(0, NX) as i:
                with dve.If(i < n_extra):
                    e = dve.value_load(tab[0:1, bass.ds(i, 1)], min_val=0, max_val=NE - 1)
                    dve.tensor_scalar(pcur, pos[:, bass.ds(e, 1), :].rearrange("p a n -> p (a n)"),
                                      off64[:, bass.ds(i, 1)], None, ALU.subtract).then_inc(s_pc, 1)
                    dve.wait_ge(s_pc, i + 1)
                    for n in TILES:
                        dve.tensor_scalar(hito[:, n], iota, pcur[:, n:n + 1], None, ALU.is_equal).then_inc(s_hito, 1)
                    dve.wait_ge(s_ido, i + 1)
                    dve.tensor_copy(idxof[0:BLK], bank[2][0:BLK, 0:1]).then_inc(s_ix1, 1)
                    dve.wait_ge(s_ix1, i + 1)
                    dve.tensor_tensor(idxo[0:BLK], idxof[0:BLK], bank[2][0:BLK, 1:2], ALU.add).then_inc(s_idxo, 1)
                    rows_t(i + (NPAIR + 1))
                    select(0, e)
                    expert(i + NE)
            dve.wait_ge(s_gfin, 16)
            for n in TILES:
                dve.wait_ge(s_yg[n], 16 * TOPK)
                for j in range(TOPK):
                    row = ring[:, (n * TOPK + j) * D:(n * TOPK + j + 1) * D]
                    ins = dve.scalar_tensor_tensor(xt3[:, n], row, gate[:, n, j:j + 1], xt3[:, n], ALU.mult, ALU.add)
                    if j < TOPK - 1:
                        link(ins)
                    else:
                        ins.then_inc(s_acc, 1)
                dve.wait_ge(s_frt, n + 1)
                link(dve.reciprocal(rr[:, n:n + 1], rr[:, n:n + 1]))
                dve.scalar_tensor_tensor(xt3[:, n], xt3[:, n], rr[:, n:n + 1], gff[:, :], ALU.mult, ALU.mult)\
                   .then_inc(s_acc, 1)

        @block.tensor
        def _(pe):
            pe.wait_ge(s_cst, 32)
            for k in range(KD):
                pe.wait_ge(s_sq, k + 1)
                mm = pe.matmul(bank[4][:, 0:T], mat("ones"), sq3[:, k], start=(k == 0), stop=(k == KD - 1))
            mm.then_inc(s_ssum, 1)
            pe.wait_ge(s_h, KD)

            def taken(j):
                return j + 1 if j < 2 * CC else (2 * CC + 2 * (j + 1 - 2 * CC) if j < 2 * CC + QC
                                                 else 2 * CC + 2 * QC + (j + 1 - 2 * CC - QC))

            for j in range(NJ):
                pe.wait_ge(s_win[j // 4 % 2], 16 * (j // 8 + 1))
                if j >= 4:
                    pe.wait_ge(s_evac, taken(j - 4))
                for k in range(KD):
                    mm = pe.matmul(bank[j % 4][:, 0:T], win4[:, j // 4 % 2, k, (j % 4) * P:(j % 4 + 1) * P], hT3[:, k],
                                   start=(k == 0), stop=(k == KD - 1))
                mm.then_inc(s_proj, 1)
                if j == 2 * CC - 1:
                    pe.wait_ge(s_ba_in, 16)
                    for n in TILES:
                        for k in range(KD):
                            mm = pe.matmul(bank[5][:, 8 * n:8 * n + 8], hT3[:, k, n * P:(n + 1) * P],
                                           gff[:, 8 * k:8 * k + 8], start=(k == 0), stop=(k == KD - 1))
                    mm.then_inc(s_ba, 1)
                if j == 2 * CC + QC - 1:
                    pe.wait_ge(s_gates, 1)
                    for n in TILES:
                        pe.matmul(bank[5][:, 32 + H * n:32 + H * (n + 1)], mat("incl_p" if n < 2 else "incl_s"),
                                  g_[:, H * n:H * (n + 1)], start=True, stop=True)
                        mm = pe.matmul(bank[5][:, 64 + H * n:64 + H * (n + 1)], mat("later_p" if n < 2 else "later_s"),
                                       g_[:, H * n:H * (n + 1)], start=True, stop=True)
                    mm.then_inc(s_cs, 1)
            pe.wait_ge(s_dwc, 2 * CC)
            for c in range(CC):
                mm = pe.matmul(bank[6][:, 0:T], mat("ones"), cb3[:, c], start=(c == 0), stop=(c == CC - 1))
            mm.then_inc(s_ln, 1)
            for c in range(CC):
                pe.wait_ge(s_lsq, c + 1)
                mm = pe.matmul(bank[7][:, 0:T], mat("ones"), sq3[:, c], start=(c == 0), stop=(c == CC - 1))
            mm.then_inc(s_ln2, 1)
            for c in range(NN):
                pe.wait_ge(s_silu, QC + c + 1)
                if c >= 4:
                    pe.wait_ge(s_nroot, c - 3)
                elif c == 0:
                    pe.wait_ge(s_evac, taken(NJ - 1))
                pe.matmul(bank[c % 4][:, 0:T], mat("ones"), sq3[:, c], start=True, stop=True).then_inc(s_n, 1)
            pe.wait_ge(s_nrm, NN)
            pe.wait_ge(s_bec, 1)
            for n in TILES:
                if n:
                    pe.wait_ge(s_a1d, n)
                    pe.wait_ge(s_gBc, 2 * n)
                tk = slice(n * P, (n + 1) * P)
                incl = mat("incl_p" if n < 2 else "incl_s")
                for h in range(H):
                    hs = slice(h * P, (h + 1) * P)
                    one = slice(H * n + h, H * n + h + 1)
                    pe.matmul(bank[4][:, hs], g_[:, one].to_broadcast([P, P]), incl, start=True, stop=True)
                    pe.matmul(bank[5][:, hs], beta[:, one].to_broadcast([P, P]), mat("ident"), start=True, stop=True)
                    pe.matmul(bank[6][:, hs], qkv3[:, H + h, tk], qkv3[:, H + h, tk], start=True, stop=True)
                    mm = pe.matmul(bank[7][:, hs], qkv3[:, H + h, tk], qkv3[:, h, tk], start=True, stop=True)
                mm.then_inc(s_a1, 1)
            for n in TILES:
                tk = slice(n * P, (n + 1) * P)
                if n:
                    pe.wait_ge(s_vke, 3 * H * n)
                else:
                    pe.wait_ge(s_a1d, NT)
                for h in range(H):
                    hs = slice(h * P, (h + 1) * P)
                    pe.transpose(bank[6][:, hs], qkv3[:, 2 * H + h, tk], mat("ident"))
                    mm = pe.transpose(bank[7][:, hs], qkv3[:, H + h, tk], mat("ident"))
                mm.then_inc(s_vk, 1)
            for n in TILES:
                pe.wait_ge(s_e1, n + 1)
                for h in range(H):
                    mm = pe.transpose(bank[2 * n][:, h * P:(h + 1) * P], tile4(e_, n)[:, h], mat("ident"))
                mm.then_inc(s_tr, 1)
            pe.wait_ge(s_d1, NT)
            for l, ns in levels():
                for n in ns:
                    if l > 1:
                        pe.wait_ge(s_de, 2 * LT_AT[l - 1, n])
                    pe.wait_ge(s_lt, LT_AT[l, n])
                    for h in range(H):
                        mm = pe.matmul(bank[2 * n][:, h * P:(h + 1) * P], tile4(lt_, n)[:, h], tile4(d_, n)[:, h],
                                       start=True, stop=True)
                    mm.then_inc(s_x, 1)
                for n in ns:
                    pe.wait_ge(s_xs, LT_AT[l, n])
                    for h in range(H):
                        hs = slice(h * P, (h + 1) * P)
                        if l < LEVELS - 1:
                            pe.matmul(bank[2 * n][:, hs], tile4(e_, n)[:, h], tile4(x_, n)[:, h], start=True, stop=True)
                        mm = pe.matmul(bank[2 * n + 1][:, hs], tile4(x_, n)[:, h], tile4(e_, n)[:, h],
                                       start=True, stop=True)
                    mm.then_inc(s_pq, 1)
            pe.wait_ge(s_de, 2 * N_STEPS)
            pe.wait_ge(s_vke, 3 * H * NT)
            pe.wait_ge(s_state, 16)
            smp4 = s_smp.rearrange("p (b h v) -> p b h v", b=NB, h=H)
            for n in TILES:
                if n >= 1:
                    for h in range(H):
                        mm = pe.matmul(bank[0][:, h * P:(h + 1) * P], tile4(kbe_, n)[:, h], tile4(e_, n)[:, h],
                                       start=True, stop=True)
                    mm.then_inc(s_wt, 1)
                    pe.wait_ge(s_wte, n)
                    pe.wait_ge(s_qg, n)
                    pe.wait_ge(s_ve, n)
                    pe.wait_ge(s_sd, n)
                if n == 2:
                    for i, src in enumerate((x_, d_)):
                        for b in range(NB):
                            for h in range(H):
                                mm = pe.matmul(bank[4 + i][:, h * P + TS * b:h * P + TS * (b + 1)], smp4[:, b, h],
                                               tile4(src, 2)[:, h, TS * b:TS * (b + 1)], start=True, stop=True)
                        mm.then_inc(s_t1, 1)
                    pe.wait_ge(s_t1e, 2)
                for h in range(H):
                    hs = slice(h * P, (h + 1) * P)
                    mm = pe.matmul(bank[1][:, hs], tile4(e_, n)[:, h], tile4(vb_, n)[:, h], start=True, stop=(n == 0))
                    if n == 1:
                        mm = pe.matmul(bank[1][:, hs], tile4(x_, n)[:, h], s_prm[:, hs], start=False, stop=True)
                    if n == 2:
                        mm = pe.matmul(bank[1][:, hs], lt_[:, hs], mat("ident"), start=False, stop=True)
                mm.then_inc(s_v, 1)
                pe.wait_ge(s_ve, n + 1)
                if n:
                    pe.wait_ge(s_on, H * n)
                for h in range(H):
                    hs = slice(h * P, (h + 1) * P)
                    if n == 1:
                        pe.matmul(bank[2][:, hs], tile4(d_, n)[:, h], s_prm[:, hs], start=True, stop=False)
                    if n == 2:
                        pe.matmul(bank[2][:, hs], mt_[:, hs], mat("ident"), start=True, stop=False)
                    mm = pe.matmul(bank[2][:, hs], tile4(at_, n)[:, h], vnew[:, hs], start=(n == 0), stop=True)
                mm.then_inc(s_o, 1)
                if n < 2:
                    for h in range(H):
                        hs = slice(h * P, (h + 1) * P)
                        mm = pe.matmul(bank[3][:, hs], tile4(kd_, n)[:, h], vnew[:, hs], start=True, stop=True)
                    mm.then_inc(s_s, 1)
                pe.wait_ge(s_on, H * (n + 1))
                if n:
                    pe.wait_ge(s_oTd, n)
                for h in range(H):
                    hs = slice(h * P, (h + 1) * P)
                    mm = pe.transpose(bank[7][:, hs], onrm[:, hs], mat("ident"))
                mm.then_inc(s_ot, 1)
            for b in range(NB):
                pe.wait_ge(s_km, b + 1)
                pe.wait_ge(s_sd, 2 + max(b - 1, 0))
                for h in range(H):
                    hs = slice(h * P, (h + 1) * P)
                    mm = pe.matmul(bank[3 + b % 2][:, hs], flat(vb_, b % 2)[:, hs], vnew[:, hs], start=True, stop=True)
                mm.then_inc(s_s, 1)
            pe.wait_ge(s_sd, 2 + NB)
            pe.drain().then_inc(s_scr, 1)
            pe.wait_ge(s_conf, CC)
            for i in range(2):
                pe.wait_ge(s_win[i], 64)
            for n in TILES:
                for a in range(2):
                    for i, k in enumerate([4, 5, 6, 7, 0, 1, 2, 3]):
                        if k == 0:
                            pe.wait_ge(s_oTd, n + 1)
                        cat = cb3[:, k - 4] if k >= 4 else oT3[:, k]
                        mm = pe.matmul(bank[2 * n + a], cat[:, n * P:(n + 1) * P], win4[:, a, k, :],
                                       start=(i == 0), stop=(i == KD - 1))
                    mm.then_inc(s_mix, 1)
            for n in TILES:
                pe.wait_ge(s_h2, n + 1)
                if n:
                    pe.wait_ge(s_h2te, 2 * n)
                for a in range(2):
                    for k in range(4):
                        mm = pe.transpose(bank[6 + a][:, k * P:(k + 1) * P], h23[:, n, (4 * a + k) * P:(4 * a + k + 1) * P],
                                          mat("ident"))
                    mm.then_inc(s_h2t, 1)
            pe.wait_ge(s_wr, 16)
            pe.wait_ge(s_x2, 2 * NT)
            for n in TILES:
                pe.wait_ge(s_h2te, 2 * n + 2)
                for k in range(KD):
                    mm = pe.matmul(bank[n][:, 0:NE], hT3[:, k, n * P:(n + 1) * P], wr[:, k, :], start=(k == 0),
                                   stop=(k == KD - 1))
                mm.then_inc(s_lg, 1)
            pe.wait_ge(s_m, NT)
            for n in range(NT + 1):
                for m in range(min(n + 1, NT)):
                    mm = pe.matmul(bank[3][:, n * NE:(n + 1) * NE], mat("strict" if m == n else "ones"), mall[:, m],
                                   start=(m == 0), stop=(m == min(n, NT - 1)))
            mm.then_inc(s_pp, 1)
            pe.wait_ge(s_hit, NT)
            for q in range(NPAIR):
                for n in TILES:
                    mm = pe.matmul(bank[6][:, 2 * q:2 * q + 2], hit[:, n, 2 * q:2 * q + 2, :].rearrange("p e s -> p (e s)"),
                                   tok2[:, n, :], start=(n == 0), stop=(n == NT - 1))
            mm.then_inc(s_id, 1)

            def turn_rows(item):
                pe.wait_ge(s_gat, item * 16 + 16)
                for k in range(KD):
                    mm = pe.transpose(bank[4 + k // 4][:, (k % 4) * P:(k % 4 + 1) * P], xg[:, k * P:(k + 1) * P], mat("ident"))
                mm.then_inc(s_xgt, 1)
                pe.wait_ge(s_xte, item * 2 + 2)

            def bias_rows(x, out, columns, close):
                for a in range(2):
                    mm = pe.matmul(out[a * BLK:(a + 1) * BLK], sel_sb[0:3 * NE, x, :],
                                   bparts[0:3 * NE, columns + a * 512:columns + (a + 1) * 512], start=True, stop=False,
                                   skip_group_check=True)

            def expert(x, item):
                pe.wait_ge(s_sel, item + 1)
                bias_rows(x, bank[0], 0, False)
                bias_rows(x, bank[1], F, False)
                for k in range(KD):
                    pe.wait_ge(s_w[k], item * 16 + 16)
                    for half in range(2):
                        for a in range(2):
                            c = k * SLOT + half * F + a * 512
                            mm = pe.matmul(bank[half][a * BLK:(a + 1) * BLK], xTe[:, k, x * BLK:(x + 1) * BLK],
                                           ring[:, c:c + 512], start=False, stop=(k == KD - 1), skip_group_check=True)
                    mm.then_inc(s_wu, 1)
                pe.drain().then_inc(s_gu, 1)
                pe.wait_ge(s_act, item + 1)
                for j in range(4):
                    mm = pe.transpose(bank[6][:, j * P:(j + 1) * P], a_s[:, j * P:(j + 1) * P], mat("ident"))
                mm.then_inc(s_att, 1)

            def down(x, item, first):
                if not first:
                    pe.wait_ge(s_yc, item)
                bias_rows(x, bank[7], 2 * F, False)
                pe.wait_ge(s_atr, item + 1)
                for k in range(KD):
                    if k % 2 == 0:
                        pe.wait_ge(s_w[KD + k // 2], item * 16 + 16)
                    for a in range(2):
                        c = (KD + k // 2) * SLOT + (k % 2) * D + a * 512
                        mm = pe.matmul(bank[7][a * BLK:(a + 1) * BLK], actT[:, (k % 4) * P + (k // 4) * BLK:][:, 0:BLK],
                                       ring[:, c:c + 512], start=False, stop=(k == KD - 1), skip_group_check=True)
                    if k % 2 == 1:
                        mm.then_inc(s_wu, 1)
                pe.drain().then_inc(s_dn, 1)

            def pair(p, first):
                turn_rows(p)
                for x in range(2):
                    expert(x, 2 * p + x)
                    down(x, 2 * p + x, first and x == 0)

            pair(0, True)
            with pe.Fori(1, NPAIR) as p:
                pair(p, False)
            pe.wait_ge(s_tabs, 1)
            n_extra = pe.value_load(tab[0:1, NX:NX + 1], min_val=0, max_val=NX)
            with pe.Fori(0, NX) as i:
                with pe.If(i < n_extra):
                    pe.wait_ge(s_hito, i * NT + NT)
                    for n in TILES:
                        mm = pe.matmul(bank[2][0:BLK, 0:2], hito[:, n, :], tok2[:, n, :], start=(n == 0), stop=(n == NT - 1))
                    mm.then_inc(s_ido, 1)
                    turn_rows(i + NPAIR)
                    expert(0, i + NE)
                    down(0, i + NE, False)


INPUTS = ["xT", "x_prompt", "x_sample", "state_gdn", "hist_q", "hist_u", "params", "consts", "w_in", "w_out", "g_ffn",
          "g_final", "w_router", "w_gate_up", "b_gate_up", "w_down", "b_down"]
OUTPUTS = {"y": (T, D), "sp": (H, P, P), "ss": (NB, H, P, P), "q_state": (P, QC * 9 * 3), "u_state": (P, CC * 9 * 30)}


def shape_constants():
    j, i = np.arange(P)[:, None], np.arange(P)[None, :]
    same = (j // TS) == (i // TS)
    mats = {"ident": j == i, "ones": (j >= 0) & (i >= 0), "incl_p": i >= j, "incl_s": (i >= j) & same, "later_p": j > i,
            "later_s": (j > i) & same, "strict": j < i}
    for l in range(LEVELS):
        s = 1 << l
        mats[f"level{l}"] = (i // (2 * s) == j // (2 * s)) & (i // s % 2 == 1) & (j // s % 2 == 0)
    cols = np.zeros((P, NXC), np.float32)
    cols[:, X_IOTA:X_IOTA + BLK] = np.arange(BLK)
    cols[:, X_BLK:X_BLK + NB] = (np.arange(P)[:, None] // TS) == np.arange(NB)
    cols[:, X_SEL:X_SEL + NE] = (np.arange(P)[:, None] % NE) == np.arange(NE)
    cols[:, X_SEL + NE] = np.arange(P)
    return np.concatenate([mats[m].astype(np.float32) for m in MATS] + [cols], axis=1)


def kernel(x_prompt, x_sample, state_gdn, state_qkv_conv, state_dwconv, norm_mix_g, w_in, w_conv_qkv, a_log, dt_bias,
           w_onorm, b_glu, w_dw, b_dw, ln_g, ln_b, w_out, norm_ffn_g, w_router, b_router, w_gate_up, b_gate_up, w_down,
           b_down, norm_final_g):
    from concourse import bacc
    from concourse.bass_utils import run_bass_kernel_spmd

    xp = np.asarray(x_prompt).reshape(TP, D)
    xs = np.asarray(x_sample).reshape(NB * TS, D)

    def channels(a, rows):
        return np.asarray(a).reshape(rows, -1, P).transpose(2, 0, 1).reshape(P, -1)

    def rows(a):
        return np.broadcast_to(np.asarray(a).reshape(1, -1), (P, np.asarray(a).size))

    params = np.concatenate([channels(norm_mix_g, 1), channels(w_conv_qkv, QW), channels(w_dw, DW), channels(b_glu, 1),
                             channels(b_dw, 1), channels(ln_g, 1), channels(ln_b, 1), channels(w_onorm, 1), rows(a_log),
                             rows(dt_bias), rows(b_router)], axis=1)

    def history(a, w):
        return np.asarray(a)[0].reshape(NB, w, -1, P).transpose(3, 2, 0, 1).reshape(P, -1)

    arrays = {
        "xT": np.concatenate([xp, xs]).T, "x_prompt": xp, "x_sample": xs, "state_gdn": np.asarray(state_gdn)[0],
        "hist_q": history(state_qkv_conv, QW - 1), "hist_u": history(state_dwconv, DW - 1), "params": params,
        "consts": shape_constants(), "w_in": np.asarray(w_in)[0], "w_out": np.asarray(w_out)[0],
        "g_ffn": np.asarray(norm_ffn_g)[0], "g_final": np.asarray(norm_final_g), "w_router": np.asarray(w_router)[0],
        "w_gate_up": np.asarray(w_gate_up)[0], "b_gate_up": np.asarray(b_gate_up)[0], "w_down": np.asarray(w_down)[0],
        "b_down": np.asarray(b_down)[0],
    }
    arrays = {n: np.ascontiguousarray(a) for n, a in arrays.items()}
    nc = bacc.Bacc("TRN2", target_bir_lowering=False, num_devices=1)
    ins = [nc.dram_tensor(f"in_{n}", arrays[n].shape, F32, kind="ExternalInput").ap() for n in INPUTS]
    outs = [nc.dram_tensor(f"out_{n}", s, F32, kind="ExternalOutput").ap() for n, s in OUTPUTS.items()]
    stream_step(nc, *ins, *outs)
    got = run_bass_kernel_spmd(nc, [{f"in_{n}": arrays[n] for n in INPUTS}], core_ids=[0]).results[0]

    y = np.asarray(got["out_y"])

    def states(a, tiles, w):
        return np.asarray(a).reshape(P, tiles, 9, w).transpose(2, 3, 1, 0).reshape(9, w, tiles * P)

    q, u = states(got["out_q_state"], QC, QW - 1), states(got["out_u_state"], CC, DW - 1)
    return (y[:TP].reshape(1, TP, D), y[TP:].reshape(NB, TS, D), np.asarray(got["out_sp"])[None, None], q[None, 0:1],
            u[None, 0:1], np.asarray(got["out_ss"])[None], q[None, 1:], u[None, 1:])
```

```python
from contextlib import ExitStack

import numpy as np

import concourse.bass as bass
from concourse import mybir

F32 = mybir.dt.float32
BF16 = mybir.dt.bfloat16
I32 = mybir.dt.int32
U32 = mybir.dt.uint32
ALU = mybir.AluOpType
ACT = mybir.ActivationFunctionType
AX_X = mybir.AxisListType.X

P = 128
D = 1024
KD = D // P
NT = 3
T = NT * P
TP = 256
NB, TS = 8, 16
H = 4
QW, DW = 4, 31
QC, CC = 12, 4
QE = QW - 1 + TP + NB * (QW - 1 + TS)
UE = DW - 1 + TP + NB * (DW - 1 + TS)
QS, US = QW - 1 + TP, DW - 1 + TP
NE, TOPK = 32, 4
F = 1024
BLK = 64
NX = (T * TOPK) // (BLK + 1)
NSLOT = 12
SLOT = 2 * F
RMS_EPS, LN_EPS, L2_EPS = 1e-6, 1e-5, 1e-6
LIMIT, ALPHA = 7.0, 1.702
NPAIR = NE // 2
SLOT_OF = (6, 7, 5, 0, 1, 2, 3, 4, 8, 9, 10, 11)
FIRST_ORDER = (0, 1, 2, 8, 9, 10, 11, 3, 4, 5, 6, 7)
LEVELS = 7
S_LEVELS = 4

C_Z, C_BA, C_GLU = 1536, 2048, 2056
CHUNKS = (None, None, 0, 512, 1024, C_Z)

MATS = ["ones", "ident", "strict", "incl_p", "incl_s", "later_p", "later_s"] + [f"level{l}" for l in range(LEVELS)]
M = {name: i for i, name in enumerate(MATS)}
X_IOTA, X_BLK, X_SEL = 0, 64, 64 + NB
NXC = 64 + NB + NE + 1
PARAMS, _at = {}, 0
for _name, _n in (("g_mix", KD), ("conv", QW * QC), ("dw", DW * CC), ("b_glu", 2 * CC), ("b_dw", CC), ("ln_g", CC),
                  ("ln_b", CC), ("onorm", 1), ("a_log", H), ("dt", H), ("b_router", NE)):
    PARAMS[_name] = _at
    _at += _n
NPARAM = _at


class Count:

    def __init__(self, sem):
        self.sem, self.n = sem, 0

    def inc(self, ins):
        self.n += 1
        ins.then_inc(self.sem, 1)
        return self.n


def stream_step(nc, xT, x_prompt, x_sample, state_gdn, hist_q, hist_u, params, consts, w_in, w_out, g_ffn,
                g_final, w_router, w_gate_up, b_gate_up, w_down, b_down,
                y_out, sp_out, ss_out, q_state_out, u_state_out):
    h2_dram = nc.dram_tensor("h2_rows", (T, D), F32, kind="Internal").ap()
    y_dram = nc.dram_tensor("expert_rows", ((NE + NX) * BLK, D), F32, kind="Internal").ap()

    with ExitStack() as ctx:
        def sb(name, shape, dt=F32):
            return ctx.enter_context(nc.sbuf_tensor(name, shape, dt))

        def sem(name):
            return ctx.enter_context(nc.semaphore(name))

        ring = sb("ring", [P, NSLOT * SLOT])
        mats = sb("mats", [P, (len(MATS) + 1) * P])
        cst = sb("cst", [P, NXC])
        par = sb("par", [P, NPARAM])
        win = sb("win", [P, 2 * KD * 512])
        hT = sb("hT", [P, KD * T])
        xt = sb("xt", [P, NT * D])
        qkvc = sb("qkvc", [P, QC * T])
        zs = sb("zs", [P, CC * T])
        cb = sb("cb", [P, CC * T])
        oT = sb("oT", [P, CC * T])
        qst = sb("qst", [P, QC * 9 * 3])
        ust = sb("ust", [P, CC * 9 * 30])
        gff = sb("gff", [P, D])
        gates_t = sb("gates_t", [P, 12 * 17])
        epst = sb("epst", [P, 12])
        bank = [ctx.enter_context(nc.psum_tensor(f"bank{i}", [P, 512], F32))[:, :] for i in range(8)]

        def mat(name):
            return mats[:, M[name] * P:(M[name] + 1) * P]

        def mat4(name):
            return mat(name).unsqueeze(1).to_broadcast([P, H, P])

        def col(name, i=0, n=1):
            return par[:, PARAMS[name] + i:PARAMS[name] + i + n]

        at = [0]

        def scratch(n):
            at[0] += n
            assert at[0] <= NSLOT * SLOT
            return ring[:, at[0] - n:at[0]]

        qx = scratch(QE * QC)
        s_smp = scratch(NB * H * P)
        eg_ = scratch(T * H)
        d_ = scratch(T * H)
        e_ = scratch(T * H)
        x_ = scratch(T * H)
        lt_ = scratch(T * H)
        mt_ = scratch(T * H)
        at_ = scratch(T * H)
        s_prm = scratch(H * P)
        assert at[0] <= 10 * SLOT
        qx3 = qx.rearrange("p (c e) -> p c e", c=QC)
        ux3 = ring[:, QE * QC + NB * H * P + T * H:][:, 0:UE * CC].rearrange("p (c e) -> p c e", c=CC)
        base_d = QE * QC + NB * H * P + T * H
        base_lt = base_d + 3 * T * H
        sq3 = ring[:, base_lt:base_lt + KD * T].rearrange("p (k t) -> p k t", k=KD)
        rB = at_[:, 0:T]
        tail = x_[:, 0:2 * T].rearrange("p (c t) -> p c t", c=2)
        prod = [at_[:, T * (i + 1):T * (i + 2)] for i in range(3)]
        lroot = ust[:, KD * NE:KD * NE + T]
        lsq3 = hT[:, 0:CC * T].rearrange("p (c t) -> p c t", c=CC)
        qw5 = ring[:, base_d:base_d + 3 * T * H].rearrange("p (g n h t) -> p g n h t", g=3, n=NT, h=H)[:, 0:3:2]
        vb_, kbe_, kd_ = qx[:, 0:T * H], qx[:, T * H:2 * T * H], qx[:, 2 * T * H:3 * T * H]

        def tile4(x, n):
            return x[:, n * 512:(n + 1) * 512].rearrange("p (h t) -> p h t", h=H)

        def flat(x, n):
            return x[:, n * 512:(n + 1) * 512]

        hT3 = hT[:].rearrange("p (k t) -> p k t", k=KD)
        qkv3 = qkvc[:].rearrange("p (c t) -> p c t", c=QC)
        zs3 = zs[:].rearrange("p (c t) -> p c t", c=CC)
        cb3 = cb[:].rearrange("p (c t) -> p c t", c=CC)
        oT3 = oT[:].rearrange("p (c t) -> p c t", c=CC)
        win4 = win[:].rearrange("p (b k n) -> p b k n", b=2, k=KD)
        hu = cb[:, 0:CC * NB * 30].rearrange("p (c b j) -> p c b j", c=CC, b=NB)
        hq = cb[:, CC * NB * 30:CC * NB * 30 + QC * NB * 3].rearrange("p (c b j) -> p c b j", c=QC, b=NB)
        xt3 = xt[:].rearrange("p (n d) -> p n d", n=NT)
        gcol = [gates_t[:, 12 * i:12 * i + 12] for i in range(15)]
        (y_, ab_, e1_, l1_, bl_, beta, g_, gc, ec, bec, ed, ea, bk, rq, rk) = gcol

        nrm24 = gates_t[:, 12 * 15:12 * 17]

        h2 = qkvc[:, 0:NT * D]
        h23 = h2.rearrange("p (n d) -> p n d", n=NT)
        xg = qkvc[:, NT * D:NT * D + D]
        actT = qkvc[:, NT * D + D:NT * D + D + 512]
        at2 = [0]

        def wscratch(n):
            at2[0] += n
            assert at2[0] <= 2 * KD * 512
            return win[:, at2[0] - n:at2[0]]

        hitf = wscratch(NT * NE * BLK // 2)
        hit = hitf.bitcast(BF16).rearrange("p (n e s) -> p n e s", n=NT, e=NE)
        hitx = hitf.bitcast(BF16)[:, 0:NT * NX * BLK].rearrange("p (n i s) -> p n i s", n=NT, i=NX)
        xTe = wscratch(KD * P).rearrange("p (k s) -> p k s", k=KD)
        g_s, l_s, sg_b, t_s, a_s = (wscratch(512) for _ in range(5))
        y_s = [wscratch(512) for _ in range(2)]
        braw = ring[:, 10 * SLOT:10 * SLOT + 3 * F]
        bparts = mats[:, 3 * P:3 * P + 3 * F // 2].bitcast(BF16)
        small = oT[:, :]
        sm = [0]

        def srow(n):
            sm[0] += n
            assert sm[0] <= CC * T
            return small[:, sm[0] - n:sm[0]]

        wr = ust[:, 0:KD * NE].rearrange("p (k e) -> p k e", k=KD)
        lg = srow(NT * NE).rearrange("p (n e) -> p n e", n=NT)
        v8 = srow(NT * 8).rearrange("p (n j) -> p n j", n=NT)
        i8 = srow(NT * 8).rearrange("p (n j) -> p n j", n=NT)
        if8 = srow(NT * 8).rearrange("p (n j) -> p n j", n=NT)
        gate = srow(NT * TOPK).rearrange("p (n j) -> p n j", n=NT)
        gsum = srow(NT)
        nv0 = srow(NT)
        mall = srow(NT * NE).rearrange("p (n e) -> p n e", n=NT)
        pos = srow(NE * NT).rearrange("p (e n) -> p e n", n=NT)
        posj = srow(NT * TOPK).rearrange("p (n j) -> p n j", n=NT)
        rowi = srow(NT * TOPK).bitcast(I32).rearrange("p (n j) -> p n j", n=NT)
        cntB = srow(NE)
        nxb = srow(NE)
        cumA, cumB = srow(NE), srow(NE)
        cmpx = cb[:, 0:NX * NE].rearrange("p (i e) -> p i e", i=NX)
        ex = srow(NX)
        stx = srow(NX)
        movej = srow(NT * TOPK).rearrange("p (n j) -> p n j", n=NT)
        pick, pick2 = (x.rearrange("p (n j e) -> p n j e", n=NT, j=TOPK) for x in (
            cb[:, NX * NE:NX * NE + NT * TOPK * NE], hT[:, 0:NT * TOPK * NE]))
        off64 = srow(NX)
        tab = srow(NX + 1).bitcast(I32)
        idxf = srow(NPAIR)
        idx = srow(NPAIR).bitcast(I32)
        idx_cur = srow(1).bitcast(I32)
        idxxf = srow(NX)
        idxx = srow(NX).bitcast(I32)
        posx = srow(NT * NX).rearrange("p (n i) -> p n i", n=NT)
        item_pos = hT[:, 0:NX * NE].rearrange("p (i e) -> p i e", i=NX)
        ssq = epst[:, 4:4 + NT]
        tokf = srow(NT)
        sel_sb = srow(BLK).bitcast(BF16).rearrange("p (x s) -> p x s", x=2)
        tok2 = srow(NT).bitcast(BF16).rearrange("p (n c) -> p n c", n=NT)
        rr = epst[:, 8:8 + NT]

        s_xT, s_cst, s_par, s_hist, s_state = (sem(x) for x in ("xT_in", "consts_in", "params_in", "hist_in", "state_in"))
        s_win = [sem(f"win_in{i}") for i in range(2)]
        s_ba_in, s_xt, s_gff, s_wr = sem("ba_in"), sem("x_in"), sem("gffn_in"), sem("router_in")
        s_bias, s_gfin = sem("bias_in"), sem("gfinal_in")
        s_ext = sem("histories_placed")
        s_eps = sem("eps_set")
        s_sq, s_ssum, s_rt, s_h = sem("x_squared"), sem("x_sum"), sem("x_root"), sem("hT_ready")
        s_proj, s_evac = sem("proj_ready"), sem("proj_taken")
        s_ba, s_bag, s_bae, s_gates = sem("ba_ready"), sem("ba_taken"), sem("ba_scalar"), sem("g_ready")
        s_cs, s_cse = sem("cumsum_ready"), sem("cumsum_exp")
        s_u, s_cv, s_dwc = sem("u_ready"), sem("qkv_conv"), sem("dw_conv")
        s_silu = sem("qkv_silu")
        s_nroot, s_nrm = sem("norm_roots"), sem("qk_normed")
        s_st = sem("conv_states_staged")
        s_ln, s_xc, s_lsq, s_ln2, s_lroot, s_lnd, s_conf = (sem(x) for x in (
            "ln_sum", "ln_centred", "ln_squared", "ln_sum2", "ln_root", "ln_scaled", "conformer_ready"))
        s_a1, s_gBc, s_dif, s_dT, s_a1d = (sem(x) for x in ("gram_ready", "decay_rows", "decay_diff", "decay_exp", "gram_taken"))
        s_lt, s_e1, s_tr, s_d1 = sem("level_rows"), sem("inverse_start"), sem("inverse_T"), sem("inverse_T_taken")
        s_x, s_xs, s_pq, s_de = sem("level_x"), sem("level_x_taken"), sem("level_pq"), sem("level_done")
        s_vk, s_vke = sem("vk_turned"), sem("vk_taken")
        s_wt, s_wte, s_v, s_ve = sem("w_ready"), sem("w_taken"), sem("vnew_ready"), sem("vnew_taken")
        s_qg, s_t1, s_t1e = sem("q_decayed"), sem("stream_terms"), sem("stream_terms_taken")
        s_o, s_osq, s_ort, s_on = sem("o_ready"), sem("o_squared"), sem("o_root"), sem("o_normed")
        s_ot, s_oTd = sem("o_turned"), sem("oT_ready")
        s_s, s_sd, s_km = sem("state_ready"), sem("state_taken"), sem("k_masked")
        s_mix, s_x2, s_x2q, s_x2r, s_h2, s_h2st = (sem(x) for x in (
            "mix_ready", "x2_ready", "x2_squared", "x2_root", "h2_ready", "h2_stored"))
        s_h2t, s_h2te = sem("h2_turned"), sem("h2T_ready")
        s_lg, s_gx, s_ge = sem("logits_ready"), sem("gate_max"), sem("gate_exp")
        s_m, s_pp, s_hit, s_id, s_idx = (sem(x) for x in (
            "mask_ready", "places_ready", "hits_ready", "index_sums", "index_ready"))
        s_tabs = sem("tables_ready")
        s_w = [sem(f"w_landed{i}") for i in range(NSLOT)]
        s_wu = sem("w_used")
        s_icur, s_gat, s_xgt, s_xte = sem("index_cur"), sem("gathered"), sem("rows_turned"), sem("rowsT_ready")
        s_sel, s_gu, s_g, s_sig, s_act = (sem(x) for x in ("sel_ready", "gu_ready", "gate_clamped", "sig_ready", "act_ready"))
        s_att, s_atr, s_dn, s_yc = sem("act_turned"), sem("actT_ready"), sem("down_ready"), sem("y_copied")
        s_ys = [sem(f"y_stored{i}") for i in range(2)]
        s_hito, s_ido, s_idxo = sem("hits_extra"), sem("index_sums_extra"), sem("index_extra")
        s_yg, s_acc = [sem(f"y_gathered{i}") for i in range(NT)], sem("y_ready")
        s_fin = sem("final_squared")
        s_frt = sem("final_root")
        s_stq = sem("states_out")
        s_yout = sem("y_out_stored")
        s_qsq = sem("qk_squared")
        s_cn, s_edk, s_bsplit = sem("lengths_squared"), sem("edges_scaled"), sem("bias_split")
        s_zero, s_zeroed, s_row = sem("zeros_set"), sem("zero_rows_stored"), sem("rows_known")
        s_go = sem("gather_may_go")
        s_lin = sem("linear_ready")
        s_dve, s_pool = sem("vector_order"), sem("pool_order")
        s_dec, s_sev, s_smp_done = sem("states_decayed"), sem("state_gain_taken"), sem("sample_states_done")
        s_ones, s_up, s_tap0, s_prd, s_padd = (sem(x) for x in (
            "ones_set", "u_ready_last", "first_taps", "tap_products", "taps_added"))
        s_tail = sem("last_taps")
        s_sout, s_ssout = sem("prompt_state_out"), sem("sample_state_out")

        JOBS = [("ga", 0), ("ga", 1), ("gb", 0), ("gb", 1), ("ga", 2), ("ga", 3), ("gb", 2), ("gb", 3)] + \
               [("qkv", c) for c in range(QC)] + [("z", c) for c in range(CC)]
        NJ = len(JOBS)
        NN = 2 * H
        JQ, JZ = 2 * CC, 2 * CC + QC
        JOB_BANK = [j % 4 for j in range(NJ - 2)] + [5, 7]
        DVE_TAPS = 10
        N_PROD = 2 * (DW - 1 - DVE_TAPS)
        TILES = range(NT)

        def levels():
            for l in range(1, LEVELS):
                yield l, [n for n in TILES if n < 2 or l < S_LEVELS]

        LT_AT, DE_AT, k_, x2_ = {}, {}, 0, 0
        for l_, ns_ in levels():
            for n_ in ns_:
                k_ += 1
                LT_AT[l_, n_] = k_
        N_STEPS = k_
        OUT_BANK = ((0, 4), (5, 6), (0, 4))
        LOGIT_BANK = (5, 6, 0)
        STATE_BANK = (1, 3, 4)

        def halves(x, l, which):
            return x.rearrange("p (g two s) -> p g two s", two=2, s=1 << l)[:, :, which]

        smp4 = s_smp.rearrange("p (b h v) -> p b h v", b=NB, h=H)
        k_only = [flat(vb_, 0), flat(vb_, 1), flat(vb_, 2), flat(kd_, 0), flat(kd_, 1), flat(kbe_, 0), flat(kbe_, 1),
                  flat(kd_, 2)]
        added = [qkvc[:, NT * D + 512 * i:NT * D + 512 * (i + 1)] for i in range(3)]

        def put_u(engine, c, done):
            engine.tensor_tensor(ux3[:, c, DW - 1:US], zs3[:, c, 0:TP], oT3[:, c, 0:TP], ALU.mult).then_inc(done, 1)
            engine.tensor_tensor(ux3[:, c, US:].rearrange("p (b e) -> p b e", b=NB)[:, :, DW - 1:],
                                 zs3[:, c, TP:].rearrange("p (b t) -> p b t", b=NB),
                                 oT3[:, c, TP:].rearrange("p (b t) -> p b t", b=NB), ALU.mult).then_inc(done, 1)

        block = ctx.enter_context(nc.Block())

        @block.sync
        def _(sp):
            sp.dma_start(hT3, xT.rearrange("(k p) t -> p k t", p=P)).then_inc(s_xT, 16)

            def load_win(i):
                c = CHUNKS[i]
                if i >= 2:
                    sp.wait_ge(s_proj, 4 * (i - 1))
                if c is None:
                    for g in range(2):
                        g0 = C_GLU + 512 * g + 256 * i
                        sp.dma_start(win4[:, i % 2, :, 256 * g:256 * (g + 1)],
                                     w_in[:, g0:g0 + 256].rearrange("(k p) n -> p k n", p=P)).then_inc(s_win[i % 2], 16)
                else:
                    sp.dma_start(win4[:, i % 2], w_in[:, c:c + 512].rearrange("(k p) n -> p k n", p=P))\
                      .then_inc(s_win[i % 2], 16)

            load_win(0)
            sp.dma_start(gff[:, 0:KD * 8].rearrange("p (k n) -> p k n", k=KD),
                         w_in[:, C_BA:C_BA + 8].rearrange("(k p) n -> p k n", p=P),
                         allow_slow_non_contiguous=True).then_inc(s_ba_in, 16)
            load_win(1)
            for j in range(3):
                rows = braw[NE * j:NE * (j + 1), :]
                sp.dma_start(rows[:, 0:2 * F], b_gate_up).then_inc(s_bias, 16)
                sp.dma_start(rows[:, 2 * F:3 * F], b_down).then_inc(s_bias, 16)
            for i in range(2, len(CHUNKS)):
                load_win(i)
            for i in range(2):
                sp.wait_ge(s_proj, 4 * (len(CHUNKS) - 1 + i))
                sp.dma_start(win4[:, i], w_out[:, 512 * i:512 * i + 512].rearrange("(k p) n -> p k n", p=P))\
                  .then_inc(s_win[i], 16)
            sp.wait_ge(s_ba, 1)
            sp.dma_start(gff[:, :], g_ffn.partition_broadcast(P)).then_inc(s_gff, 16)
            sp.wait_ge(s_conf, CC)
            sp.wait_ge(s_sout, 16)
            sp.wait_ge(s_stq, 32)
            sp.wait_ge(s_oTd, NT)
            sp.wait_ge(s_ve, NT)
            sp.wait_ge(s_dec, NB)

            def load_expert(ld, e, value):
                for i, r in enumerate(range(NSLOT) if value else FIRST_ORDER):
                    s = SLOT_OF[r]
                    if not value and s == 10:
                        ld.wait_ge(s_bsplit, 1)
                    if not value and s == 0:
                        ld.wait_ge(s_s, NB + 2)
                    if not value and s == 2:
                        ld.wait_ge(s_ssout, 16)
                    if value:
                        ld.wait_ge(s_wu, value(i))
                    dst = ring[:, s * SLOT:(s + 1) * SLOT]
                    if r < KD:
                        src = w_gate_up[bass.ds(e, 1), r * P:(r + 1) * P, :].rearrange("a p n -> (a p) n")
                        ld.dma_start(dst, src).then_inc(s_w[s], 16)
                    else:
                        r0 = (r - KD) * 2 * P
                        src = w_down[bass.ds(e, 1), r0:r0 + 2 * P, :].rearrange("a (k p) n -> (a p) k n", p=P)
                        ld.dma_start(dst.rearrange("p (k n) -> p k n", k=2), src).then_inc(s_w[s], 16)

            load_expert(sp, 0, None)
            with sp.Fori(1, NE) as e:
                load_expert(sp, e, lambda s: e * NSLOT + (s + 1 - NSLOT))
            sp.wait_ge(s_tabs, 1)
            n_extra = sp.value_load(tab[0:1, NX:NX + 1], min_val=0, max_val=NX)
            with sp.Fori(0, NX) as i:
                with sp.If(i < n_extra):
                    ei = sp.value_load(tab[0:1, bass.ds(i, 1)], min_val=0, max_val=NE - 1)
                    load_expert(sp, ei, lambda s: i * NSLOT + (NE - 1) * NSLOT + s + 1)
            for n in TILES:
                sp.wait_ge(s_acc, 2 * n + 2)
                sp.dma_start(y_out[n * P:(n + 1) * P, :], xt3[:, n, :]).then_inc(s_yout, 16)
            sp.wait_ge(s_yout, 16 * NT)

        @block.gpsimd
        def _(pool):
            order = Count(s_pool)

            def link(ins):
                pool.wait_ge(s_pool, order.inc(ins))

            pool.memset(mat("ones"), 1.0).then_inc(s_ones, 1)
            pool.memset(epst[:, 0:1], RMS_EPS).then_inc(s_eps, 1)
            pool.memset(epst[:, 1:2], LN_EPS).then_inc(s_eps, 1)
            pool.memset(epst[:, 2:3], L2_EPS).then_inc(s_eps, 1)
            pool.memset(ux3[:, :, 0:DW - 1], 0.0).then_inc(s_ext, 1)
            pool.memset(qx3[:, :, 0:QW - 1], 0.0).then_inc(s_ext, 1)
            pool.wait_ge(s_hist, 32)
            for c in range(CC):
                pool.tensor_copy(ux3[:, c, US:].rearrange("p (b e) -> p b e", b=NB)[:, :, 0:DW - 1],
                                 hu[:, c]).then_inc(s_ext, 1)
            for c in range(QC):
                pool.tensor_copy(qx3[:, c, QS:].rearrange("p (b e) -> p b e", b=NB)[:, :, 0:QW - 1],
                                 hq[:, c]).then_inc(s_ext, 1)
            pool.memset(eg_[:, 0:D], 0.0).then_inc(s_zero, 1)
            pool.wait_ge(s_zero, 1)
            pool.wait_ge(s_proj, 2)
            for i in range(0, NX * BLK, P):
                m = min(P, NX * BLK - i)
                pool.dma_start(y_dram[NE * BLK + i:NE * BLK + i + m, :], eg_[0:m, 0:D]).then_inc(s_zeroed, 16)
            pool.wait_ge(s_ext, 2 + CC + QC)
            for c in (2, 3):
                pool.wait_ge(s_evac, CC + c + 1)
                put_u(pool, c, s_up)
            for k in range(N_PROD):
                pool.wait_ge(s_prd, 2 * (k + 1))
                if k == 0:
                    pool.wait_ge(s_tap0, 4)
                if k >= 2:
                    pool.wait_ge(s_padd, k - 1)
                c = 2 + k % 2
                pool.tensor_tensor(cb3[:, c], cb3[:, c], prod[k % 3], ALU.add).then_inc(s_padd, 1)
            pool.wait_ge(s_tail, 4)
            for i in range(2):
                pool.wait_ge(s_padd, N_PROD - 1 + i)
                pool.tensor_tensor(cb3[:, 2 + i], cb3[:, 2 + i], tail[:, i], ALU.add).then_inc(s_padd, 1)
            ust4 = ust[:].rearrange("p (c b j) -> p c b j", c=CC, b=9)
            qst4 = qst[:].rearrange("p (c b j) -> p c b j", c=QC, b=9)
            pool.wait_ge(s_u, 4)
            pool.wait_ge(s_up, 4)
            for c in range(CC):
                pool.tensor_copy(ust4[:, c, 0, :], ux3[:, c, TP:US]).then_inc(s_st, 1)
                pool.tensor_copy(ust4[:, c, 1:9, :],
                                 ux3[:, c, US:].rearrange("p (b e) -> p b e", b=NB)[:, :, TS:]).then_inc(s_st, 1)
            for c in range(QC):
                pool.wait_ge(s_evac, 2 * CC + 2 * (c + 1))
                pool.tensor_copy(qst4[:, c, 0, :], qx3[:, c, TP:QS]).then_inc(s_st, 1)
                pool.tensor_copy(qst4[:, c, 1:9, :],
                                 qx3[:, c, QS:].rearrange("p (b e) -> p b e", b=NB)[:, :, TS:]).then_inc(s_st, 1)
            pool.wait_ge(s_st, 2 * (CC + QC))
            pool.dma_start(q_state_out, qst[:]).then_inc(s_stq, 16)
            pool.dma_start(u_state_out, ust[:]).then_inc(s_stq, 16)
            for l, ns in levels():
                for n in ns:
                    pool.wait_ge(s_a1d, n + 1)
                    if l == 1:
                        pool.wait_ge(s_e1, n + 1)
                    else:
                        pool.wait_ge(s_x, LT_AT[l - 1, n])
                    pool.tensor_tensor(tile4(lt_, n), tile4(mt_, n), mat4(f"level{l}"), ALU.mult).then_inc(s_lt, 1)
            pool.wait_ge(s_bias, 96)
            pool.wait_ge(s_lt, N_STEPS)
            pool.wait_ge(s_e1, NT)
            pool.wait_ge(s_a1, NT)
            link(pool.tensor_copy(bparts[0:3 * NE], braw[0:3 * NE, :]))
            link(pool.tensor_tensor(braw[0:3 * NE, :], braw[0:3 * NE, :], bparts[0:3 * NE], ALU.subtract))
            for j in (1, 2):
                link(pool.tensor_copy(bparts[NE * j:NE * (j + 1)], braw[NE * j:NE * (j + 1), :]))
            link(pool.tensor_tensor(braw[2 * NE:3 * NE, :], braw[2 * NE:3 * NE, :], bparts[2 * NE:3 * NE], ALU.subtract))
            pool.tensor_copy(bparts[2 * NE:3 * NE], braw[2 * NE:3 * NE, :]).then_inc(s_bsplit, 1)
            pool.wait_ge(s_bsplit, 1)
            pool.wait_ge(s_sd, 2)
            pool.dma_start(sp_out.rearrange("h k v -> k h v"), s_prm.rearrange("p (h v) -> p h v", h=H)).then_inc(s_sout, 16)
            pool.wait_ge(s_t1, 1)
            for b in range(NB):
                pool.tensor_tensor(smp4[:, b], smp4[:, b],
                                   tile4(eg_, 2)[:, :, TS * b + TS - 1:TS * b + TS].to_broadcast([P, H, P]),
                                   ALU.mult).then_inc(s_dec, 1)
            pool.wait_ge(s_v, NT)
            for b in range(NB):
                pool.tensor_scalar(k_only[b], flat(kd_, 2), cst[:, X_BLK + b:X_BLK + b + 1], None,
                                   ALU.mult).then_inc(s_km, 1)
            pool.wait_ge(s_dec, NB)
            for b in range(NB):
                pool.wait_ge(s_sev, b + 1)
                pool.tensor_tensor(smp4[:, b], smp4[:, b], added[b % 3].rearrange("p (h v) -> p h v", h=H),
                                   ALU.add).then_inc(s_smp_done, 1)
            pool.wait_ge(s_h2st, 16 * NT)
            pool.wait_ge(s_idx, 1)

            def gather(p, first):
                if not first:
                    pool.wait_ge(s_xgt, p)
                pool.tensor_copy(idx_cur, idx[:, bass.ds(p, 1)]).then_inc(s_icur, 1)
                pool.wait_ge(s_icur, p + 1)
                pool.sem_inc(s_go, 1)
                pool.indirect_dma_start(xg, None, h2_dram, bass.IndirectOffsetOnAxis(idx_cur, 0)).then_inc(s_gat, 16)

            gather(0, True)
            pool.wait_ge(s_smp_done, NB)
            pool.dma_start(ss_out.rearrange("b h k v -> k (b h) v"),
                           s_smp.rearrange("p (b v) -> p b v", v=P)).then_inc(s_ssout, 16)
            pool.wait_ge(s_idx, 2)
            with pool.Fori(1, NPAIR) as p:
                gather(p, False)
            pool.wait_ge(s_idxo, 1)
            n_extra = pool.value_load(tab[0:1, NX:NX + 1], min_val=0, max_val=NX)
            with pool.Fori(0, NX) as i:
                with pool.If(i < n_extra):
                    pool.wait_ge(s_xgt, i + NPAIR)
                    pool.tensor_copy(idx_cur[0:BLK], idxx[0:BLK, bass.ds(i, 1)]).then_inc(s_icur, 1)
                    pool.wait_ge(s_icur, i + (NPAIR + 1))
                    pool.sem_inc(s_go, 1)
                    pool.indirect_dma_start(xg[0:BLK], None, h2_dram,
                                            bass.IndirectOffsetOnAxis(idx_cur[0:BLK], 0)).then_inc(s_gat, 16)
            pool.wait_ge(s_row, 1)
            pool.wait_ge(s_ys[1], 32 * NPAIR)
            pool.wait_ge(s_ys[0], n_extra * 32 + 32 * NPAIR)
            pool.sem_inc(s_go, 1)
            for n in TILES:
                for j in range(TOPK):
                    pool.indirect_dma_start(ring[:, (n * TOPK + j) * D:(n * TOPK + j + 1) * D], None, y_dram,
                                            bass.IndirectOffsetOnAxis(rowi[:, n, j:j + 1], 0)).then_inc(s_yg[n], 16)

        @block.scalar
        def _(act):
            act.dma_start(par[:], params).then_inc(s_par, 16)
            act.dma_start(mats[:, P:len(MATS) * P], consts[:, P:len(MATS) * P]).then_inc(s_cst, 16)
            act.dma_start(cst[:], consts[:, len(MATS) * P:]).then_inc(s_cst, 16)
            act.dma_start(cb[:, 0:CC * NB * 30], hist_u).then_inc(s_hist, 16)
            act.dma_start(cb[:, CC * NB * 30:CC * NB * 30 + QC * NB * 3], hist_q).then_inc(s_hist, 16)
            act.dma_start(s_smp.rearrange("p (b v) -> p b v", v=P),
                          state_gdn.rearrange("b h k v -> k (b h) v")).then_inc(s_state, 16)
            for n in TILES:
                src = x_prompt[n * P:(n + 1) * P, :] if n < 2 else x_sample
                act.dma_start(xt3[:, n, :], src).then_inc(s_xt, 16)
            act.wait_ge(s_xT, 16)
            for k in range(KD):
                act.activation(sq3[:, k], hT3[:, k], ACT.Square).then_inc(s_sq, 1)
            act.wait_ge(s_eps, 3)
            act.wait_ge(s_ssum, 1)
            act.activation(rB, bank[4][:, 0:T], ACT.Sqrt, bias=epst[:, 0:1], scale=1.0 / D).then_inc(s_rt, 1)
            act.wait_ge(s_par, 16)

            def evac(j):
                kind, c = JOBS[j]
                ps = bank[JOB_BANK[j]][:, 0:T]
                act.wait_ge(s_proj, j + 1)
                if kind == "ga":
                    act.activation(zs3[:, c], ps, ACT.Identity, bias=col("b_glu", c)).then_inc(s_evac, 1)
                elif kind == "gb":
                    act.activation(oT3[:, c], ps, ACT.Sigmoid, bias=col("b_glu", CC + c)).then_inc(s_evac, 1)
                elif kind == "qkv":
                    act.activation(qx3[:, c, QW - 1:QS], ps[:, 0:TP], ACT.Copy).then_inc(s_evac, 1)
                    act.activation(qx3[:, c, QS:].rearrange("p (b e) -> p b e", b=NB)[:, :, QW - 1:],
                                   ps[:, TP:T].rearrange("p (b t) -> p b t", b=NB), ACT.Copy).then_inc(s_evac, 1)
                else:
                    if c == 0:
                        act.wait_ge(s_u, 4)
                        act.wait_ge(s_up, 4)
                    act.activation(zs3[:, c], ps, ACT.Silu).then_inc(s_evac, 1)

            made = [0]

            def two_parts(k, c, j, out, **how):
                w = col("dw", j * CC + c)
                act.activation(out[:, 0:TP], ux3[:, c, j:j + TP], scale=w, **how).then_inc(k, 1)
                act.activation(out[:, TP:].rearrange("p (b t) -> p b t", b=NB),
                               ux3[:, c, US:].rearrange("p (b e) -> p b e", b=NB)[:, :, j:j + TS], scale=w, **how)\
                   .then_inc(k, 1)

            def products(count):
                for k in range(made[0], min(made[0] + count, N_PROD)):
                    if k >= 3:
                        act.wait_ge(s_padd, k - 2)
                    two_parts(s_prd, 2 + k % 2, 1 + k // 2, prod[k % 3], func=ACT.Copy)
                made[0] += count

            def silu(c):
                act.wait_ge(s_cv, 4 * (c // 2 + 1))
                act.activation(qkv3[:, c], qkv3[:, c], ACT.Silu).then_inc(s_silu, 1)
                if c < NN:
                    act.wait_ge(s_silu, c + 1)
                    act.activation(sq3[:, c], qkv3[:, c], ACT.Square).then_inc(s_qsq, 1)

            for j in range(JQ):
                evac(j)
            act.wait_ge(s_ext, 2 + CC + QC)
            act.wait_ge(s_up, 4)
            for c in (2, 3):
                two_parts(s_tap0, c, 0, cb3[:, c], func=ACT.Identity, bias=col("b_dw", c))
            products(3)
            for j in range(JQ, JQ + QC):
                evac(j)
                if j == JQ + 5:
                    act.wait_ge(s_bag, 3)
                    act.activation(e1_, ab_, ACT.Exp, scale=-1.0).then_inc(s_bae, 1)
                    act.activation(ea[:, 0:H], col("a_log", 0, H), ACT.Exp).then_inc(s_bae, 1)
                    act.wait_ge(s_bag, 4)
                    act.activation(l1_, e1_, ACT.Ln).then_inc(s_bae, 1)
                    act.activation(beta, bl_, ACT.Sigmoid).then_inc(s_bae, 1)
                c = 2 * (j - JQ - 6)
                if 0 <= c < NN:
                    silu(c)
                    silu(c + 1)
                products(5)
                if j == JZ - 2:
                    act.wait_ge(s_cn, 1)
                    act.activation(nrm24, bank[5][:, 96:96 + 2 * NT * H], ACT.Sqrt, bias=epst[:, 2:3]).then_inc(s_nroot, 1)
            assert made[0] >= N_PROD
            act.wait_ge(s_cs, 1)
            act.activation(ec, bank[5][:, 32:44], ACT.Exp).then_inc(s_cse, 1)
            act.activation(ed, bank[5][:, 64:76], ACT.Exp).then_inc(s_cse, 1)
            act.activation(gc, bank[5][:, 32:44], ACT.Copy).then_inc(s_cse, 1)
            for c in range(NN, QC):
                silu(c)
            evac(JZ)
            evac(JZ + 1)

            def copy_heads(dst, src, cols, n):
                for h in range(H):
                    act.activation(dst[:, h], src[:, h * P:(h + 1) * P], ACT.Copy, scale=cols[:, H * n + h:H * n + h + 1])\
                       .then_inc(s_vke, 1)

            act.wait_ge(s_zeroed, 16 * (-(-NX * BLK // P)))
            for n in TILES:
                bk0 = 4 * (n % 2)
                act.wait_ge(s_a1, n + 1)
                act.activation(flat(eg_, n), bank[bk0], ACT.Exp).then_inc(s_gBc, 1)
                act.wait_ge(s_dif, H * (n + 1))
                act.activation(flat(x_, n), flat(x_, n), ACT.Exp).then_inc(s_dT, 1)
            evac(JZ + 2)
            evac(JZ + 3)
            for c in range(CC):
                act.wait_ge(s_xc, c + 1)
                act.activation(lsq3[:, c], cb3[:, c], ACT.Square).then_inc(s_lsq, 1)
            for n in TILES:
                act.wait_ge(s_tr, n + 1)
                act.activation(flat(d_, n), bank[2 * n], ACT.Copy).then_inc(s_d1, 1)
            for l, ns in levels():
                for n in ns:
                    act.wait_ge(s_x, LT_AT[l, n])
                    act.activation(flat(x_, n), bank[2 * n], ACT.Copy).then_inc(s_xs, 1)
                n = l - 1
                if n < NT:
                    act.wait_ge(s_vk, n + 1)
                    if n == 0:
                        act.wait_ge(s_edk, 1)
                        act.wait_ge(s_st, 2 * (CC + QC))
                    copy_heads(tile4(vb_, n), bank[6], beta, n)
                    copy_heads(tile4(kbe_, n), bank[7], bec, n)
                    copy_heads(tile4(kd_, n), bank[7], ed, n)
                elif l == NT + 1:
                    act.wait_ge(s_ln2, 1)
                    act.wait_ge(s_stq, 32)
                    act.activation(lroot, bank[6][:, 0:T], ACT.Sqrt, bias=epst[:, 1:2], scale=1.0 / (CC * P))\
                       .then_inc(s_lroot, 1)
            for c in range(CC):
                act.wait_ge(s_lnd, c + 1)
                act.activation(cb3[:, c], cb3[:, c], ACT.Silu, bias=col("ln_b", c), scale=col("ln_g", c))\
                   .then_inc(s_conf, 1)
            def v_new(n):
                act.wait_ge(s_v, n + 1)
                act.activation(flat(kbe_, n), bank[1], ACT.Copy).then_inc(s_ve, 1)

            def out_root(n):
                act.wait_ge(s_o, n + 1)
                for h in range(H):
                    act.activation(tile4(at_, n)[:, h], bank[2][:, h * P:(h + 1) * P], ACT.Square,
                                   scale=rq[:, H * n + h:H * n + h + 1], accum_out=ea[:, 4 + h:5 + h]).then_inc(s_osq, 1)
                act.wait_ge(s_osq, H * (n + 1))
                act.activation(y_[:, 0:H], ea[:, 4:8], ACT.Sqrt, bias=epst[:, 0:1], scale=1.0 / P).then_inc(s_ort, 1)

            def second_norm(n):
                act.wait_ge(s_x2, 2 * (n + 1))
                act.activation(h23[:, n], xt3[:, n], ACT.Square, accum_out=ssq[:, n:n + 1]).then_inc(s_x2q, 1)
                act.wait_ge(s_x2q, n + 1)
                act.activation(rr[:, n:n + 1], ssq[:, n:n + 1], ACT.Sqrt, bias=epst[:, 0:1], scale=1.0 / D).then_inc(s_x2r, 1)

            v_new(0)
            for n in (1, 2):
                act.wait_ge(s_wt, n)
                act.activation(flat(x_, n), bank[4 * (n - 1)], ACT.Copy, scale=-1.0).then_inc(s_wte, 1)
            out_root(0)
            act.wait_ge(s_t1, 1)
            for i in range(2):
                act.activation(lt_[:, 512 * i:512 * (i + 1)], bank[5 + i], ACT.Copy).then_inc(s_t1e, 1)
            v_new(1)
            out_root(1)
            second_norm(0)
            v_new(2)
            out_root(2)
            act.wait_ge(s_stq, 32)
            act.dma_start(wr, w_router.rearrange("(k p) e -> p k e", p=P)).then_inc(s_wr, 16)
            second_norm(1)

            def h_stored(n):
                act.wait_ge(s_h2, n + 1)
                act.dma_start(h2_dram[n * P:(n + 1) * P, :], h23[:, n, :]).then_inc(s_h2st, 16)

            def h_first(n):
                act.wait_ge(s_h2t, 2 * n + 1)
                act.activation(hT3[:, 0:4, n * P:(n + 1) * P], bank[2].rearrange("p (k t) -> p k t", k=4),
                               ACT.Copy).then_inc(s_h2te, 1)

            h_stored(0)
            h_first(0)
            h_stored(1)
            second_norm(2)
            h_first(1)
            h_stored(2)
            h_first(2)
            for b in range(NB):
                act.wait_ge(s_s, 3 + b)
                if b >= 3:
                    act.wait_ge(s_smp_done, b - 2)
                act.activation(added[b % 3], bank[STATE_BANK[b % 3]], ACT.Copy).then_inc(s_sev, 1)
            act.dma_start(gff[:, :], g_final.partition_broadcast(P)).then_inc(s_gfin, 16)
            act.wait_ge(s_gx, NT)
            for n in TILES:
                act.activation(gate[:, n], v8[:, n, 0:TOPK], ACT.Exp, bias=nv0[:, n:n + 1],
                               accum_out=gsum[:, n:n + 1]).then_inc(s_ge, 1)

            def rows_t(turned):
                act.wait_ge(s_xgt, turned)
                act.activation(xTe[:, 4:8, :], bank[5].rearrange("p (k s) -> p k s", k=4), ACT.Copy).then_inc(s_xte, 1)

            def sigmoid(item):
                act.wait_ge(s_g, item + 1)
                act.activation(sg_b, g_s, ACT.Sigmoid, scale=ALPHA).then_inc(s_sig, 1)

            def rows_out(item, x, row):
                act.wait_ge(s_dn, item + 1)
                act.activation(y_s[x], bank[7], ACT.Copy).then_inc(s_yc, 1)
                act.wait_ge(s_yc, item + 1)
                for a in range(2):
                    act.dma_start(y_dram[bass.ds(row, BLK), a * 512:(a + 1) * 512],
                                  y_s[x][a * BLK:(a + 1) * BLK]).then_inc(s_ys[x], 16)

            def pair(p, first):
                rows_t(p + 1)
                for x in range(2):
                    sigmoid(2 * p + x)
                    if not first:
                        act.wait_ge(s_ys[x], 32 * p)
                    rows_out(2 * p + x, x, p * (2 * BLK) + x * BLK)

            pair(0, True)
            with act.Fori(1, NPAIR) as p:
                pair(p, False)
            act.wait_ge(s_tabs, 1)
            n_extra = act.value_load(tab[0:1, NX:NX + 1], min_val=0, max_val=NX)
            with act.Fori(0, NX) as i:
                with act.If(i < n_extra):
                    rows_t(i + (NPAIR + 1))
                    sigmoid(i + NE)
                    act.wait_ge(s_ys[0], i * 32 + 32 * NPAIR)
                    rows_out(i + NE, 0, i * BLK + NE * BLK)
            for n in TILES:
                act.wait_ge(s_acc, 2 * n + 1)
                act.activation(h23[:, n], xt3[:, n], ACT.Square, accum_out=ssq[:, n:n + 1]).then_inc(s_fin, 1)
                act.wait_ge(s_fin, n + 1)
                act.activation(rr[:, n:n + 1], ssq[:, n:n + 1], ACT.Sqrt, bias=epst[:, 0:1], scale=1.0 / D).then_inc(s_frt, 1)

        @block.vector
        def _(dve):
            order = Count(s_dve)

            def link(ins):
                dve.wait_ge(s_dve, order.inc(ins))

            dve.wait_ge(s_rt, 1)
            link(dve.reciprocal(rB, rB))
            dve.wait_ge(s_par, 16)
            for k in range(KD):
                dve.scalar_tensor_tensor(hT3[:, k], hT3[:, k], col("g_mix", k), rB, ALU.mult, ALU.mult).then_inc(s_h, 1)
            def conv(src, wide, dst, tiles, taps, w, bias, last, first=0, shift=0):
                start = wide - TP
                chains = []
                for c in tiles:
                    to = dst[:, c - shift]
                    chains.append((c, lambda j, c=c: src[:, c, j:j + TP], to[:, 0:TP]))
                    chains.append((c, lambda j, c=c: src[:, c, start + TP:].rearrange("p (b e) -> p b e", b=NB)[:, :, j:j + TS],
                                   to[:, TP:].rearrange("p (b t) -> p b t", b=NB)))
                done = [0] * len(chains)
                for j in range(first, taps):
                    for i, (c, at_tap, out) in enumerate(chains):
                        if j == first:
                            ins = dve.tensor_scalar(out, at_tap(j), w(j, c), bias(c) if bias else None, ALU.mult,
                                                    ALU.add if bias else ALU.bypass)
                        else:
                            dve.wait_ge(s_dve, done[i])
                            ins = dve.scalar_tensor_tensor(out, at_tap(j), w(j, c), out, ALU.mult, ALU.add)
                        if j == taps - 1:
                            ins.then_inc(last, 1)
                        else:
                            done[i] = order.inc(ins)

            for c in (0, 1):
                dve.wait_ge(s_evac, 3 + c)
                put_u(dve, c, s_u)
            dve.wait_ge(s_ext, 2 + CC + QC)
            dve.wait_ge(s_u, 4)
            conv(ux3, US, cb3, (0, 1), DW, lambda j, c: col("dw", j * CC + c), lambda c: col("b_dw", c), s_dwc)
            ba = bank[5][:, 0:NT * 8].rearrange("p (n c) -> p n c", n=NT)

            def by_tile(x):
                return x.rearrange("p (n h) -> p n h", n=NT)

            dve.wait_ge(s_ba, 1)
            dve.tensor_tensor(by_tile(y_), ba[:, :, H:2 * H], col("dt", 0, H).unsqueeze(1).to_broadcast([P, NT, H]),
                              ALU.add).then_inc(s_bag, 1)
            dve.tensor_copy(by_tile(bl_), ba[:, :, 0:H]).then_inc(s_bag, 1)
            dve.wait_ge(s_bag, 2)
            dve.scalar_tensor_tensor(ab_, y_, -1.0, y_, ALU.mult, ALU.max).then_inc(s_bag, 1)
            dve.wait_ge(s_up, 4)
            conv(ux3, US, tail, (2, 3), DW, lambda j, c: col("dw", j * CC + c), None, s_tail, DW - DVE_TAPS, 2)
            def conv_qkv(c):
                dve.wait_ge(s_evac, JQ + 2 * (c + 2))
                conv(qx3, QS, qkv3, (c, c + 1), QW, lambda j, c: col("conv", j * QC + c), None, s_cv)

            conv_qkv(0)
            dve.wait_ge(s_bae, 2)
            dve.tensor_scalar(e1_, e1_, 1.0, None, ALU.add).then_inc(s_bag, 1)
            dve.wait_ge(s_bae, 4)
            link(dve.scalar_tensor_tensor(g_, y_, 0.0, l1_, ALU.max, ALU.add))
            dve.scalar_tensor_tensor(by_tile(g_), by_tile(g_), -1.0, ea[:, 0:H].unsqueeze(1).to_broadcast([P, NT, H]),
                                     ALU.mult, ALU.mult).then_inc(s_gates, 1)

            for c in range(2, NN + 2, 2):
                conv_qkv(c)
            nrm = nrm24.rearrange("p (q n h) -> p q n h", q=2, n=NT)
            dve.wait_ge(s_nroot, 1)
            link(dve.reciprocal(nrm24, nrm24))
            link(dve.tensor_scalar(by_tile(rq), nrm[:, 0], float(P) ** -0.5, None, ALU.mult))
            link(dve.tensor_copy(by_tile(rk), nrm[:, 1]))
            dve.tensor_tensor(bk, beta, rk, ALU.mult).then_inc(s_nrm, 1)
            conv_qkv(NN + 2)
            dve.wait_ge(s_cse, 3)
            link(dve.tensor_tensor(bec, beta, ec, ALU.mult))
            link(dve.tensor_tensor(bec, bec, rk, ALU.mult))
            dve.tensor_tensor(ed, ed, rk, ALU.mult).then_inc(s_edk, 1)
            dve.wait_ge(s_padd, N_PROD + 2)
            dve.wait_ge(s_cst, 32)
            dve.wait_ge(s_st, 2 * (CC + QC))
            for n in TILES:
                b0 = 4 * (n % 2)
                incl = mat4("incl_p" if n < 2 else "incl_s")
                dve.wait_ge(s_gBc, n + 1)
                for h in range(H):
                    dve.tensor_scalar(tile4(x_, n)[:, h], bank[b0][:, h * P:(h + 1) * P], gc[:, H * n + h:H * n + h + 1],
                                      0.0, ALU.subtract, ALU.min).then_inc(s_dif, 1)
                dve.wait_ge(s_dT, n + 1)
                for dst, b in ((mt_, b0 + 2), (at_, b0 + 3)):
                    for h in range(H):
                        order.inc(dve.scalar_tensor_tensor(tile4(dst, n)[:, h], bank[b][:, h * P:(h + 1) * P],
                                                           rk[:, H * n + h:H * n + h + 1], tile4(x_, n)[:, h],
                                                           ALU.mult, ALU.mult))
                dve.wait_ge(s_dve, order.n)
                dve.tensor_tensor(flat(mt_, n), flat(mt_, n), bank[b0 + 1], ALU.mult).then_inc(s_a1d, 1)
                order.inc(dve.tensor_tensor(tile4(at_, n), tile4(at_, n), incl, ALU.mult))
                dve.wait_ge(s_a1d, n + 1)
                link(dve.tensor_tensor(tile4(e_, n), tile4(mt_, n), mat4("level0"), ALU.mult))
                dve.tensor_tensor(tile4(e_, n), mat4("ident"), tile4(e_, n), ALU.subtract).then_inc(s_e1, 1)
            dve.wait_ge(s_ln, 1)
            for c in range(CC):
                dve.scalar_tensor_tensor(cb3[:, c], bank[6][:, 0:T], -1.0 / (CC * P), cb3[:, c], ALU.mult, ALU.add)\
                   .then_inc(s_xc, 1)
            for l, ns in levels():
                for n in ns:
                    dve.wait_ge(s_pq, LT_AT[l, n])
                    if l < LEVELS - 1:
                        dve.tensor_tensor(halves(flat(d_, n), l, 0), halves(flat(d_, n), l, 0), halves(bank[2 * n], l, 0),
                                          ALU.subtract).then_inc(s_de, 1)
                    else:
                        dve.nop().then_inc(s_de, 1)
                    dve.tensor_tensor(halves(flat(e_, n), l, 1), halves(flat(e_, n), l, 1), halves(bank[2 * n + 1], l, 1),
                                      ALU.subtract).then_inc(s_de, 1)
                if l == NT + 1:
                    dve.wait_ge(s_lroot, 1)
                    dve.wait_ge(s_lsq, CC)
                    link(dve.reciprocal(lroot, lroot))
                    for c in range(CC):
                        dve.tensor_tensor(cb3[:, c], cb3[:, c], lroot, ALU.mult).then_inc(s_lnd, 1)
            for n in (1, 2):
                dve.wait_ge(s_de, 2 * N_STEPS)
                dve.tensor_tensor(tile4(d_, n), qkv3[:, 0:H, n * P:(n + 1) * P], tile4(eg_, n), ALU.mult).then_inc(s_qg, 1)


            def normed(n):
                dve.wait_ge(s_ort, n + 1)
                link(dve.reciprocal(y_[:, 4:8], y_[:, 0:4]))
                link(dve.tensor_tensor(y_[:, 4:8], y_[:, 4:8], rq[:, H * n:H * (n + 1)], ALU.mult))
                for h in range(H):
                    dve.tensor_scalar(tile4(at_, n)[:, h], bank[2][:, h * P:(h + 1) * P], y_[:, 4 + h:5 + h],
                                      None, ALU.mult).then_inc(s_on, 1)

            def gated(n):
                dve.wait_ge(s_ot, n + 1)
                dve.scalar_tensor_tensor(oT3[:, :, n * P:(n + 1) * P], bank[7].rearrange("p (h t) -> p h t", h=H),
                                         col("onorm"), zs3[:, :, n * P:(n + 1) * P], ALU.mult, ALU.mult).then_inc(s_oTd, 1)

            def residual(n):
                for a in range(2):
                    dve.wait_ge(s_mix, 2 * n + a + 1)
                    dve.tensor_tensor(xt3[:, n, a * 512:(a + 1) * 512], xt3[:, n, a * 512:(a + 1) * 512],
                                      bank[OUT_BANK[n][a]], ALU.add).then_inc(s_x2, 1)

            def h_rows(n):
                dve.wait_ge(s_x2r, n + 1)
                link(dve.reciprocal(rr[:, n:n + 1], rr[:, n:n + 1]))
                dve.scalar_tensor_tensor(h23[:, n], xt3[:, n], rr[:, n:n + 1], gff[:, :], ALU.mult, ALU.mult)\
                   .then_inc(s_h2, 1)

            def h_turned(n):
                dve.wait_ge(s_h2t, 2 * n + 2)
                dve.tensor_copy(hT3[:, 4:8, n * P:(n + 1) * P], bank[7].rearrange("p (k t) -> p k t", k=4))\
                   .then_inc(s_h2te, 1)

            dve.wait_ge(s_s, 1)
            dve.tensor_copy(s_prm, bank[3]).then_inc(s_sd, 1)
            normed(0)
            gated(0)
            dve.wait_ge(s_s, 2)
            for h in range(H):
                last = dve.scalar_tensor_tensor(s_prm[:, h * P:(h + 1) * P], s_prm[:, h * P:(h + 1) * P],
                                                tile4(eg_, 1)[:, h, P - 1:P], bank[3][:, h * P:(h + 1) * P],
                                                ALU.mult, ALU.add)
                if h < H - 1:
                    order.inc(last)
            last.then_inc(s_sd, 1)
            normed(1)
            dve.wait_ge(s_xt, 16 * NT)
            residual(0)
            gated(1)
            dve.wait_ge(s_gff, 16)
            h_rows(0)
            normed(2)
            gated(2)
            residual(1)
            h_turned(0)
            h_rows(1)

            iota = cst[:, X_IOTA:X_IOTA + BLK]

            def choose(n):
                dve.wait_ge(s_lg, n + 1)
                link(dve.tensor_tensor(lg[:, n], bank[LOGIT_BANK[n]][:, 0:NE], col("b_router", 0, NE), ALU.add))
                link(dve.max(v8[:, n], lg[:, n]))
                dve.tensor_scalar(nv0[:, n:n + 1], v8[:, n, 0:1], -1.0, None, ALU.mult).then_inc(s_gx, 1)
                link(dve.max_index(i8[:, n].bitcast(U32), v8[:, n], lg[:, n]))
                link(dve.tensor_copy(if8[:, n], i8[:, n].bitcast(U32)))
                link(dve.tensor_scalar(mall[:, n], iota[:, 0:NE], if8[:, n, 0:1], None, ALU.is_equal))
                for j in range(1, TOPK):
                    ins = dve.scalar_tensor_tensor(mall[:, n], iota[:, 0:NE], if8[:, n, j:j + 1], mall[:, n],
                                                   ALU.is_equal, ALU.add)
                    if j < TOPK - 1:
                        link(ins)
                    else:
                        ins.then_inc(s_m, 1)

            residual(2)
            for n in TILES:
                order.inc(dve.memset(tok2[:, n, 0:1], float(P * n)))
                order.inc(dve.tensor_copy(tok2[:, n, 1:2], cst[:, X_SEL + NE:X_SEL + NE + 1]))
            dve.wait_ge(s_dve, order.n)
            h_turned(1)
            h_rows(2)
            choose(0)
            h_turned(2)
            choose(1)
            choose(2)
            dve.wait_ge(s_pp, 1)
            places = bank[6][:, 0:NT * NE].rearrange("p (n e) -> p n e", n=NT)
            pos_n = pos.rearrange("p e n -> p n e")
            link(dve.scalar_tensor_tensor(pos_n, places, 1.0, mall, ALU.add, ALU.mult))
            link(dve.tensor_scalar(pos_n, pos_n, -1.0, None, ALU.add))
            dve.tensor_tensor(hit[:, :, 0:2], pos_n[:, :, 0:2].unsqueeze(3).to_broadcast([P, NT, 2, BLK]),
                              iota.unsqueeze(1).unsqueeze(1).to_broadcast([P, NT, 2, BLK]), ALU.is_equal).then_inc(s_hit, 1)
            link(dve.tensor_copy(cntB, bank[6][:, NT * NE:(NT + 1) * NE]))
            ids = bank[0][:, 0:2 * NPAIR].rearrange("p (q c) -> p q c", c=2)

            def indices(part, q, r):
                dve.wait_ge(s_id, part)
                link(dve.tensor_copy(idxf[:, q:r], ids[:, q:r, 0]))
                dve.tensor_tensor(idx[:, q:r], idxf[:, q:r], ids[:, q:r, 1], ALU.add).then_inc(s_idx, 1)

            for n in TILES:
                dve.tensor_tensor(hit[:, n, 2:], pos[:, 2:, n].unsqueeze(2).to_broadcast([P, NE - 2, BLK]),
                                  iota.unsqueeze(1).to_broadcast([P, NE - 2, BLK]), ALU.is_equal).then_inc(s_hit, 1)
                if n == 0:
                    indices(1, 0, 1)
            indices(2, 1, NPAIR)

            def tables():
                dve.wait_ge(s_ge, NT)
                link(dve.reciprocal(gsum, gsum))
                for n in TILES:
                    link(dve.tensor_scalar(gate[:, n], gate[:, n], gsum[:, n:n + 1], None, ALU.mult))
                link(dve.tensor_scalar(nxb, cntB, float(BLK), None, ALU.is_gt))
                for b in range(2, T // BLK):
                    link(dve.scalar_tensor_tensor(nxb, cntB, float(BLK * b), nxb, ALU.is_gt, ALU.add))
                link(dve.tensor_copy(cumA, nxb))
                a, b, s = cumA, cumB, 1
                while s < NE:
                    link(dve.tensor_copy(b[:, 0:s], a[:, 0:s]))
                    link(dve.tensor_tensor(b[:, s:], a[:, s:], a[:, 0:NE - s], ALU.add))
                    a, b, s = b, a, 2 * s
                link(dve.tensor_tensor(cmpx, a.unsqueeze(1).to_broadcast([P, NX, NE]),
                                       iota[:, 0:NX].unsqueeze(2).to_broadcast([P, NX, NE]), ALU.is_le))
                link(dve.tensor_reduce(ex, cmpx, AX_X, ALU.add))
                link(dve.tensor_scalar(ex, ex, float(NE - 1), None, ALU.min))
                link(dve.tensor_tensor(cmpx, cmpx, nxb.unsqueeze(1).to_broadcast([P, NX, NE]), ALU.mult))
                link(dve.tensor_reduce(stx, cmpx, AX_X, ALU.add))
                link(dve.tensor_tensor(off64, iota[:, 0:NX], stx, ALU.subtract))
                link(dve.tensor_scalar(off64, off64, 1.0, float(BLK), ALU.add, ALU.mult))
                link(dve.tensor_copy(tab[:, 0:NX], ex))
                dve.tensor_copy(tab[:, NX:NX + 1], a[:, NE - 1:NE]).then_inc(s_tabs, 1)
                link(dve.tensor_tensor(b, a, nxb, ALU.subtract))
                link(dve.tensor_tensor(b, b, iota[:, 0:NE], ALU.subtract))
                link(dve.tensor_scalar(b, b, float(NE - 1), float(BLK), ALU.add, ALU.mult))
                four = [P, NT, TOPK, NE]
                link(dve.tensor_tensor(pick, iota[:, 0:NE].unsqueeze(1).unsqueeze(1).to_broadcast(four),
                                       if8[:, :, 0:TOPK].unsqueeze(3).to_broadcast(four), ALU.is_equal))
                link(dve.tensor_tensor(pick2, pick, pos.rearrange("p e n -> p n e").unsqueeze(2).to_broadcast(four),
                                       ALU.mult))
                link(dve.tensor_reduce(posj, pick2, AX_X, ALU.add))
                link(dve.tensor_tensor(pick2, pick, b.unsqueeze(1).unsqueeze(1).to_broadcast(four), ALU.mult))
                link(dve.tensor_reduce(movej, pick2, AX_X, ALU.add))
                link(dve.scalar_tensor_tensor(movej, posj, float(BLK), movej, ALU.is_ge, ALU.mult))
                link(dve.tensor_tensor(posj, posj, movej, ALU.add))
                dve.scalar_tensor_tensor(rowi, if8[:, :, 0:TOPK], float(BLK), posj, ALU.mult, ALU.add).then_inc(s_row, 1)

            def item_slots():
                link(dve.tensor_tensor(cmpx, iota[:, 0:NE].unsqueeze(1).to_broadcast([P, NX, NE]),
                                       ex.unsqueeze(2).to_broadcast([P, NX, NE]), ALU.is_equal))
                for n in TILES:
                    link(dve.tensor_tensor(item_pos, cmpx, pos[:, :, n].unsqueeze(1).to_broadcast([P, NX, NE]), ALU.mult))
                    link(dve.tensor_reduce(posx[:, n], item_pos, AX_X, ALU.add))
                    link(dve.tensor_tensor(posx[:, n], posx[:, n], off64, ALU.subtract))
                    dve.tensor_tensor(hitx[:, n], posx[:, n].unsqueeze(2).to_broadcast([P, NX, BLK]),
                                      iota.unsqueeze(1).to_broadcast([P, NX, BLK]), ALU.is_equal).then_inc(s_hito, 1)

            def rows_t(turned):
                dve.wait_ge(s_xgt, turned)
                dve.tensor_copy(xTe[:, 0:4, :], bank[4].rearrange("p (k s) -> p k s", k=4)).then_inc(s_xte, 1)

            def select(x, e):
                dve.tensor_scalar(sel_sb[0:3 * NE, x], mat("ones")[0:3 * NE, 0:BLK],
                                  cst[0:3 * NE, bass.ds(e + X_SEL, 1)], None, ALU.mult).then_inc(s_sel, 1)

            def expert(item):
                dve.wait_ge(s_gu, item + 1)
                dve.tensor_scalar(g_s, bank[0], LIMIT, None, ALU.min).then_inc(s_g, 1)
                dve.tensor_scalar(l_s, bank[1], -LIMIT, LIMIT, ALU.max, ALU.min).then_inc(s_lin, 1)
                dve.wait_ge(s_sig, item + 1)
                dve.wait_ge(s_g, item + 1)
                dve.tensor_tensor(t_s, g_s, sg_b, ALU.mult).then_inc(s_lin, 1)
                dve.wait_ge(s_lin, item * 2 + 2)
                dve.scalar_tensor_tensor(a_s, l_s, 1.0, t_s, ALU.add, ALU.mult).then_inc(s_act, 1)
                dve.wait_ge(s_att, item + 1)
                dve.tensor_copy(actT, bank[6]).then_inc(s_atr, 1)

            def pair(p, between=None):
                rows_t(p + 1)
                for x in range(2):
                    select(x, 2 * p + x)
                for x in range(2):
                    expert(2 * p + x)
                    if x == 0 and between:
                        between()

            pair(0, tables)
            pair(1, item_slots)
            dve.wait_ge(s_ido, 1)
            ids_x = bank[2][0:BLK, 0:2 * NX].rearrange("p (i c) -> p i c", c=2)
            link(dve.tensor_copy(idxxf[0:BLK], ids_x[:, :, 0]))
            dve.tensor_tensor(idxx[0:BLK], idxxf[0:BLK], ids_x[:, :, 1], ALU.add).then_inc(s_idxo, 1)
            with dve.Fori(2, NPAIR) as p:
                pair(p)
            n_extra = dve.value_load(tab[0:1, NX:NX + 1], min_val=0, max_val=NX)
            with dve.Fori(0, NX) as i:
                with dve.If(i < n_extra):
                    e = dve.value_load(tab[0:1, bass.ds(i, 1)], min_val=0, max_val=NE - 1)
                    rows_t(i + (NPAIR + 1))
                    select(0, e)
                    expert(i + NE)
            dve.wait_ge(s_gfin, 16)
            for n in TILES:
                dve.wait_ge(s_yg[n], 16 * TOPK)
                for j in range(TOPK):
                    row = ring[:, (n * TOPK + j) * D:(n * TOPK + j + 1) * D]
                    ins = dve.scalar_tensor_tensor(xt3[:, n], row, gate[:, n, j:j + 1], xt3[:, n], ALU.mult, ALU.add)
                    if j < TOPK - 1:
                        link(ins)
                    else:
                        ins.then_inc(s_acc, 1)
                dve.wait_ge(s_frt, n + 1)
                link(dve.reciprocal(rr[:, n:n + 1], rr[:, n:n + 1]))
                dve.scalar_tensor_tensor(xt3[:, n], xt3[:, n], rr[:, n:n + 1], gff[:, :], ALU.mult, ALU.mult)\
                   .then_inc(s_acc, 1)

        @block.tensor
        def _(pe):
            pe.wait_ge(s_ones, 1)
            for k in range(KD):
                pe.wait_ge(s_sq, k + 1)
                mm = pe.matmul(bank[4][:, 0:T], mat("ones"), sq3[:, k], start=(k == 0), stop=(k == KD - 1))
            mm.then_inc(s_ssum, 1)

            def taken(j):
                return j + 1 if j < 2 * CC else (2 * CC + 2 * (j + 1 - 2 * CC) if j < 2 * CC + QC
                                                 else 2 * CC + 2 * QC + (j + 1 - 2 * CC - QC))

            def project_in(j):
                pe.wait_ge(s_win[j // 4 % 2], 16 * (j // 8 + 2))
                if 4 <= j < NJ - 2:
                    pe.wait_ge(s_evac, taken(j - 4))
                for k in range(KD):
                    if j == 0:
                        pe.wait_ge(s_h, k + 1)
                    mm = pe.matmul(bank[JOB_BANK[j]][:, 0:T], win4[:, j // 4 % 2, k, (j % 4) * P:(j % 4 + 1) * P], hT3[:, k],
                                   start=(k == 0), stop=(k == KD - 1))
                mm.then_inc(s_proj, 1)

            for j in range(JZ + 2):
                project_in(j)
                if j == JQ - 1:
                    pe.wait_ge(s_ba_in, 16)
                    for n in TILES:
                        for k in range(KD):
                            mm = pe.matmul(bank[5][:, 8 * n:8 * n + 8], hT3[:, k, n * P:(n + 1) * P],
                                           gff[:, 8 * k:8 * k + 8], start=(k == 0), stop=(k == KD - 1))
                    mm.then_inc(s_ba, 1)
                if j == JZ - 3:
                    for c in range(NN):
                        pe.wait_ge(s_qsq, c + 1)
                        for n in TILES:
                            at_col = 96 + (c // H) * NT * H + H * n + c % H
                            mm = pe.matmul(bank[5][:, at_col:at_col + 1], sq3[:, c, n * P:(n + 1) * P], mat("ones")[:, 0:1],
                                           start=True, stop=True)
                    mm.then_inc(s_cn, 1)
                if j == JZ - 1:
                    pe.wait_ge(s_nroot, 1)
                    pe.wait_ge(s_gates, 1)
                    pe.wait_ge(s_cst, 32)
                    for n in TILES:
                        pe.matmul(bank[5][:, 32 + H * n:32 + H * (n + 1)], mat("incl_p" if n < 2 else "incl_s"),
                                  g_[:, H * n:H * (n + 1)], start=True, stop=True)
                        mm = pe.matmul(bank[5][:, 64 + H * n:64 + H * (n + 1)], mat("later_p" if n < 2 else "later_s"),
                                       g_[:, H * n:H * (n + 1)], start=True, stop=True)
                    mm.then_inc(s_cs, 1)

            def turn_vk(n):
                tk = slice(n * P, (n + 1) * P)
                if n:
                    pe.wait_ge(s_vke, 3 * H * n)
                for h in range(H):
                    hs = slice(h * P, (h + 1) * P)
                    pe.transpose(bank[6][:, hs], qkv3[:, 2 * H + h, tk], mat("ident"))
                    mm = pe.transpose(bank[7][:, hs], qkv3[:, H + h, tk], mat("ident"))
                mm.then_inc(s_vk, 1)

            pe.wait_ge(s_nrm, 1)
            pe.wait_ge(s_cse, 3)
            pe.wait_ge(s_evac, taken(JZ + 1))
            for n in TILES:
                b0 = 4 * (n % 2)
                if n == 2:
                    pe.wait_ge(s_a1d, 1)
                tk = slice(n * P, (n + 1) * P)
                incl = mat("incl_p" if n < 2 else "incl_s")
                for h in range(H):
                    pe.matmul(bank[b0][:, h * P:(h + 1) * P], g_[:, H * n + h:H * n + h + 1].to_broadcast([P, P]), incl,
                              start=True, stop=True)
                mm = None
                for h in range(H):
                    hs = slice(h * P, (h + 1) * P)
                    one = slice(H * n + h, H * n + h + 1)
                    pe.matmul(bank[b0 + 2][:, hs], qkv3[:, H + h, tk], qkv3[:, H + h, tk], start=True, stop=True)
                    pe.matmul(bank[b0 + 3][:, hs], qkv3[:, H + h, tk], qkv3[:, h, tk], start=True, stop=True)
                    mm = pe.matmul(bank[b0 + 1][:, hs], bk[:, one].to_broadcast([P, P]), mat("ident"), start=True, stop=True)
                mm.then_inc(s_a1, 1)
            pe.wait_ge(s_a1d, 2)
            project_in(JZ + 2)
            pe.wait_ge(s_dwc, 4)
            pe.wait_ge(s_padd, N_PROD + 2)
            for c in range(CC):
                mm = pe.matmul(bank[6][:, 0:T], mat("ones"), cb3[:, c], start=(c == 0), stop=(c == CC - 1))
            mm.then_inc(s_ln, 1)
            project_in(JZ + 3)
            for n in TILES:
                pe.wait_ge(s_e1, n + 1 if n else NT)
                for h in range(H):
                    mm = pe.transpose(bank[2 * n][:, h * P:(h + 1) * P], tile4(e_, n)[:, h], mat("ident"))
                mm.then_inc(s_tr, 1)
            pe.wait_ge(s_d1, NT)
            for l, ns in levels():
                for n in ns:
                    if l > 1:
                        pe.wait_ge(s_de, 2 * LT_AT[l - 1, n])
                    pe.wait_ge(s_lt, LT_AT[l, n])
                    for h in range(H):
                        mm = pe.matmul(bank[2 * n][:, h * P:(h + 1) * P], tile4(lt_, n)[:, h], tile4(d_, n)[:, h],
                                       start=True, stop=True)
                    mm.then_inc(s_x, 1)
                if l <= NT:
                    if l == 1:
                        pe.wait_ge(s_silu, QC)
                        pe.wait_ge(s_xc, CC)
                        pe.wait_ge(s_evac, taken(NJ - 1))
                    turn_vk(l - 1)
                elif l == NT + 1:
                    pe.wait_ge(s_vke, 3 * H * NT)
                    for c in range(CC):
                        mm = pe.matmul(bank[6][:, 0:T], mat("ones"), lsq3[:, c], start=(c == 0), stop=(c == CC - 1))
                    mm.then_inc(s_ln2, 1)
                for n in ns:
                    pe.wait_ge(s_xs, LT_AT[l, n])
                    for h in range(H):
                        hs = slice(h * P, (h + 1) * P)
                        if l < LEVELS - 1:
                            pe.matmul(halves(bank[2 * n][:, hs], l, 0), tile4(e_, n)[:, h], halves(tile4(x_, n)[:, h], l, 0),
                                      start=True, stop=True)
                        mm = pe.matmul(halves(bank[2 * n + 1][:, hs], l, 1), tile4(x_, n)[:, h],
                                       halves(tile4(e_, n)[:, h], l, 1), start=True, stop=True)
                    mm.then_inc(s_pq, 1)
            pe.wait_ge(s_de, 2 * N_STEPS)
            pe.wait_ge(s_vke, 3 * H * NT)
            pe.wait_ge(s_state, 16)

            def w_rows(n):
                for h in range(H):
                    mm = pe.matmul(bank[4 * (n - 1)][:, h * P:(h + 1) * P], tile4(kbe_, n)[:, h], tile4(e_, n)[:, h],
                                   start=True, stop=True)
                mm.then_inc(s_wt, 1)

            def own_states():
                pe.wait_ge(s_wte, 2)
                pe.wait_ge(s_qg, 2)
                for h in range(H):
                    out = bank[5 + h // 2].rearrange("p (h g t) -> p h g t", h=2, g=2)[:, h % 2]
                    for b in range(NB):
                        mm = pe.matmul(out[:, :, TS * b:TS * (b + 1)], smp4[:, b, h], qw5[:, :, 2, h, TS * b:TS * (b + 1)],
                                       start=True, stop=True)
                mm.then_inc(s_t1, 1)

            def term(h, g):
                c = (h // 2) * 512 + (h % 2) * 256 + g * P
                return lt_[:, c:c + P]

            def v_new(n):
                if n == 1:
                    pe.wait_ge(s_sd, 1)
                    pe.wait_ge(s_wte, 1)
                if n == 2:
                    pe.wait_ge(s_t1e, 2)
                if n:
                    pe.wait_ge(s_ve, n)
                for h in range(H):
                    hs = slice(h * P, (h + 1) * P)
                    mm = pe.matmul(bank[1][:, hs], tile4(e_, n)[:, h], tile4(vb_, n)[:, h], start=True, stop=(n == 0))
                    if n == 1:
                        mm = pe.matmul(bank[1][:, hs], tile4(x_, n)[:, h], s_prm[:, hs], start=False, stop=True)
                    if n == 2:
                        mm = pe.matmul(bank[1][:, hs], term(h, 1), mat("ident"), start=False, stop=True)
                mm.then_inc(s_v, 1)

            def outputs(n):
                pe.wait_ge(s_ve, n + 1)
                if n == 1:
                    pe.wait_ge(s_qg, 1)
                if n:
                    pe.wait_ge(s_on, H * n)
                for h in range(H):
                    hs = slice(h * P, (h + 1) * P)
                    if n == 1:
                        pe.matmul(bank[2][:, hs], tile4(d_, n)[:, h], s_prm[:, hs], start=True, stop=False)
                    if n == 2:
                        pe.matmul(bank[2][:, hs], term(h, 0), mat("ident"), start=True, stop=False)
                    mm = pe.matmul(bank[2][:, hs], tile4(at_, n)[:, h], tile4(kbe_, n)[:, h], start=(n == 0), stop=True)
                mm.then_inc(s_o, 1)

            def state(n):
                if n:
                    pe.wait_ge(s_sd, n)
                for h in range(H):
                    mm = pe.matmul(bank[3][:, h * P:(h + 1) * P], tile4(kd_, n)[:, h], tile4(kbe_, n)[:, h],
                                   start=True, stop=True)
                mm.then_inc(s_s, 1)

            def turn_o(n):
                pe.wait_ge(s_on, H * (n + 1))
                if n:
                    pe.wait_ge(s_oTd, n)
                for h in range(H):
                    mm = pe.transpose(bank[7][:, h * P:(h + 1) * P], tile4(at_, n)[:, h], mat("ident"))
                mm.then_inc(s_ot, 1)

            def state_of(b):
                pe.wait_ge(s_km, b + 1)
                if b >= 3:
                    pe.wait_ge(s_sev, b - 2)
                for h in range(H):
                    hs = slice(h * P, (h + 1) * P)
                    mm = pe.matmul(bank[STATE_BANK[b % 3]][:, hs], k_only[b][:, hs], flat(kbe_, 2)[:, hs],
                                   start=True, stop=True)
                mm.then_inc(s_s, 1)

            def project(n, a):
                if n == 2:
                    pe.wait_ge(s_x2, 2)
                for i, k in enumerate([4, 5, 6, 7, 0, 1, 2, 3]):
                    if k == 0:
                        pe.wait_ge(s_oTd, n + 1)
                    cat = cb3[:, k - 4] if k >= 4 else oT3[:, k]
                    mm = pe.matmul(bank[OUT_BANK[n][a]], cat[:, n * P:(n + 1) * P], win4[:, a, k, :],
                                   start=(i == 0), stop=(i == KD - 1))
                mm.then_inc(s_mix, 1)

            def turn_h(n):
                pe.wait_ge(s_h2, n + 1)
                if n:
                    pe.wait_ge(s_h2te, 2 * n)
                for a in range(2):
                    for k in range(4):
                        mm = pe.transpose(bank[(2, 7)[a]][:, k * P:(k + 1) * P],
                                          h23[:, n, (4 * a + k) * P:(4 * a + k + 1) * P], mat("ident"))
                    mm.then_inc(s_h2t, 1)

            def logits(n):
                pe.wait_ge(s_h2te, 2 * n + 2)
                for k in range(KD):
                    mm = pe.matmul(bank[LOGIT_BANK[n]][:, 0:NE], hT3[:, k, n * P:(n + 1) * P], wr[:, k, :],
                                   start=(k == 0), stop=(k == KD - 1))
                mm.then_inc(s_lg, 1)

            v_new(0)
            w_rows(1)
            w_rows(2)
            outputs(0)
            state(0)
            own_states()
            turn_o(0)
            v_new(1)
            outputs(1)
            state(1)
            pe.wait_ge(s_conf, CC)
            for i in range(2):
                pe.wait_ge(s_win[i], 80)
            project(0, 0)
            project(0, 1)
            v_new(2)
            turn_o(1)
            outputs(2)
            project(1, 0)
            project(1, 1)
            turn_o(2)
            project(2, 0)
            turn_h(0)
            project(2, 1)
            turn_h(1)
            pe.wait_ge(s_wr, 16)
            pe.wait_ge(s_x2, 4)
            logits(0)
            logits(1)
            turn_h(2)
            pe.wait_ge(s_ve, NT)
            pe.wait_ge(s_sd, 2)
            pe.wait_ge(s_x2, 6)
            state_of(0)
            state_of(1)
            logits(2)
            for b in range(2, 5):
                state_of(b)
            pe.wait_ge(s_m, NT)
            for n in range(NT + 1):
                for m in range(min(n + 1, NT)):
                    mm = pe.matmul(bank[6][:, n * NE:(n + 1) * NE], mat("strict" if m == n else "ones"), mall[:, m],
                                   start=(m == 0), stop=(m == min(n, NT - 1)))
            mm.then_inc(s_pp, 1)
            state_of(5)

            def slot_ids(q):
                for n in TILES:
                    mm = pe.matmul(bank[0][:, 2 * q:2 * q + 2], hit[:, n, 2 * q:2 * q + 2, :].rearrange("p e s -> p (e s)"),
                                   tok2[:, n, :], start=(n == 0), stop=(n == NT - 1))
                return mm

            pe.wait_ge(s_hit, 1)
            slot_ids(0).then_inc(s_id, 1)
            state_of(6)
            state_of(7)
            pe.wait_ge(s_hit, 1 + NT)
            for q in range(1, NPAIR):
                mm = slot_ids(q)
            mm.then_inc(s_id, 1)

            def turn_rows(item):
                pe.wait_ge(s_gat, item * 16 + 16)
                for k in range(KD):
                    mm = pe.transpose(bank[4 + k // 4][:, (k % 4) * P:(k % 4 + 1) * P], xg[:, k * P:(k + 1) * P], mat("ident"))
                mm.then_inc(s_xgt, 1)
                pe.wait_ge(s_xte, item * 2 + 2)

            def bias_rows(x, out, columns, close):
                for a in range(2):
                    mm = pe.matmul(out[a * BLK:(a + 1) * BLK], sel_sb[0:3 * NE, x, :],
                                   bparts[0:3 * NE, columns + a * 512:columns + (a + 1) * 512], start=True, stop=False,
                                   skip_group_check=True)

            def expert(x, item):
                pe.wait_ge(s_sel, item + 1)
                bias_rows(x, bank[0], 0, False)
                bias_rows(x, bank[1], F, False)
                for k in range(KD):
                    pe.wait_ge(s_w[SLOT_OF[k]], item * 16 + 16)
                    for half in range(2):
                        for a in range(2):
                            c = SLOT_OF[k] * SLOT + half * F + a * 512
                            mm = pe.matmul(bank[half][a * BLK:(a + 1) * BLK], xTe[:, k, x * BLK:(x + 1) * BLK],
                                           ring[:, c:c + 512], start=False, stop=(k == KD - 1), skip_group_check=True)
                    mm.then_inc(s_wu, 1)
                pe.drain().then_inc(s_gu, 1)
                pe.wait_ge(s_act, item + 1)
                for j in range(4):
                    mm = pe.transpose(bank[6][:, j * P:(j + 1) * P], a_s[:, j * P:(j + 1) * P], mat("ident"))
                mm.then_inc(s_att, 1)

            def down(x, item, first):
                if not first:
                    pe.wait_ge(s_yc, item)
                bias_rows(x, bank[7], 2 * F, False)
                pe.wait_ge(s_atr, item + 1)
                for k in range(KD):
                    if k % 2 == 0:
                        pe.wait_ge(s_w[KD + k // 2], item * 16 + 16)
                    for a in range(2):
                        c = (KD + k // 2) * SLOT + (k % 2) * D + a * 512
                        mm = pe.matmul(bank[7][a * BLK:(a + 1) * BLK], actT[:, (k % 4) * P + (k // 4) * BLK:][:, 0:BLK],
                                       ring[:, c:c + 512], start=False, stop=(k == KD - 1), skip_group_check=True)
                    if k % 2 == 1:
                        mm.then_inc(s_wu, 1)
                pe.drain().then_inc(s_dn, 1)

            def pair(p, first):
                turn_rows(p)
                for x in range(2):
                    expert(x, 2 * p + x)
                    down(x, 2 * p + x, first and x == 0)

            pair(0, True)
            pair(1, False)
            pe.wait_ge(s_hito, NT)
            for i in range(NX):
                for n in TILES:
                    mm = pe.matmul(bank[2][0:BLK, 2 * i:2 * i + 2], hitx[:, n, i, :], tok2[:, n, :],
                                   start=(n == 0), stop=(n == NT - 1))
            mm.then_inc(s_ido, 1)
            with pe.Fori(2, NPAIR) as p:
                pair(p, False)
            pe.wait_ge(s_tabs, 1)
            n_extra = pe.value_load(tab[0:1, NX:NX + 1], min_val=0, max_val=NX)
            with pe.Fori(0, NX) as i:
                with pe.If(i < n_extra):
                    turn_rows(i + NPAIR)
                    expert(0, i + NE)
                    down(0, i + NE, False)


INPUTS = ["xT", "x_prompt", "x_sample", "state_gdn", "hist_q", "hist_u", "params", "consts", "w_in", "w_out", "g_ffn",
          "g_final", "w_router", "w_gate_up", "b_gate_up", "w_down", "b_down"]
OUTPUTS = {"y": (T, D), "sp": (H, P, P), "ss": (NB, H, P, P), "q_state": (P, QC * 9 * 3), "u_state": (P, CC * 9 * 30)}


def shape_constants():
    j, i = np.arange(P)[:, None], np.arange(P)[None, :]
    same = (j // TS) == (i // TS)
    mats = {"ident": j == i, "ones": (j >= 0) & (i >= 0), "incl_p": i >= j, "incl_s": (i >= j) & same, "later_p": j > i,
            "later_s": (j > i) & same, "strict": j < i}
    for l in range(LEVELS):
        s = 1 << l
        mats[f"level{l}"] = (i // (2 * s) == j // (2 * s)) & (i // s % 2 == 1) & (j // s % 2 == 0)
    cols = np.zeros((P, NXC), np.float32)
    cols[:, X_IOTA:X_IOTA + BLK] = np.arange(BLK)
    cols[:, X_BLK:X_BLK + NB] = (np.arange(P)[:, None] // TS) == np.arange(NB)
    cols[:, X_SEL:X_SEL + NE] = (np.arange(P)[:, None] % NE) == np.arange(NE)
    cols[:, X_SEL + NE] = np.arange(P)
    return np.concatenate([mats[m].astype(np.float32) for m in MATS] + [cols], axis=1)


def kernel(x_prompt, x_sample, state_gdn, state_qkv_conv, state_dwconv, norm_mix_g, w_in, w_conv_qkv, a_log, dt_bias,
           w_onorm, b_glu, w_dw, b_dw, ln_g, ln_b, w_out, norm_ffn_g, w_router, b_router, w_gate_up, b_gate_up, w_down,
           b_down, norm_final_g):
    from concourse import bacc
    from concourse.bass_utils import run_bass_kernel_spmd

    xp = np.asarray(x_prompt).reshape(TP, D)
    xs = np.asarray(x_sample).reshape(NB * TS, D)

    def channels(a, rows):
        return np.asarray(a).reshape(rows, -1, P).transpose(2, 0, 1).reshape(P, -1)

    def rows(a):
        return np.broadcast_to(np.asarray(a).reshape(1, -1), (P, np.asarray(a).size))

    params = np.concatenate([channels(norm_mix_g, 1), channels(w_conv_qkv, QW), channels(w_dw, DW), channels(b_glu, 1),
                             channels(b_dw, 1), channels(ln_g, 1), channels(ln_b, 1), channels(w_onorm, 1), rows(a_log),
                             rows(dt_bias), rows(b_router)], axis=1)

    def history(a, w):
        return np.asarray(a)[0].reshape(NB, w, -1, P).transpose(3, 2, 0, 1).reshape(P, -1)

    arrays = {
        "xT": np.concatenate([xp, xs]).T, "x_prompt": xp, "x_sample": xs, "state_gdn": np.asarray(state_gdn)[0],
        "hist_q": history(state_qkv_conv, QW - 1), "hist_u": history(state_dwconv, DW - 1), "params": params,
        "consts": shape_constants(), "w_in": np.asarray(w_in)[0], "w_out": np.asarray(w_out)[0],
        "g_ffn": np.asarray(norm_ffn_g)[0], "g_final": np.asarray(norm_final_g), "w_router": np.asarray(w_router)[0],
        "w_gate_up": np.asarray(w_gate_up)[0], "b_gate_up": np.asarray(b_gate_up)[0], "w_down": np.asarray(w_down)[0],
        "b_down": np.asarray(b_down)[0],
    }
    arrays = {n: np.ascontiguousarray(a) for n, a in arrays.items()}
    nc = bacc.Bacc("TRN2", target_bir_lowering=False, num_devices=1)
    ins = [nc.dram_tensor(f"in_{n}", arrays[n].shape, F32, kind="ExternalInput").ap() for n in INPUTS]
    outs = [nc.dram_tensor(f"out_{n}", s, F32, kind="ExternalOutput").ap() for n, s in OUTPUTS.items()]
    stream_step(nc, *ins, *outs)
    got = run_bass_kernel_spmd(nc, [{f"in_{n}": arrays[n] for n in INPUTS}], core_ids=[0]).results[0]

    y = np.asarray(got["out_y"])

    def states(a, tiles, w):
        return np.asarray(a).reshape(P, tiles, 9, w).transpose(2, 3, 1, 0).reshape(9, w, tiles * P)

    q, u = states(got["out_q_state"], QC, QW - 1), states(got["out_u_state"], CC, DW - 1)
    return (y[:TP].reshape(1, TP, D), y[TP:].reshape(NB, TS, D), np.asarray(got["out_sp"])[None, None], q[None, 0:1],
            u[None, 0:1], np.asarray(got["out_ss"])[None], q[None, 1:], u[None, 1:])
```

```python
from contextlib import ExitStack

import numpy as np

import concourse.bass as bass
from concourse import mybir

F32 = mybir.dt.float32
BF16 = mybir.dt.bfloat16
I32 = mybir.dt.int32
U32 = mybir.dt.uint32
ALU = mybir.AluOpType
ACT = mybir.ActivationFunctionType
AX_X = mybir.AxisListType.X

P = 128
D = 1024
KD = D // P
NT = 3
T = NT * P
TP = 256
NB, TS = 8, 16
H = 4
QW, DW = 4, 31
QC, CC = 12, 4
QE = QW - 1 + TP + NB * (QW - 1 + TS)
UE = DW - 1 + TP + NB * (DW - 1 + TS)
QS, US = QW - 1 + TP, DW - 1 + TP
NE, TOPK = 32, 4
F = 1024
BLK = 64
NX = (T * TOPK) // (BLK + 1)
NX_OUTER, NX_INNER = 6, 4
assert NX_OUTER * NX_INNER >= NX
NSLOT = 12
SLOT = 2 * F
RMS_EPS, LN_EPS, L2_EPS = 1e-6, 1e-5, 1e-6
LIMIT, ALPHA = 7.0, 1.702
NPAIR = NE // 2
SLOT_OF = (6, 7, 5, 0, 1, 2, 3, 4, 8, 9, 10, 11)
FIRST_ORDER = (0, 1, 2, 8, 9, 3, 4, 5, 6, 7, 10, 11)
LEVELS = 7
S_LEVELS = 4

C_Z, C_BA, C_GLU = 1536, 2048, 2056
CHUNKS = (None, None, 0, 512, 1024, C_Z)

MATS = ["ones", "ident", "strict", "incl_p", "incl_s", "later_p", "later_s"] + [f"level{l}" for l in range(LEVELS)]
M = {name: i for i, name in enumerate(MATS)}
X_IOTA, X_BLK, X_SEL = 0, 64, 64 + NB
NXC = 64 + NB + NE + 1
PARAMS, _at = {}, 0
for _name, _n in (("g_mix", KD), ("conv", QW * QC), ("dw", DW * CC), ("b_glu", 2 * CC), ("b_dw", CC), ("ln_g", CC),
                  ("ln_b", CC), ("onorm", 1), ("a_log", H), ("dt", H), ("b_router", NE)):
    PARAMS[_name] = _at
    _at += _n
NPARAM = _at


class Count:

    def __init__(self, sem):
        self.sem, self.n = sem, 0

    def inc(self, ins):
        self.n += 1
        ins.then_inc(self.sem, 1)
        return self.n


def stream_step(nc, xT, x_prompt, x_sample, state_gdn, hist_q, hist_u, params, consts, w_in, w_out, g_ffn,
                g_final, w_router, w_gate_up, b_gate_up, w_down, b_down,
                y_out, sp_out, ss_out, q_state_out, u_state_out):
    with ExitStack() as ctx:
        def sb(name, shape, dt=F32):
            return ctx.enter_context(nc.sbuf_tensor(name, shape, dt))

        def sem(name):
            return ctx.enter_context(nc.semaphore(name))

        ring = sb("ring", [P, NSLOT * SLOT])
        mats = sb("mats", [P, (len(MATS) + 1) * P])
        cst = sb("cst", [P, NXC])
        par = sb("par", [P, NPARAM])
        win = sb("win", [P, 2 * KD * 512])
        hT = sb("hT", [P, KD * T])
        xt = sb("xt", [P, NT * D])
        qkvc = sb("qkvc", [P, QC * T])
        zs = sb("zs", [P, CC * T])
        cb = sb("cb", [P, CC * T])
        oT = sb("oT", [P, CC * T])
        qst = sb("qst", [P, QC * 9 * 3])
        ust = sb("ust", [P, CC * 9 * 30])
        gff = sb("gff", [P, D])
        gates_t = sb("gates_t", [P, 12 * 17])
        epst = sb("epst", [P, 12])
        bank = [ctx.enter_context(nc.psum_tensor(f"bank{i}", [P, 512], F32))[:, :] for i in range(8)]

        def mat(name):
            return mats[:, M[name] * P:(M[name] + 1) * P]

        def mat4(name):
            return mat(name).unsqueeze(1).to_broadcast([P, H, P])

        def col(name, i=0, n=1):
            return par[:, PARAMS[name] + i:PARAMS[name] + i + n]

        at = [0]

        def scratch(n):
            at[0] += n
            assert at[0] <= NSLOT * SLOT
            return ring[:, at[0] - n:at[0]]

        qx = scratch(QE * QC)
        s_smp = scratch(NB * H * P)
        eg_ = scratch(T * H)
        d_ = scratch(T * H)
        e_ = scratch(T * H)
        x_ = scratch(T * H)
        lt_ = scratch(T * H)
        mt_ = scratch(T * H)
        at_ = scratch(T * H)
        s_prm = scratch(H * P)
        assert at[0] <= 10 * SLOT
        qx3 = qx.rearrange("p (c e) -> p c e", c=QC)
        ux3 = ring[:, QE * QC + NB * H * P + T * H:][:, 0:UE * CC].rearrange("p (c e) -> p c e", c=CC)
        base_d = QE * QC + NB * H * P + T * H
        base_lt = base_d + 3 * T * H
        sq3 = ring[:, base_lt:base_lt + KD * T].rearrange("p (k t) -> p k t", k=KD)
        rB = at_[:, 0:T]
        tail = x_[:, 0:2 * T].rearrange("p (c t) -> p c t", c=2)
        prod = [at_[:, T * (i + 1):T * (i + 2)] for i in range(3)]
        lroot = ust[:, KD * NE:KD * NE + T]
        lsq3 = hT[:, 0:CC * T].rearrange("p (c t) -> p c t", c=CC)
        qw5 = ring[:, base_d:base_d + 3 * T * H].rearrange("p (g n h t) -> p g n h t", g=3, n=NT, h=H)[:, 0:3:2]
        vb_, kbe_, kd_ = qx[:, 0:T * H], qx[:, T * H:2 * T * H], qx[:, 2 * T * H:3 * T * H]

        def tile4(x, n):
            return x[:, n * 512:(n + 1) * 512].rearrange("p (h t) -> p h t", h=H)

        def flat(x, n):
            return x[:, n * 512:(n + 1) * 512]

        hT3 = hT[:].rearrange("p (k t) -> p k t", k=KD)
        qkv3 = qkvc[:].rearrange("p (c t) -> p c t", c=QC)
        zs3 = zs[:].rearrange("p (c t) -> p c t", c=CC)
        cb3 = cb[:].rearrange("p (c t) -> p c t", c=CC)
        oT3 = oT[:].rearrange("p (c t) -> p c t", c=CC)
        win4 = win[:].rearrange("p (b k n) -> p b k n", b=2, k=KD)
        hu = cb[:, 0:CC * NB * 30].rearrange("p (c b j) -> p c b j", c=CC, b=NB)
        hq = cb[:, CC * NB * 30:CC * NB * 30 + QC * NB * 3].rearrange("p (c b j) -> p c b j", c=QC, b=NB)
        xt3 = xt[:].rearrange("p (n d) -> p n d", n=NT)
        gcol = [gates_t[:, 12 * i:12 * i + 12] for i in range(15)]
        (y_, ab_, e1_, l1_, bl_, beta, g_, gc, ec, bec, ed, ea, bk, rq, rk) = gcol

        nrm24 = gates_t[:, 12 * 15:12 * 17]

        h2 = qkvc[:, 0:NT * D]
        h23 = h2.rearrange("p (n d) -> p n d", n=NT)
        at2 = [0]

        def wscratch(n):
            at2[0] += n
            assert at2[0] <= 2 * KD * 512
            return win[:, at2[0] - n:at2[0]]

        hp = wscratch(NT * P).rearrange("p (n s) -> p n s", n=NT)
        hg = wscratch(NT * P).rearrange("p (n s) -> p n s", n=NT)
        gT = [[wscratch(T) for _ in range(2)] for _ in range(2)]
        xTe = wscratch(KD * P).rearrange("p (k s) -> p k s", k=KD)
        g_s, l_s, sg_b, t_s, a_s, actT, y_s = (wscratch(512) for _ in range(7))
        braw = ring[:, 10 * SLOT:10 * SLOT + 3 * F]
        bparts = mats[:, 3 * P:3 * P + 3 * F // 2].bitcast(BF16)
        small = oT[:, :]
        sm = [0]

        def srow(n):
            sm[0] += n
            assert sm[0] <= CC * T
            return small[:, sm[0] - n:sm[0]]

        wr = ust[:, 0:KD * NE].rearrange("p (k e) -> p k e", k=KD)
        lg = srow(NT * NE).rearrange("p (n e) -> p n e", n=NT)
        v8 = srow(NT * 8).rearrange("p (n j) -> p n j", n=NT)
        i8 = srow(NT * 8).rearrange("p (n j) -> p n j", n=NT)
        if8 = srow(NT * 8).rearrange("p (n j) -> p n j", n=NT)
        gate = srow(NT * NE).rearrange("p (n e) -> p n e", n=NT)
        gsum = srow(NT)
        nv0 = srow(NT)
        mall = srow(NT * NE // 2).bitcast(BF16).rearrange("p (n e) -> p n e", n=NT)
        ones_b = ust[:, KD * NE + T:KD * NE + T + P // 2].bitcast(BF16)
        strict_b = ust[:, KD * NE + T + P // 2:KD * NE + T + P].bitcast(BF16)
        pos = srow(NE * NT).rearrange("p (e n) -> p e n", n=NT)
        cntB = srow(NE)
        nxb = srow(NE)
        cumA, cumB = srow(NE), srow(NE)
        cmpx = cb[:, 0:NX * NE].rearrange("p (i e) -> p i e", i=NX)
        ex = srow(NX)
        stx = srow(NX)
        off64x = srow(NX_OUTER * NX_INNER + 1)
        off64 = off64x[:, 0:NX]
        tabf = srow(NX_OUTER * NX_INNER + 1)
        tab = tabf.bitcast(I32)
        pcur = srow(NT)
        ssq = epst[:, 4:4 + NT]
        sel_sb = srow(BLK).bitcast(BF16).rearrange("p (x s) -> p x s", x=2)
        rr = epst[:, 8:8 + NT]

        s_xT, s_cst, s_par, s_hist, s_state = (sem(x) for x in ("xT_in", "consts_in", "params_in", "hist_in", "state_in"))
        s_win = [sem(f"win_in{i}") for i in range(2)]
        s_ba_in, s_xt, s_gff, s_wr = sem("ba_in"), sem("x_in"), sem("gffn_in"), sem("router_in")
        s_bias, s_gfin = sem("bias_in"), sem("gfinal_in")
        s_ext = sem("histories_placed")
        s_eps = sem("eps_set")
        s_sq, s_ssum, s_rt, s_h = sem("x_squared"), sem("x_sum"), sem("x_root"), sem("hT_ready")
        s_proj, s_evac = sem("proj_ready"), sem("proj_taken")
        s_ba, s_bag, s_bae, s_gates = sem("ba_ready"), sem("ba_taken"), sem("ba_scalar"), sem("g_ready")
        s_cs, s_cse = sem("cumsum_ready"), sem("cumsum_exp")
        s_u, s_cv, s_dwc = sem("u_ready"), sem("qkv_conv"), sem("dw_conv")
        s_silu = sem("qkv_silu")
        s_nroot, s_nrm = sem("norm_roots"), sem("qk_normed")
        s_st = sem("conv_states_staged")
        s_ln, s_xc, s_lsq, s_ln2, s_lroot, s_lnd, s_conf = (sem(x) for x in (
            "ln_sum", "ln_centred", "ln_squared", "ln_sum2", "ln_root", "ln_scaled", "conformer_ready"))
        s_a1, s_gBc, s_dif, s_dT, s_a1d = (sem(x) for x in ("gram_ready", "decay_rows", "decay_diff", "decay_exp", "gram_taken"))
        s_lt, s_e1, s_tr, s_d1 = sem("level_rows"), sem("inverse_start"), sem("inverse_T"), sem("inverse_T_taken")
        s_x, s_xs, s_pq, s_de = sem("level_x"), sem("level_x_taken"), sem("level_pq"), sem("level_done")
        s_vk, s_vke = sem("vk_turned"), sem("vk_taken")
        s_wt, s_wte, s_v, s_ve = sem("w_ready"), sem("w_taken"), sem("vnew_ready"), sem("vnew_taken")
        s_qg, s_t1, s_t1e = sem("q_decayed"), sem("stream_terms"), sem("stream_terms_taken")
        s_o, s_osq, s_ort, s_on = sem("o_ready"), sem("o_squared"), sem("o_root"), sem("o_normed")
        s_ot, s_oTd = sem("o_turned"), sem("oT_ready")
        s_s, s_sd, s_km = sem("state_ready"), sem("state_taken"), sem("k_masked")
        s_mix, s_x2, s_x2q, s_x2r, s_h2 = (sem(x) for x in (
            "mix_ready", "x2_ready", "x2_squared", "x2_root", "h2_ready"))
        s_h2t, s_h2te = sem("h2_turned"), sem("h2T_ready")
        s_lg, s_gx, s_ge = sem("logits_ready"), sem("gate_max"), sem("gate_exp")
        s_m, s_pp, s_hp, s_hg = sem("mask_ready"), sem("places_ready"), sem("row_hits_ready"), sem("gate_hits_ready")
        s_tabs = sem("tables_ready")
        s_w = [sem(f"w_landed{i}") for i in range(NSLOT)]
        s_wu = sem("w_used")
        s_xgt, s_xte = sem("rows_gathered"), sem("rowsT_ready")
        s_gt, s_gtc, s_cmb, s_add = sem("gates_turned"), sem("gatesT_ready"), sem("rows_combined"), sem("rows_added")
        s_sel, s_gu, s_g, s_sig, s_act = (sem(x) for x in ("sel_ready", "gu_ready", "gate_clamped", "sig_ready", "act_ready"))
        s_att, s_atr, s_dn, s_yc = sem("act_turned"), sem("actT_ready"), sem("down_ready"), sem("y_copied")
        s_acc = sem("y_ready")
        s_pc = sem("places_extra")
        s_fin = sem("final_squared")
        s_frt = sem("final_root")
        s_stq = sem("states_out")
        s_yout = sem("y_out_stored")
        s_qsq = sem("qk_squared")
        s_cn, s_edk, s_bsplit = sem("lengths_squared"), sem("edges_scaled"), sem("bias_split")
        s_zero, s_masks, s_causal = sem("zeros_set"), sem("masks_rounded"), sem("attention_masked")
        s_bpart, s_brest = sem("bias_parts"), sem("bias_rests")
        s_lin = sem("linear_ready")
        s_dve, s_pool = sem("vector_order"), sem("pool_order")
        s_dec, s_sev, s_smp_done = sem("states_decayed"), sem("state_gain_taken"), sem("sample_states_done")
        s_ones, s_up, s_tap0, s_prd, s_padd = (sem(x) for x in (
            "ones_set", "u_ready_last", "first_taps", "tap_products", "taps_added"))
        s_tail = sem("last_taps")
        s_sout, s_ssout = sem("prompt_state_out"), sem("sample_state_out")

        JOBS = [("ga", 0), ("ga", 1), ("gb", 0), ("gb", 1), ("ga", 2), ("ga", 3), ("gb", 2), ("gb", 3)] + \
               [("qkv", c) for c in range(QC)] + [("z", c) for c in range(CC)]
        NJ = len(JOBS)
        NN = 2 * H
        JQ, JZ = 2 * CC, 2 * CC + QC
        JOB_BANK = [j % 4 for j in range(NJ - 2)] + [5, 7]
        DVE_TAPS = 10
        N_PROD = 2 * (DW - 1 - DVE_TAPS)
        TILES = range(NT)

        def levels():
            for l in range(1, LEVELS):
                yield l, [n for n in TILES if n < 2 or l < S_LEVELS]

        LT_AT, k_ = {}, 0
        for l_, ns_ in levels():
            for n_ in ns_:
                k_ += 1
                LT_AT[l_, n_] = k_
        N_STEPS = k_
        OUT_BANK = ((0, 4), (5, 6), (0, 4))
        LOGIT_BANK = (5, 6, 0)
        STATE_BANK = (1, 3, 4, 1, 3, 1, 3, 5)
        FIRST_STATES = 5

        def halves(x, l, which):
            return x.rearrange("p (g two s) -> p g two s", two=2, s=1 << l)[:, :, which]

        smp4 = s_smp.rearrange("p (b h v) -> p b h v", b=NB, h=H)
        k_only = [flat(vb_, 0), flat(vb_, 1), flat(vb_, 2), flat(kd_, 0), flat(kd_, 1), flat(kbe_, 0), flat(kbe_, 1),
                  flat(kd_, 2)]
        added = [qkvc[:, NT * D + 512 * i:NT * D + 512 * (i + 1)] for i in range(3)]

        def put_u(engine, c, done):
            engine.tensor_tensor(ux3[:, c, DW - 1:US], zs3[:, c, 0:TP], oT3[:, c, 0:TP], ALU.mult).then_inc(done, 1)
            engine.tensor_tensor(ux3[:, c, US:].rearrange("p (b e) -> p b e", b=NB)[:, :, DW - 1:],
                                 zs3[:, c, TP:].rearrange("p (b t) -> p b t", b=NB),
                                 oT3[:, c, TP:].rearrange("p (b t) -> p b t", b=NB), ALU.mult).then_inc(done, 1)

        block = ctx.enter_context(nc.Block())

        @block.sync
        def _(sp):
            sp.dma_start(hT3, xT.rearrange("(k p) t -> p k t", p=P)).then_inc(s_xT, 16)

            def load_win(i):
                c = CHUNKS[i]
                if i >= 2:
                    sp.wait_ge(s_proj, 4 * (i - 1))
                if c is None:
                    for g in range(2):
                        g0 = C_GLU + 512 * g + 256 * i
                        sp.dma_start(win4[:, i % 2, :, 256 * g:256 * (g + 1)],
                                     w_in[:, g0:g0 + 256].rearrange("(k p) n -> p k n", p=P)).then_inc(s_win[i % 2], 16)
                else:
                    sp.dma_start(win4[:, i % 2], w_in[:, c:c + 512].rearrange("(k p) n -> p k n", p=P))\
                      .then_inc(s_win[i % 2], 16)

            load_win(0)
            sp.dma_start(gff[:, 0:KD * 8].rearrange("p (k n) -> p k n", k=KD),
                         w_in[:, C_BA:C_BA + 8].rearrange("(k p) n -> p k n", p=P),
                         allow_slow_non_contiguous=True).then_inc(s_ba_in, 16)
            load_win(1)
            for j in range(3):
                rows = braw[NE * j:NE * (j + 1), :]
                sp.dma_start(rows[:, 0:2 * F], b_gate_up).then_inc(s_bias, 16)
                sp.dma_start(rows[:, 2 * F:3 * F], b_down).then_inc(s_bias, 16)
            for i in range(2, len(CHUNKS)):
                load_win(i)
            for i in range(2):
                sp.wait_ge(s_proj, 4 * (len(CHUNKS) - 1 + i))
                sp.dma_start(win4[:, i], w_out[:, 512 * i:512 * i + 512].rearrange("(k p) n -> p k n", p=P))\
                  .then_inc(s_win[i], 16)
            sp.wait_ge(s_ba, 1)
            sp.dma_start(gff[:, :], g_ffn.partition_broadcast(P)).then_inc(s_gff, 16)
            sp.wait_ge(s_conf, CC)
            sp.wait_ge(s_sout, 16)
            sp.wait_ge(s_stq, 32)
            sp.wait_ge(s_oTd, NT)
            sp.wait_ge(s_ve, NT)
            sp.wait_ge(s_dec, NB)

            def load_expert(ld, e, value):
                for i, r in enumerate(range(NSLOT) if value else FIRST_ORDER):
                    s = SLOT_OF[r]
                    if not value and s == 10:
                        ld.wait_ge(s_bsplit, 1)
                    if not value and s == 0:
                        ld.wait_ge(s_s, NB + 2)
                    if not value and s == 2:
                        ld.wait_ge(s_ssout, 16)
                    if value:
                        ld.wait_ge(s_wu, value(i))
                    dst = ring[:, s * SLOT:(s + 1) * SLOT]
                    if r < KD:
                        src = w_gate_up[bass.ds(e, 1), r * P:(r + 1) * P, :].rearrange("a p n -> (a p) n")
                        ld.dma_start(dst, src).then_inc(s_w[s], 16)
                    else:
                        r0 = (r - KD) * 2 * P
                        src = w_down[bass.ds(e, 1), r0:r0 + 2 * P, :].rearrange("a (k p) n -> (a p) k n", p=P)
                        ld.dma_start(dst.rearrange("p (k n) -> p k n", k=2), src).then_inc(s_w[s], 16)

            load_expert(sp, 0, None)
            with sp.Fori(1, NE) as e:
                load_expert(sp, e, lambda s: e * NSLOT + (s + 1 - NSLOT))
            sp.wait_ge(s_tabs, 1)
            n_extra = sp.value_load(tab[0:1, NX:NX + 1], min_val=0, max_val=NX)
            with sp.Fori(0, NX_OUTER) as g:
                with sp.If(g * NX_INNER < n_extra):
                    with sp.Fori(0, NX_INNER) as i0:
                        i = g * NX_INNER + i0
                        with sp.If(i < n_extra):
                            ei = sp.value_load(tab[0:1, bass.ds(i, 1)], min_val=0, max_val=NE - 1)
                            load_expert(sp, ei, lambda s: i * NSLOT + (NE - 1) * NSLOT + s + 1)
            for n in TILES:
                sp.wait_ge(s_acc, n + 1)
                sp.dma_start(y_out[n * P:(n + 1) * P, :], xt3[:, n, :]).then_inc(s_yout, 16)
            sp.wait_ge(s_yout, 16 * NT)

        @block.gpsimd
        def _(pool):
            order = Count(s_pool)

            def link(ins):
                pool.wait_ge(s_pool, order.inc(ins))

            pool.memset(mat("ones"), 1.0).then_inc(s_ones, 1)
            pool.memset(epst[:, 0:1], RMS_EPS).then_inc(s_eps, 1)
            pool.memset(epst[:, 1:2], LN_EPS).then_inc(s_eps, 1)
            pool.memset(epst[:, 2:3], L2_EPS).then_inc(s_eps, 1)
            pool.memset(ux3[:, :, 0:DW - 1], 0.0).then_inc(s_ext, 1)
            pool.memset(qx3[:, :, 0:QW - 1], 0.0).then_inc(s_ext, 1)
            pool.wait_ge(s_hist, 32)
            for c in range(CC):
                pool.tensor_copy(ux3[:, c, US:].rearrange("p (b e) -> p b e", b=NB)[:, :, 0:DW - 1],
                                 hu[:, c]).then_inc(s_ext, 1)
            for c in range(QC):
                pool.tensor_copy(qx3[:, c, QS:].rearrange("p (b e) -> p b e", b=NB)[:, :, 0:QW - 1],
                                 hq[:, c]).then_inc(s_ext, 1)
            pool.wait_ge(s_ext, 2 + CC + QC)
            for c in (2, 3):
                pool.wait_ge(s_evac, CC + c + 1)
                put_u(pool, c, s_up)
            for k in range(N_PROD):
                pool.wait_ge(s_prd, 2 * (k + 1))
                if k == 0:
                    pool.wait_ge(s_tap0, 4)
                if k >= 2:
                    pool.wait_ge(s_padd, k - 1)
                c = 2 + k % 2
                pool.tensor_tensor(cb3[:, c], cb3[:, c], prod[k % 3], ALU.add).then_inc(s_padd, 1)
            pool.wait_ge(s_tail, 4)
            for i in range(2):
                pool.wait_ge(s_padd, N_PROD - 1 + i)
                pool.tensor_tensor(cb3[:, 2 + i], cb3[:, 2 + i], tail[:, i], ALU.add).then_inc(s_padd, 1)
            ust4 = ust[:].rearrange("p (c b j) -> p c b j", c=CC, b=9)
            qst4 = qst[:].rearrange("p (c b j) -> p c b j", c=QC, b=9)
            pool.wait_ge(s_u, 4)
            pool.wait_ge(s_up, 4)
            for c in range(CC):
                pool.tensor_copy(ust4[:, c, 0, :], ux3[:, c, TP:US]).then_inc(s_st, 1)
                pool.tensor_copy(ust4[:, c, 1:9, :],
                                 ux3[:, c, US:].rearrange("p (b e) -> p b e", b=NB)[:, :, TS:]).then_inc(s_st, 1)
            for c in range(QC):
                pool.wait_ge(s_evac, 2 * CC + 2 * (c + 1))
                pool.tensor_copy(qst4[:, c, 0, :], qx3[:, c, TP:QS]).then_inc(s_st, 1)
                pool.tensor_copy(qst4[:, c, 1:9, :],
                                 qx3[:, c, QS:].rearrange("p (b e) -> p b e", b=NB)[:, :, TS:]).then_inc(s_st, 1)
            pool.wait_ge(s_st, 2 * (CC + QC))
            pool.dma_start(q_state_out, qst[:]).then_inc(s_stq, 16)
            pool.dma_start(u_state_out, ust[:]).then_inc(s_stq, 16)
            pool.wait_ge(s_cst, 32)
            for n in TILES:
                pool.wait_ge(s_a1d, n + 1)
                pool.tensor_tensor(tile4(at_, n), tile4(at_, n), mat4("incl_p" if n < 2 else "incl_s"), ALU.mult)\
                    .then_inc(s_causal, 1)
            for l, ns in levels():
                for n in ns:
                    pool.wait_ge(s_a1d, n + 1)
                    if l == 1:
                        pool.wait_ge(s_e1, n + 1)
                    else:
                        pool.wait_ge(s_x, LT_AT[l - 1, n])
                    pool.tensor_tensor(tile4(lt_, n), tile4(mt_, n), mat4(f"level{l}"), ALU.mult).then_inc(s_lt, 1)
            pool.wait_ge(s_bias, 96)
            pool.wait_ge(s_lt, N_STEPS)
            pool.wait_ge(s_e1, NT)
            pool.wait_ge(s_a1, NT)
            link(pool.tensor_copy(bparts[0:3 * NE], braw[0:3 * NE, :]))
            pool.tensor_tensor(braw[0:3 * NE, :], braw[0:3 * NE, :], bparts[0:3 * NE], ALU.subtract).then_inc(s_brest, 1)
            pool.wait_ge(s_brest, 1)
            pool.wait_ge(s_sd, 2)
            pool.dma_start(sp_out.rearrange("h k v -> k h v"), s_prm.rearrange("p (h v) -> p h v", h=H)).then_inc(s_sout, 16)
            pool.wait_ge(s_t1, 1)
            for b in range(NB):
                pool.tensor_tensor(smp4[:, b], smp4[:, b],
                                   tile4(eg_, 2)[:, :, TS * b + TS - 1:TS * b + TS].to_broadcast([P, H, P]),
                                   ALU.mult).then_inc(s_dec, 1)
            pool.wait_ge(s_v, NT)
            for b in range(NB):
                pool.tensor_scalar(k_only[b], flat(kd_, 2), cst[:, X_BLK + b:X_BLK + b + 1], None,
                                   ALU.mult).then_inc(s_km, 1)
            pool.wait_ge(s_dec, NB)
            for b in range(NB):
                pool.wait_ge(s_sev, b + 1)
                pool.tensor_tensor(smp4[:, b], smp4[:, b], added[b % 3].rearrange("p (h v) -> p h v", h=H),
                                   ALU.add).then_inc(s_smp_done, 1)
            pool.wait_ge(s_smp_done, NB)
            pool.dma_start(ss_out.rearrange("b h k v -> k (b h) v"),
                           s_smp.rearrange("p (b v) -> p b v", v=P)).then_inc(s_ssout, 16)
            pool.wait_ge(s_mix, 2 * NT)
            for x in range(2):
                for a in range(2):
                    pool.memset(gT[x][a], 0.0).then_inc(s_zero, 1)
            pool.wait_ge(s_zero, 4)
            pool.wait_ge(s_bpart, 2)
            pool.tensor_tensor(braw[2 * NE:3 * NE, :], braw[2 * NE:3 * NE, :], bparts[2 * NE:3 * NE], ALU.subtract)\
                .then_inc(s_brest, 1)

        @block.scalar
        def _(act):
            act.dma_start(par[:], params).then_inc(s_par, 16)
            act.dma_start(mats[:, P:len(MATS) * P], consts[:, P:len(MATS) * P]).then_inc(s_cst, 16)
            act.dma_start(cst[:], consts[:, len(MATS) * P:]).then_inc(s_cst, 16)
            act.dma_start(cb[:, 0:CC * NB * 30], hist_u).then_inc(s_hist, 16)
            act.dma_start(cb[:, CC * NB * 30:CC * NB * 30 + QC * NB * 3], hist_q).then_inc(s_hist, 16)
            act.dma_start(s_smp.rearrange("p (b v) -> p b v", v=P),
                          state_gdn.rearrange("b h k v -> k (b h) v")).then_inc(s_state, 16)
            for n in TILES:
                src = x_prompt[n * P:(n + 1) * P, :] if n < 2 else x_sample
                act.dma_start(xt3[:, n, :], src).then_inc(s_xt, 16)
            act.wait_ge(s_eps, 3)
            act.wait_ge(s_ssum, 1)
            act.activation(rB, bank[4][:, 0:T], ACT.Sqrt, bias=epst[:, 0:1], scale=1.0 / D).then_inc(s_rt, 1)
            act.wait_ge(s_par, 16)

            def evac(j):
                kind, c = JOBS[j]
                ps = bank[JOB_BANK[j]][:, 0:T]
                act.wait_ge(s_proj, j + 1)
                if kind == "ga":
                    act.activation(zs3[:, c], ps, ACT.Identity, bias=col("b_glu", c)).then_inc(s_evac, 1)
                elif kind == "gb":
                    act.activation(oT3[:, c], ps, ACT.Sigmoid, bias=col("b_glu", CC + c)).then_inc(s_evac, 1)
                elif kind == "qkv":
                    act.activation(qx3[:, c, QW - 1:QS], ps[:, 0:TP], ACT.Copy).then_inc(s_evac, 1)
                    act.activation(qx3[:, c, QS:].rearrange("p (b e) -> p b e", b=NB)[:, :, QW - 1:],
                                   ps[:, TP:T].rearrange("p (b t) -> p b t", b=NB), ACT.Copy).then_inc(s_evac, 1)
                else:
                    if c == 0:
                        act.wait_ge(s_u, 4)
                        act.wait_ge(s_up, 4)
                    act.activation(zs3[:, c], ps, ACT.Silu).then_inc(s_evac, 1)

            made = [0]

            def two_parts(k, c, j, out, **how):
                w = col("dw", j * CC + c)
                act.activation(out[:, 0:TP], ux3[:, c, j:j + TP], scale=w, **how).then_inc(k, 1)
                act.activation(out[:, TP:].rearrange("p (b t) -> p b t", b=NB),
                               ux3[:, c, US:].rearrange("p (b e) -> p b e", b=NB)[:, :, j:j + TS], scale=w, **how)\
                   .then_inc(k, 1)

            def products(count):
                for k in range(made[0], min(made[0] + count, N_PROD)):
                    if k >= 3:
                        act.wait_ge(s_padd, k - 2)
                    two_parts(s_prd, 2 + k % 2, 1 + k // 2, prod[k % 3], func=ACT.Copy)
                made[0] += count

            def silu(c):
                act.wait_ge(s_cv, 4 * (c // 2 + 1))
                act.activation(qkv3[:, c], qkv3[:, c], ACT.Silu).then_inc(s_silu, 1)
                if c < NN:
                    act.wait_ge(s_silu, c + 1)
                    act.activation(sq3[:, c], qkv3[:, c], ACT.Square).then_inc(s_qsq, 1)

            for j in range(JQ):
                evac(j)
            act.wait_ge(s_ext, 2 + CC + QC)
            act.wait_ge(s_up, 4)
            for c in (2, 3):
                two_parts(s_tap0, c, 0, cb3[:, c], func=ACT.Identity, bias=col("b_dw", c))
            products(3)
            for j in range(JQ, JQ + QC):
                evac(j)
                if j == JQ + 5:
                    act.wait_ge(s_bag, 3)
                    act.activation(e1_, ab_, ACT.Exp, scale=-1.0).then_inc(s_bae, 1)
                    act.activation(ea[:, 0:H], col("a_log", 0, H), ACT.Exp).then_inc(s_bae, 1)
                    act.wait_ge(s_bag, 4)
                    act.activation(l1_, e1_, ACT.Ln).then_inc(s_bae, 1)
                    act.activation(beta, bl_, ACT.Sigmoid).then_inc(s_bae, 1)
                c = 2 * (j - JQ - 6)
                if 0 <= c < NN:
                    silu(c)
                    silu(c + 1)
                products(5)
                if j == JZ - 2:
                    act.wait_ge(s_cn, 1)
                    act.activation(nrm24, bank[5][:, 96:96 + 2 * NT * H], ACT.Sqrt, bias=epst[:, 2:3]).then_inc(s_nroot, 1)
            assert made[0] >= N_PROD
            act.wait_ge(s_cs, 1)
            act.activation(ec, bank[5][:, 32:44], ACT.Exp).then_inc(s_cse, 1)
            act.activation(ed, bank[5][:, 64:76], ACT.Exp).then_inc(s_cse, 1)
            act.activation(gc, bank[5][:, 32:44], ACT.Copy).then_inc(s_cse, 1)
            for c in range(NN, QC):
                silu(c)
            evac(JZ)
            evac(JZ + 1)

            def copy_heads(dst, src, cols, n):
                for h in range(H):
                    act.activation(dst[:, h], src[:, h * P:(h + 1) * P], ACT.Copy, scale=cols[:, H * n + h:H * n + h + 1])\
                       .then_inc(s_vke, 1)

            for n in TILES:
                bk0 = 4 * (n % 2)
                act.wait_ge(s_a1, n + 1)
                act.activation(flat(eg_, n), bank[bk0], ACT.Exp).then_inc(s_gBc, 1)
                act.wait_ge(s_dif, H * (n + 1))
                act.activation(flat(x_, n), flat(x_, n), ACT.Exp).then_inc(s_dT, 1)
            evac(JZ + 2)
            evac(JZ + 3)
            for c in range(CC):
                act.wait_ge(s_xc, c + 1)
                act.activation(lsq3[:, c], cb3[:, c], ACT.Square).then_inc(s_lsq, 1)
            for n in TILES:
                act.wait_ge(s_tr, n + 1)
                act.activation(flat(d_, n), bank[2 * n], ACT.Copy).then_inc(s_d1, 1)
            for l, ns in levels():
                for n in ns:
                    act.wait_ge(s_x, LT_AT[l, n])
                    act.activation(flat(x_, n), bank[2 * n], ACT.Copy).then_inc(s_xs, 1)
                n = l - 1
                if n < NT:
                    act.wait_ge(s_vk, n + 1)
                    if n == 0:
                        act.wait_ge(s_edk, 1)
                        act.wait_ge(s_st, 2 * (CC + QC))
                    copy_heads(tile4(vb_, n), bank[6], beta, n)
                    copy_heads(tile4(kbe_, n), bank[7], bec, n)
                    copy_heads(tile4(kd_, n), bank[7], ed, n)
                elif l == NT + 1:
                    act.wait_ge(s_ln2, 1)
                    act.wait_ge(s_stq, 32)
                    act.activation(lroot, bank[6][:, 0:T], ACT.Sqrt, bias=epst[:, 1:2], scale=1.0 / (CC * P))\
                       .then_inc(s_lroot, 1)
            for c in range(CC):
                act.wait_ge(s_lnd, c + 1)
                act.activation(cb3[:, c], cb3[:, c], ACT.Silu, bias=col("ln_b", c), scale=col("ln_g", c))\
                   .then_inc(s_conf, 1)
            def v_new(n):
                act.wait_ge(s_v, n + 1)
                act.activation(flat(kbe_, n), bank[1], ACT.Copy).then_inc(s_ve, 1)

            def out_root(n):
                act.wait_ge(s_o, n + 1)
                for h in range(H):
                    act.activation(tile4(at_, n)[:, h], bank[2][:, h * P:(h + 1) * P], ACT.Square,
                                   scale=rq[:, H * n + h:H * n + h + 1], accum_out=ea[:, 4 + h:5 + h]).then_inc(s_osq, 1)
                act.wait_ge(s_osq, H * (n + 1))
                act.activation(y_[:, 0:H], ea[:, 4:8], ACT.Sqrt, bias=epst[:, 0:1], scale=1.0 / P).then_inc(s_ort, 1)

            def second_norm(n):
                act.wait_ge(s_x2, 2 * (n + 1))
                act.activation(h23[:, n], xt3[:, n], ACT.Square, accum_out=ssq[:, n:n + 1]).then_inc(s_x2q, 1)
                act.wait_ge(s_x2q, n + 1)
                act.activation(rr[:, n:n + 1], ssq[:, n:n + 1], ACT.Sqrt, bias=epst[:, 0:1], scale=1.0 / D).then_inc(s_x2r, 1)

            v_new(0)
            for n in (1, 2):
                act.wait_ge(s_wt, n)
                act.activation(flat(x_, n), bank[4 * (n - 1)], ACT.Copy, scale=-1.0).then_inc(s_wte, 1)
            out_root(0)
            act.wait_ge(s_t1, 1)
            for i in range(2):
                act.activation(lt_[:, 512 * i:512 * (i + 1)], bank[5 + i], ACT.Copy).then_inc(s_t1e, 1)
            v_new(1)
            out_root(1)
            second_norm(0)
            v_new(2)
            out_root(2)
            act.wait_ge(s_stq, 32)
            act.dma_start(wr, w_router.rearrange("(k p) e -> p k e", p=P)).then_inc(s_wr, 16)
            act.activation(ones_b, mat("ones"), ACT.Copy).then_inc(s_masks, 1)
            act.activation(strict_b, mat("strict"), ACT.Copy).then_inc(s_masks, 1)
            second_norm(1)

            def h_first(n):
                act.wait_ge(s_h2t, 2 * n + 1)
                act.activation(hT3[:, 0:4, n * P:(n + 1) * P], bank[2].rearrange("p (k t) -> p k t", k=4),
                               ACT.Copy).then_inc(s_h2te, 1)

            def gains(streams):
                for b in streams:
                    act.wait_ge(s_s, 3 + b)
                    if b >= 3:
                        act.wait_ge(s_smp_done, b - 2)
                    act.activation(added[b % 3], bank[STATE_BANK[b]], ACT.Copy).then_inc(s_sev, 1)
            gains(range(FIRST_STATES))
            act.wait_ge(s_brest, 1)
            for j in (1, 2):
                act.activation(bparts[NE * j:NE * (j + 1)], braw[NE * j:NE * (j + 1), :], ACT.Copy).then_inc(s_bpart, 1)
            h_first(0)
            second_norm(2)
            gains(range(FIRST_STATES, NB))
            h_first(1)
            h_first(2)
            act.wait_ge(s_brest, 2)
            act.activation(bparts[2 * NE:3 * NE], braw[2 * NE:3 * NE, :], ACT.Copy).then_inc(s_bsplit, 1)
            act.dma_start(gff[:, :], g_final.partition_broadcast(P)).then_inc(s_gfin, 16)
            act.wait_ge(s_gx, NT)
            for n in TILES:
                act.activation(gate[:, n], lg[:, n], ACT.Exp, bias=nv0[:, n:n + 1]).then_inc(s_ge, 1)

            def gates_t(item, x):
                act.wait_ge(s_gt, item + 1)
                for a in range(2):
                    act.activation(gT[x][a][a * BLK:(a + 1) * BLK], bank[6][a * BLK:(a + 1) * BLK, 0:T], ACT.Copy)\
                       .then_inc(s_gtc, 1)

            def rows_t(call):
                act.wait_ge(s_xgt, call + 1)
                act.activation(xTe[:, 4:8, :], bank[5].rearrange("p (k s) -> p k s", k=4), ACT.Copy).then_inc(s_xte, 1)

            def sigmoid(item):
                act.wait_ge(s_g, item + 1)
                act.activation(sg_b, g_s, ACT.Sigmoid, scale=ALPHA).then_inc(s_sig, 1)

            def rows_out(item):
                act.wait_ge(s_dn, item + 1)
                act.activation(y_s, bank[7], ACT.Copy).then_inc(s_yc, 1)

            def pair(p):
                for x in range(2):
                    gates_t(2 * p + x, x)
                    sigmoid(2 * p + x)
                    if x == 1:
                        rows_t(p + 1)
                    rows_out(2 * p + x)

            rows_t(0)
            act.wait_ge(s_zero, 4)
            with act.Fori(0, NPAIR) as p:
                pair(p)
            act.wait_ge(s_tabs, 1)
            n_extra = act.value_load(tab[0:1, NX:NX + 1], min_val=0, max_val=NX)
            with act.Fori(0, NX_OUTER) as g:
                with act.If(g * NX_INNER < n_extra):
                    with act.Fori(0, NX_INNER) as i0:
                        i = g * NX_INNER + i0
                        with act.If(i < n_extra):
                            sigmoid(i + NE)
                            rows_out(i + NE)
                            gates_t(i + NE, 1)
                            with act.If(i + 1 < n_extra):
                                rows_t(i + (NPAIR + 1))
            for n in TILES:
                act.wait_ge(s_add, n_extra * 6 + (6 * NE - 4 + 2 * n))
                act.activation(h23[:, n], xt3[:, n], ACT.Square, accum_out=ssq[:, n:n + 1]).then_inc(s_fin, 1)
                act.wait_ge(s_fin, n + 1)
                act.activation(rr[:, n:n + 1], ssq[:, n:n + 1], ACT.Sqrt, bias=epst[:, 0:1], scale=1.0 / D).then_inc(s_frt, 1)

        @block.vector
        def _(dve):
            order = Count(s_dve)

            def link(ins):
                dve.wait_ge(s_dve, order.inc(ins))

            dve.wait_ge(s_xT, 16)
            for k in range(KD):
                dve.tensor_tensor(sq3[:, k], hT3[:, k], hT3[:, k], ALU.mult).then_inc(s_sq, 1)
            dve.wait_ge(s_rt, 1)
            link(dve.reciprocal(rB, rB))
            dve.wait_ge(s_par, 16)
            for k in range(KD):
                dve.scalar_tensor_tensor(hT3[:, k], hT3[:, k], col("g_mix", k), rB, ALU.mult, ALU.mult).then_inc(s_h, 1)
            def conv(src, wide, dst, tiles, taps, w, bias, last, first=0, shift=0):
                start = wide - TP
                chains = []
                for c in tiles:
                    to = dst[:, c - shift]
                    chains.append((c, lambda j, c=c: src[:, c, j:j + TP], to[:, 0:TP]))
                    chains.append((c, lambda j, c=c: src[:, c, start + TP:].rearrange("p (b e) -> p b e", b=NB)[:, :, j:j + TS],
                                   to[:, TP:].rearrange("p (b t) -> p b t", b=NB)))
                done = [0] * len(chains)
                for j in range(first, taps):
                    for i, (c, at_tap, out) in enumerate(chains):
                        if j == first:
                            ins = dve.tensor_scalar(out, at_tap(j), w(j, c), bias(c) if bias else None, ALU.mult,
                                                    ALU.add if bias else ALU.bypass)
                        else:
                            dve.wait_ge(s_dve, done[i])
                            ins = dve.scalar_tensor_tensor(out, at_tap(j), w(j, c), out, ALU.mult, ALU.add)
                        if j == taps - 1:
                            ins.then_inc(last, 1)
                        else:
                            done[i] = order.inc(ins)

            for c in (0, 1):
                dve.wait_ge(s_evac, 3 + c)
                put_u(dve, c, s_u)
            dve.wait_ge(s_ext, 2 + CC + QC)
            dve.wait_ge(s_u, 4)
            conv(ux3, US, cb3, (0, 1), DW, lambda j, c: col("dw", j * CC + c), lambda c: col("b_dw", c), s_dwc)
            ba = bank[5][:, 0:NT * 8].rearrange("p (n c) -> p n c", n=NT)

            def by_tile(x):
                return x.rearrange("p (n h) -> p n h", n=NT)

            dve.wait_ge(s_ba, 1)
            dve.tensor_tensor(by_tile(y_), ba[:, :, H:2 * H], col("dt", 0, H).unsqueeze(1).to_broadcast([P, NT, H]),
                              ALU.add).then_inc(s_bag, 1)
            dve.tensor_copy(by_tile(bl_), ba[:, :, 0:H]).then_inc(s_bag, 1)
            dve.wait_ge(s_bag, 2)
            dve.scalar_tensor_tensor(ab_, y_, -1.0, y_, ALU.mult, ALU.max).then_inc(s_bag, 1)
            dve.wait_ge(s_up, 4)
            conv(ux3, US, tail, (2, 3), DW, lambda j, c: col("dw", j * CC + c), None, s_tail, DW - DVE_TAPS, 2)
            def conv_qkv(c):
                dve.wait_ge(s_evac, JQ + 2 * (c + 2))
                conv(qx3, QS, qkv3, (c, c + 1), QW, lambda j, c: col("conv", j * QC + c), None, s_cv)

            conv_qkv(0)
            dve.wait_ge(s_bae, 2)
            dve.tensor_scalar(e1_, e1_, 1.0, None, ALU.add).then_inc(s_bag, 1)
            dve.wait_ge(s_bae, 4)
            link(dve.scalar_tensor_tensor(g_, y_, 0.0, l1_, ALU.max, ALU.add))
            dve.scalar_tensor_tensor(by_tile(g_), by_tile(g_), -1.0, ea[:, 0:H].unsqueeze(1).to_broadcast([P, NT, H]),
                                     ALU.mult, ALU.mult).then_inc(s_gates, 1)

            for c in range(2, NN + 2, 2):
                conv_qkv(c)
            nrm = nrm24.rearrange("p (q n h) -> p q n h", q=2, n=NT)
            dve.wait_ge(s_nroot, 1)
            link(dve.reciprocal(nrm24, nrm24))
            link(dve.tensor_scalar(by_tile(rq), nrm[:, 0], float(P) ** -0.5, None, ALU.mult))
            link(dve.tensor_copy(by_tile(rk), nrm[:, 1]))
            dve.tensor_tensor(bk, beta, rk, ALU.mult).then_inc(s_nrm, 1)
            conv_qkv(NN + 2)
            dve.wait_ge(s_cse, 3)
            link(dve.tensor_tensor(bec, beta, ec, ALU.mult))
            link(dve.tensor_tensor(bec, bec, rk, ALU.mult))
            dve.tensor_tensor(ed, ed, rk, ALU.mult).then_inc(s_edk, 1)
            dve.wait_ge(s_padd, N_PROD + 2)
            dve.wait_ge(s_cst, 32)
            dve.wait_ge(s_st, 2 * (CC + QC))
            for n in TILES:
                b0 = 4 * (n % 2)
                dve.wait_ge(s_gBc, n + 1)
                for h in range(H):
                    dve.tensor_scalar(tile4(x_, n)[:, h], bank[b0][:, h * P:(h + 1) * P], gc[:, H * n + h:H * n + h + 1],
                                      0.0, ALU.subtract, ALU.min).then_inc(s_dif, 1)
                dve.wait_ge(s_dT, n + 1)
                for dst, b in ((mt_, b0 + 2), (at_, b0 + 3)):
                    for h in range(H):
                        order.inc(dve.scalar_tensor_tensor(tile4(dst, n)[:, h], bank[b][:, h * P:(h + 1) * P],
                                                           rk[:, H * n + h:H * n + h + 1], tile4(x_, n)[:, h],
                                                           ALU.mult, ALU.mult))
                dve.wait_ge(s_dve, order.n)
                dve.tensor_tensor(flat(mt_, n), flat(mt_, n), bank[b0 + 1], ALU.mult).then_inc(s_a1d, 1)
                dve.wait_ge(s_a1d, n + 1)
                link(dve.tensor_tensor(tile4(e_, n), tile4(mt_, n), mat4("level0"), ALU.mult))
                dve.tensor_tensor(tile4(e_, n), mat4("ident"), tile4(e_, n), ALU.subtract).then_inc(s_e1, 1)
            dve.wait_ge(s_ln, 1)
            for c in range(CC):
                dve.scalar_tensor_tensor(cb3[:, c], bank[6][:, 0:T], -1.0 / (CC * P), cb3[:, c], ALU.mult, ALU.add)\
                   .then_inc(s_xc, 1)
            for l, ns in levels():
                for n in ns:
                    dve.wait_ge(s_pq, LT_AT[l, n])
                    if l < LEVELS - 1:
                        dve.tensor_tensor(halves(flat(d_, n), l, 0), halves(flat(d_, n), l, 0), halves(bank[2 * n], l, 0),
                                          ALU.subtract).then_inc(s_de, 1)
                    else:
                        dve.nop().then_inc(s_de, 1)
                    dve.tensor_tensor(halves(flat(e_, n), l, 1), halves(flat(e_, n), l, 1), halves(bank[2 * n + 1], l, 1),
                                      ALU.subtract).then_inc(s_de, 1)
                if l == NT + 1:
                    dve.wait_ge(s_lroot, 1)
                    dve.wait_ge(s_lsq, CC)
                    link(dve.reciprocal(lroot, lroot))
                    for c in range(CC):
                        dve.tensor_tensor(cb3[:, c], cb3[:, c], lroot, ALU.mult).then_inc(s_lnd, 1)
            for n in (1, 2):
                dve.wait_ge(s_de, 2 * N_STEPS)
                dve.tensor_tensor(tile4(d_, n), qkv3[:, 0:H, n * P:(n + 1) * P], tile4(eg_, n), ALU.mult).then_inc(s_qg, 1)


            def normed(n):
                dve.wait_ge(s_ort, n + 1)
                link(dve.reciprocal(y_[:, 4:8], y_[:, 0:4]))
                link(dve.tensor_tensor(y_[:, 4:8], y_[:, 4:8], rq[:, H * n:H * (n + 1)], ALU.mult))
                for h in range(H):
                    dve.tensor_scalar(tile4(at_, n)[:, h], bank[2][:, h * P:(h + 1) * P], y_[:, 4 + h:5 + h],
                                      None, ALU.mult).then_inc(s_on, 1)

            def gated(n):
                dve.wait_ge(s_ot, n + 1)
                dve.scalar_tensor_tensor(oT3[:, :, n * P:(n + 1) * P], bank[7].rearrange("p (h t) -> p h t", h=H),
                                         col("onorm"), zs3[:, :, n * P:(n + 1) * P], ALU.mult, ALU.mult).then_inc(s_oTd, 1)

            def residual(n):
                for a in range(2):
                    dve.wait_ge(s_mix, 2 * n + a + 1)
                    dve.tensor_tensor(xt3[:, n, a * 512:(a + 1) * 512], xt3[:, n, a * 512:(a + 1) * 512],
                                      bank[OUT_BANK[n][a]], ALU.add).then_inc(s_x2, 1)

            def h_rows(n):
                dve.wait_ge(s_x2r, n + 1)
                link(dve.reciprocal(rr[:, n:n + 1], rr[:, n:n + 1]))
                dve.scalar_tensor_tensor(h23[:, n], xt3[:, n], rr[:, n:n + 1], gff[:, :], ALU.mult, ALU.mult)\
                   .then_inc(s_h2, 1)

            def h_turned(n):
                dve.wait_ge(s_h2t, 2 * n + 2)
                dve.tensor_copy(hT3[:, 4:8, n * P:(n + 1) * P], bank[7].rearrange("p (k t) -> p k t", k=4))\
                   .then_inc(s_h2te, 1)

            dve.wait_ge(s_s, 1)
            dve.tensor_copy(s_prm, bank[3]).then_inc(s_sd, 1)
            normed(0)
            gated(0)
            dve.wait_ge(s_s, 2)
            for h in range(H):
                last = dve.scalar_tensor_tensor(s_prm[:, h * P:(h + 1) * P], s_prm[:, h * P:(h + 1) * P],
                                                tile4(eg_, 1)[:, h, P - 1:P], bank[3][:, h * P:(h + 1) * P],
                                                ALU.mult, ALU.add)
                if h < H - 1:
                    order.inc(last)
            last.then_inc(s_sd, 1)
            normed(1)
            dve.wait_ge(s_xt, 16 * NT)
            residual(0)
            gated(1)
            dve.wait_ge(s_gff, 16)
            h_rows(0)
            normed(2)
            gated(2)
            residual(1)
            h_turned(0)
            h_rows(1)

            iota = cst[:, X_IOTA:X_IOTA + BLK]

            def choose(n):
                dve.wait_ge(s_lg, n + 1)
                link(dve.tensor_tensor(lg[:, n], bank[LOGIT_BANK[n]][:, 0:NE], col("b_router", 0, NE), ALU.add))
                link(dve.max(v8[:, n], lg[:, n]))
                dve.tensor_scalar(nv0[:, n:n + 1], v8[:, n, 0:1], -1.0, None, ALU.mult).then_inc(s_gx, 1)
                link(dve.max_index(i8[:, n].bitcast(U32), v8[:, n], lg[:, n]))
                link(dve.tensor_copy(if8[:, n], i8[:, n].bitcast(U32)))
                link(dve.tensor_scalar(mall[:, n], iota[:, 0:NE], if8[:, n, 0:1], None, ALU.is_equal))
                for j in range(1, TOPK):
                    ins = dve.scalar_tensor_tensor(mall[:, n], iota[:, 0:NE], if8[:, n, j:j + 1], mall[:, n],
                                                   ALU.is_equal, ALU.add)
                    if j < TOPK - 1:
                        link(ins)
                    else:
                        ins.then_inc(s_m, 1)

            residual(2)
            h_turned(1)
            h_rows(2)
            choose(0)
            h_turned(2)
            choose(1)
            choose(2)
            dve.wait_ge(s_pp, 1)
            places = bank[6][:, 0:NT * NE].rearrange("p (n e) -> p n e", n=NT)
            pos_n = pos.rearrange("p e n -> p n e")
            link(dve.scalar_tensor_tensor(pos_n, places, 1.0, mall, ALU.add, ALU.mult))
            link(dve.tensor_scalar(pos_n, pos_n, -1.0, None, ALU.add))

            def row_hits(p):
                dve.tensor_tensor(hp.rearrange("p n (x s) -> p n x s", x=2),
                                  pos_n[:, :, bass.ds(2 * p, 2)].unsqueeze(3).to_broadcast([P, NT, 2, BLK]),
                                  iota.unsqueeze(1).unsqueeze(1).to_broadcast([P, NT, 2, BLK]), ALU.is_equal).then_inc(s_hp, 1)

            iota2 = iota.unsqueeze(1).to_broadcast([P, 2, BLK])

            def gate_hits(place, e):
                for n in TILES:
                    dve.tensor_scalar(hg[:, n].rearrange("p (a s) -> p a s", a=2), iota2, place(n),
                                      gate[:, n, bass.ds(e, 1)], ALU.is_equal, ALU.mult).then_inc(s_hg, 1)

            def place_of(e):
                return lambda n: pos[:, bass.ds(e, 1), n]

            row_hits(0)
            link(dve.tensor_copy(cntB, bank[6][:, NT * NE:(NT + 1) * NE]))
            dve.wait_ge(s_ge, NT)
            link(dve.tensor_tensor(gate, gate, mall, ALU.mult))
            link(dve.tensor_reduce(gsum, gate, AX_X, ALU.add))
            link(dve.reciprocal(gsum, gsum))
            link(dve.tensor_tensor(gate, gate, gsum.unsqueeze(2).to_broadcast([P, NT, NE]), ALU.mult))
            gate_hits(place_of(0), 0)

            def tables():
                link(dve.memset(off64x, 0.0))
                link(dve.memset(tabf, 0.0))
                link(dve.tensor_scalar(nxb, cntB, float(BLK), None, ALU.is_gt))
                for b in range(2, T // BLK):
                    link(dve.scalar_tensor_tensor(nxb, cntB, float(BLK * b), nxb, ALU.is_gt, ALU.add))
                link(dve.tensor_copy(cumA, nxb))
                a, b, s = cumA, cumB, 1
                while s < NE:
                    link(dve.tensor_copy(b[:, 0:s], a[:, 0:s]))
                    link(dve.tensor_tensor(b[:, s:], a[:, s:], a[:, 0:NE - s], ALU.add))
                    a, b, s = b, a, 2 * s
                link(dve.tensor_tensor(cmpx, a.unsqueeze(1).to_broadcast([P, NX, NE]),
                                       iota[:, 0:NX].unsqueeze(2).to_broadcast([P, NX, NE]), ALU.is_le))
                link(dve.tensor_reduce(ex, cmpx, AX_X, ALU.add))
                link(dve.tensor_scalar(ex, ex, float(NE - 1), None, ALU.min))
                link(dve.tensor_tensor(cmpx, cmpx, nxb.unsqueeze(1).to_broadcast([P, NX, NE]), ALU.mult))
                link(dve.tensor_reduce(stx, cmpx, AX_X, ALU.add))
                link(dve.tensor_tensor(off64, iota[:, 0:NX], stx, ALU.subtract))
                link(dve.tensor_scalar(off64, off64, 1.0, float(BLK), ALU.add, ALU.mult))
                link(dve.tensor_copy(tab[:, 0:NX], ex))
                dve.tensor_copy(tab[:, NX:NX + 1], a[:, NE - 1:NE]).then_inc(s_tabs, 1)

            def rows_t(call):
                dve.wait_ge(s_xgt, call + 1)
                dve.tensor_copy(xTe[:, 0:4, :], bank[4].rearrange("p (k s) -> p k s", k=4)).then_inc(s_xte, 1)

            def select(x, e):
                dve.tensor_scalar(sel_sb[0:3 * NE, x], mat("ones")[0:3 * NE, 0:BLK],
                                  cst[0:3 * NE, bass.ds(e + X_SEL, 1)], None, ALU.mult).then_inc(s_sel, 1)

            def add(m, o):
                n, a = divmod(o, 2)
                dve.wait_ge(s_cmb, m * 6 + (o + 1))
                dve.tensor_tensor(xt3[:, n, a * 512:(a + 1) * 512], xt3[:, n, a * 512:(a + 1) * 512], bank[2 + o % 2],
                                  ALU.add).then_inc(s_add, 1)

            def clamp(item):
                dve.wait_ge(s_gu, item + 1)
                dve.tensor_scalar(g_s, bank[0], LIMIT, None, ALU.min).then_inc(s_g, 1)
                dve.tensor_scalar(l_s, bank[1], -LIMIT, LIMIT, ALU.max, ALU.min).then_inc(s_lin, 1)

            def swiglu(item):
                dve.wait_ge(s_sig, item + 1)
                dve.wait_ge(s_g, item + 1)
                dve.tensor_tensor(t_s, g_s, sg_b, ALU.mult).then_inc(s_lin, 1)
                dve.wait_ge(s_lin, item * 2 + 2)
                dve.scalar_tensor_tensor(a_s, l_s, 1.0, t_s, ALU.add, ALU.mult).then_inc(s_act, 1)

            def turned(item):
                dve.wait_ge(s_att, item + 1)
                dve.tensor_copy(actT, bank[6]).then_inc(s_atr, 1)

            def extra_hits(i):
                e = dve.value_load(tab[0:1, bass.ds(i, 1)], min_val=0, max_val=NE - 1)
                dve.tensor_scalar(pcur, pos[:, bass.ds(e, 1), :].rearrange("p a n -> p (a n)"),
                                  off64x[:, bass.ds(i, 1)], None, ALU.subtract).then_inc(s_pc, 1)
                dve.wait_ge(s_pc, i + 1)
                dve.wait_ge(s_gt, i + NE)
                gate_hits(lambda n: pcur[:, n:n + 1], e)
                dve.wait_ge(s_xgt, i + NPAIR)
                dve.tensor_tensor(hp[:, :, 0:BLK], pcur.unsqueeze(2).to_broadcast([P, NT, BLK]),
                                  iota.unsqueeze(1).to_broadcast([P, NT, BLK]), ALU.is_equal).then_inc(s_hp, 1)

            def pair(p, first, last, between=None):
                for x in range(2):
                    item = 2 * p + x
                    alone = first and x == 0
                    if not (last and x == 1):
                        if not alone:
                            dve.wait_ge(s_dn, item)
                        select(1 - x, item + 1)
                        dve.wait_ge(s_gt, item + 1)
                        gate_hits(place_of(item + 1), item + 1)
                    else:
                        extra_hits(0)
                    if x == 0 and not last:
                        dve.wait_ge(s_xgt, p + 1)
                        row_hits(p + 1)
                    clamp(item)
                    if not alone:
                        add(item - 1, 0)
                    swiglu(item)
                    if not alone:
                        add(item - 1, 1)
                    if x == 1:
                        rows_t(p + 1)
                    turned(item)
                    if not alone:
                        for o in range(2, 6):
                            add(item - 1, o)
                    if x == 0 and between:
                        between()

            rows_t(0)
            select(0, 0)
            pair(0, True, False, tables)
            with dve.Fori(1, NPAIR - 1) as p:
                pair(p, False, False)
            pair(NPAIR - 1, False, True)
            n_extra = dve.value_load(tab[0:1, NX:NX + 1], min_val=0, max_val=NX)
            with dve.Fori(0, NX_OUTER) as g:
                with dve.If(g * NX_INNER < n_extra):
                    with dve.Fori(0, NX_INNER) as i0:
                        i = g * NX_INNER + i0
                        with dve.If(i < n_extra):
                            e = dve.value_load(tab[0:1, bass.ds(i, 1)], min_val=0, max_val=NE - 1)
                            dve.wait_ge(s_dn, i + NE)
                            select(0, e)
                            clamp(i + NE)
                            add(i + (NE - 1), 0)
                            swiglu(i + NE)
                            add(i + (NE - 1), 1)
                            turned(i + NE)
                            for o in range(2, 6):
                                add(i + (NE - 1), o)
                            with dve.If(i + 1 < n_extra):
                                extra_hits(i + 1)
                                rows_t(i + (NPAIR + 1))
            for o in range(6):
                add(n_extra + (NE - 1), o)
            dve.wait_ge(s_gfin, 16)
            for n in TILES:
                dve.wait_ge(s_frt, n + 1)
                link(dve.reciprocal(rr[:, n:n + 1], rr[:, n:n + 1]))
                dve.scalar_tensor_tensor(xt3[:, n], xt3[:, n], rr[:, n:n + 1], gff[:, :], ALU.mult, ALU.mult)\
                   .then_inc(s_acc, 1)

        @block.tensor
        def _(pe):
            pe.wait_ge(s_ones, 1)
            for k in range(KD):
                pe.wait_ge(s_sq, k + 1)
                mm = pe.matmul(bank[4][:, 0:T], mat("ones"), sq3[:, k], start=(k == 0), stop=(k == KD - 1))
            mm.then_inc(s_ssum, 1)

            def taken(j):
                return j + 1 if j < 2 * CC else (2 * CC + 2 * (j + 1 - 2 * CC) if j < 2 * CC + QC
                                                 else 2 * CC + 2 * QC + (j + 1 - 2 * CC - QC))

            def project_in(j):
                pe.wait_ge(s_win[j // 4 % 2], 16 * (j // 8 + 2))
                if 4 <= j < NJ - 2:
                    pe.wait_ge(s_evac, taken(j - 4))
                for k in range(KD):
                    if j == 0:
                        pe.wait_ge(s_h, k + 1)
                    mm = pe.matmul(bank[JOB_BANK[j]][:, 0:T], win4[:, j // 4 % 2, k, (j % 4) * P:(j % 4 + 1) * P], hT3[:, k],
                                   start=(k == 0), stop=(k == KD - 1))
                mm.then_inc(s_proj, 1)

            for j in range(JZ + 2):
                project_in(j)
                if j == JQ - 1:
                    pe.wait_ge(s_ba_in, 16)
                    for n in TILES:
                        for k in range(KD):
                            mm = pe.matmul(bank[5][:, 8 * n:8 * n + 8], hT3[:, k, n * P:(n + 1) * P],
                                           gff[:, 8 * k:8 * k + 8], start=(k == 0), stop=(k == KD - 1))
                    mm.then_inc(s_ba, 1)
                if j == JZ - 3:
                    for c in range(NN):
                        pe.wait_ge(s_qsq, c + 1)
                        for n in TILES:
                            at_col = 96 + (c // H) * NT * H + H * n + c % H
                            mm = pe.matmul(bank[5][:, at_col:at_col + 1], sq3[:, c, n * P:(n + 1) * P], mat("ones")[:, 0:1],
                                           start=True, stop=True)
                    mm.then_inc(s_cn, 1)
                if j == JZ - 1:
                    pe.wait_ge(s_nroot, 1)
                    pe.wait_ge(s_gates, 1)
                    pe.wait_ge(s_cst, 32)
                    for n in TILES:
                        pe.matmul(bank[5][:, 32 + H * n:32 + H * (n + 1)], mat("incl_p" if n < 2 else "incl_s"),
                                  g_[:, H * n:H * (n + 1)], start=True, stop=True)
                        mm = pe.matmul(bank[5][:, 64 + H * n:64 + H * (n + 1)], mat("later_p" if n < 2 else "later_s"),
                                       g_[:, H * n:H * (n + 1)], start=True, stop=True)
                    mm.then_inc(s_cs, 1)

            def turn_vk(n):
                tk = slice(n * P, (n + 1) * P)
                if n:
                    pe.wait_ge(s_vke, 3 * H * n)
                for h in range(H):
                    hs = slice(h * P, (h + 1) * P)
                    pe.transpose(bank[6][:, hs], qkv3[:, 2 * H + h, tk], mat("ident"))
                    mm = pe.transpose(bank[7][:, hs], qkv3[:, H + h, tk], mat("ident"))
                mm.then_inc(s_vk, 1)

            pe.wait_ge(s_nrm, 1)
            pe.wait_ge(s_cse, 3)
            pe.wait_ge(s_evac, taken(JZ + 1))
            for n in TILES:
                b0 = 4 * (n % 2)
                if n == 2:
                    pe.wait_ge(s_a1d, 1)
                tk = slice(n * P, (n + 1) * P)
                incl = mat("incl_p" if n < 2 else "incl_s")
                for h in range(H):
                    pe.matmul(bank[b0][:, h * P:(h + 1) * P], g_[:, H * n + h:H * n + h + 1].to_broadcast([P, P]), incl,
                              start=True, stop=True)
                mm = None
                for h in range(H):
                    hs = slice(h * P, (h + 1) * P)
                    one = slice(H * n + h, H * n + h + 1)
                    pe.matmul(bank[b0 + 2][:, hs], qkv3[:, H + h, tk], qkv3[:, H + h, tk], start=True, stop=True)
                    pe.matmul(bank[b0 + 3][:, hs], qkv3[:, H + h, tk], qkv3[:, h, tk], start=True, stop=True)
                    mm = pe.matmul(bank[b0 + 1][:, hs], bk[:, one].to_broadcast([P, P]), mat("ident"), start=True, stop=True)
                mm.then_inc(s_a1, 1)
            pe.wait_ge(s_a1d, 2)
            project_in(JZ + 2)
            pe.wait_ge(s_dwc, 4)
            pe.wait_ge(s_padd, N_PROD + 2)
            for c in range(CC):
                mm = pe.matmul(bank[6][:, 0:T], mat("ones"), cb3[:, c], start=(c == 0), stop=(c == CC - 1))
            mm.then_inc(s_ln, 1)
            project_in(JZ + 3)
            for n in TILES:
                pe.wait_ge(s_e1, n + 1 if n else NT)
                for h in range(H):
                    mm = pe.transpose(bank[2 * n][:, h * P:(h + 1) * P], tile4(e_, n)[:, h], mat("ident"))
                mm.then_inc(s_tr, 1)
            for l, ns in levels():
                for n in ns:
                    if l == 1:
                        pe.wait_ge(s_d1, n + 1)
                    else:
                        pe.wait_ge(s_de, 2 * LT_AT[l - 1, n])
                    pe.wait_ge(s_lt, LT_AT[l, n])
                    for h in range(H):
                        mm = pe.matmul(bank[2 * n][:, h * P:(h + 1) * P], tile4(lt_, n)[:, h], tile4(d_, n)[:, h],
                                       start=True, stop=True)
                    mm.then_inc(s_x, 1)
                if l <= NT:
                    if l == 1:
                        pe.wait_ge(s_silu, QC)
                        pe.wait_ge(s_xc, CC)
                        pe.wait_ge(s_evac, taken(NJ - 1))
                    turn_vk(l - 1)
                elif l == NT + 1:
                    pe.wait_ge(s_vke, 3 * H * NT)
                    for c in range(CC):
                        mm = pe.matmul(bank[6][:, 0:T], mat("ones"), lsq3[:, c], start=(c == 0), stop=(c == CC - 1))
                    mm.then_inc(s_ln2, 1)
                for n in ns:
                    pe.wait_ge(s_xs, LT_AT[l, n])
                    for h in range(H):
                        hs = slice(h * P, (h + 1) * P)
                        if l < LEVELS - 1:
                            pe.matmul(halves(bank[2 * n][:, hs], l, 0), tile4(e_, n)[:, h], halves(tile4(x_, n)[:, h], l, 0),
                                      start=True, stop=True)
                        mm = pe.matmul(halves(bank[2 * n + 1][:, hs], l, 1), tile4(x_, n)[:, h],
                                       halves(tile4(e_, n)[:, h], l, 1), start=True, stop=True)
                    mm.then_inc(s_pq, 1)
            pe.wait_ge(s_de, 2 * N_STEPS)
            pe.wait_ge(s_vke, 3 * H * NT)
            pe.wait_ge(s_state, 16)

            def w_rows(n):
                for h in range(H):
                    mm = pe.matmul(bank[4 * (n - 1)][:, h * P:(h + 1) * P], tile4(kbe_, n)[:, h], tile4(e_, n)[:, h],
                                   start=True, stop=True)
                mm.then_inc(s_wt, 1)

            def own_states():
                pe.wait_ge(s_wte, 2)
                pe.wait_ge(s_qg, 2)
                for h in range(H):
                    out = bank[5 + h // 2].rearrange("p (h g t) -> p h g t", h=2, g=2)[:, h % 2]
                    for b in range(NB):
                        mm = pe.matmul(out[:, :, TS * b:TS * (b + 1)], smp4[:, b, h], qw5[:, :, 2, h, TS * b:TS * (b + 1)],
                                       start=True, stop=True)
                mm.then_inc(s_t1, 1)

            def term(h, g):
                c = (h // 2) * 512 + (h % 2) * 256 + g * P
                return lt_[:, c:c + P]

            def v_new(n):
                if n == 1:
                    pe.wait_ge(s_sd, 1)
                    pe.wait_ge(s_wte, 1)
                if n == 2:
                    pe.wait_ge(s_t1e, 2)
                if n:
                    pe.wait_ge(s_ve, n)
                for h in range(H):
                    hs = slice(h * P, (h + 1) * P)
                    mm = pe.matmul(bank[1][:, hs], tile4(e_, n)[:, h], tile4(vb_, n)[:, h], start=True, stop=(n == 0))
                    if n == 1:
                        mm = pe.matmul(bank[1][:, hs], tile4(x_, n)[:, h], s_prm[:, hs], start=False, stop=True)
                    if n == 2:
                        mm = pe.matmul(bank[1][:, hs], term(h, 1), mat("ident"), start=False, stop=True)
                mm.then_inc(s_v, 1)

            def outputs(n):
                pe.wait_ge(s_causal, n + 1)
                pe.wait_ge(s_ve, n + 1)
                if n == 1:
                    pe.wait_ge(s_qg, 1)
                if n:
                    pe.wait_ge(s_on, H * n)
                for h in range(H):
                    hs = slice(h * P, (h + 1) * P)
                    if n == 1:
                        pe.matmul(bank[2][:, hs], tile4(d_, n)[:, h], s_prm[:, hs], start=True, stop=False)
                    if n == 2:
                        pe.matmul(bank[2][:, hs], term(h, 0), mat("ident"), start=True, stop=False)
                    mm = pe.matmul(bank[2][:, hs], tile4(at_, n)[:, h], tile4(kbe_, n)[:, h], start=(n == 0), stop=True)
                mm.then_inc(s_o, 1)

            def state(n):
                if n:
                    pe.wait_ge(s_sd, n)
                for h in range(H):
                    mm = pe.matmul(bank[3][:, h * P:(h + 1) * P], tile4(kd_, n)[:, h], tile4(kbe_, n)[:, h],
                                   start=True, stop=True)
                mm.then_inc(s_s, 1)

            def turn_o(n):
                pe.wait_ge(s_on, H * (n + 1))
                if n:
                    pe.wait_ge(s_oTd, n)
                for h in range(H):
                    mm = pe.transpose(bank[7][:, h * P:(h + 1) * P], tile4(at_, n)[:, h], mat("ident"))
                mm.then_inc(s_ot, 1)

            def state_of(b):
                pe.wait_ge(s_km, b + 1)
                if STATE_BANK[b] in STATE_BANK[:b]:
                    pe.wait_ge(s_sev, b - STATE_BANK[:b][::-1].index(STATE_BANK[b]))
                for h in range(H):
                    hs = slice(h * P, (h + 1) * P)
                    mm = pe.matmul(bank[STATE_BANK[b]][:, hs], k_only[b][:, hs], flat(kbe_, 2)[:, hs],
                                   start=True, stop=True)
                mm.then_inc(s_s, 1)

            def project(n, a):
                if n == 2:
                    pe.wait_ge(s_x2, 2)
                for i, k in enumerate([4, 5, 6, 7, 0, 1, 2, 3]):
                    if k == 0:
                        pe.wait_ge(s_oTd, n + 1)
                    cat = cb3[:, k - 4] if k >= 4 else oT3[:, k]
                    mm = pe.matmul(bank[OUT_BANK[n][a]], cat[:, n * P:(n + 1) * P], win4[:, a, k, :],
                                   start=(i == 0), stop=(i == KD - 1))
                mm.then_inc(s_mix, 1)

            def turn_h(n):
                pe.wait_ge(s_h2, n + 1)
                if n:
                    pe.wait_ge(s_h2te, 2 * n)
                for a in range(2):
                    for k in range(4):
                        mm = pe.transpose(bank[(2, 7)[a]][:, k * P:(k + 1) * P],
                                          h23[:, n, (4 * a + k) * P:(4 * a + k + 1) * P], mat("ident"))
                    mm.then_inc(s_h2t, 1)

            def logits(n):
                pe.wait_ge(s_h2te, 2 * n + 2)
                for k in range(KD):
                    mm = pe.matmul(bank[LOGIT_BANK[n]][:, 0:NE], hT3[:, k, n * P:(n + 1) * P], wr[:, k, :],
                                   start=(k == 0), stop=(k == KD - 1))
                mm.then_inc(s_lg, 1)

            v_new(0)
            w_rows(1)
            w_rows(2)
            outputs(0)
            state(0)
            own_states()
            turn_o(0)
            v_new(1)
            outputs(1)
            state(1)
            pe.wait_ge(s_conf, CC)
            for i in range(2):
                pe.wait_ge(s_win[i], 80)
            project(0, 0)
            project(0, 1)
            v_new(2)
            turn_o(1)
            outputs(2)
            project(1, 0)
            project(1, 1)
            turn_o(2)
            pe.wait_ge(s_ve, NT)
            pe.wait_ge(s_sd, 2)
            pe.wait_ge(s_x2, 2)
            for b in range(FIRST_STATES):
                state_of(b)
            project(2, 0)
            turn_h(0)
            pe.wait_ge(s_sev, FIRST_STATES)
            project(2, 1)
            pe.wait_ge(s_x2, 4)
            for b in range(FIRST_STATES, NB):
                state_of(b)
            turn_h(1)
            pe.wait_ge(s_wr, 16)
            pe.wait_ge(s_sev, NB)
            logits(0)
            turn_h(2)
            logits(1)
            pe.wait_ge(s_x2, 6)
            logits(2)
            pe.wait_ge(s_masks, 2)
            pe.wait_ge(s_m, NT)
            for n in range(NT + 1):
                for m in range(min(n + 1, NT)):
                    mm = pe.matmul(bank[6][:, n * NE:(n + 1) * NE], strict_b if m == n else ones_b, mall[:, m],
                                   start=(m == 0), stop=(m == min(n, NT - 1)))
            mm.then_inc(s_pp, 1)
            def rows(call, width):
                pe.wait_ge(s_hp, call + 1)
                for k in range(KD):
                    for n in TILES:
                        mm = pe.matmul(bank[4 + k // 4][:, (k % 4) * P:(k % 4) * P + width],
                                       h23[:, n, k * P:(k + 1) * P], hp[:, n, 0:width], start=(n == 0), stop=(n == NT - 1))
                mm.then_inc(s_xgt, 1)

            def turn_gates(item):
                pe.wait_ge(s_hg, item * NT + NT)
                for n in TILES:
                    mm = pe.transpose(bank[6][:, n * P:(n + 1) * P], hg[:, n], mat("ident"))
                mm.then_inc(s_gt, 1)

            def combine(m, o, x, free):
                n, a = divmod(o, 2)
                if o == 0:
                    pe.wait_ge(s_yc, m + 1)
                if not free:
                    pe.wait_ge(s_add, m * 6 + (o - 1))
                pe.matmul(bank[2 + o % 2], gT[x][a][:, n * P:(n + 1) * P], y_s, start=True, stop=True).then_inc(s_cmb, 1)

            def bias_rows(x, out, columns):
                for a in range(2):
                    mm = pe.matmul(out[a * BLK:(a + 1) * BLK], sel_sb[0:3 * NE, x, :],
                                   bparts[0:3 * NE, columns + a * 512:columns + (a + 1) * 512], start=True, stop=False,
                                   skip_group_check=True)

            def expert(x, item):
                pe.wait_ge(s_sel, item + 1)
                bias_rows(x, bank[0], 0)
                bias_rows(x, bank[1], F)
                for k in range(KD):
                    pe.wait_ge(s_w[SLOT_OF[k]], item * 16 + 16)
                    for half in range(2):
                        for a in range(2):
                            c = SLOT_OF[k] * SLOT + half * F + a * 512
                            mm = pe.matmul(bank[half][a * BLK:(a + 1) * BLK], xTe[:, k, x * BLK:(x + 1) * BLK],
                                           ring[:, c:c + 512], start=False, stop=(k == KD - 1), skip_group_check=True)
                    mm.then_inc(s_wu, 1)
                pe.drain().then_inc(s_gu, 1)

            def turn_act(item, taken):
                pe.wait_ge(s_gtc, taken)
                pe.wait_ge(s_act, item + 1)
                for j in range(4):
                    mm = pe.transpose(bank[6][:, j * P:(j + 1) * P], a_s[:, j * P:(j + 1) * P], mat("ident"))
                mm.then_inc(s_att, 1)

            def down(x, item, first):
                if not first:
                    pe.wait_ge(s_yc, item)
                bias_rows(x, bank[7], 2 * F)
                pe.wait_ge(s_atr, item + 1)
                for k in range(KD):
                    if k % 2 == 0:
                        pe.wait_ge(s_w[KD + k // 2], item * 16 + 16)
                    for a in range(2):
                        c = (KD + k // 2) * SLOT + (k % 2) * D + a * 512
                        mm = pe.matmul(bank[7][a * BLK:(a + 1) * BLK], actT[:, (k % 4) * P + (k // 4) * BLK:][:, 0:BLK],
                                       ring[:, c:c + 512], start=False, stop=(k == KD - 1), skip_group_check=True)
                    if k % 2 == 1:
                        mm.then_inc(s_wu, 1)
                pe.drain().then_inc(s_dn, 1)

            def pair(p, first, last):
                for x in range(2):
                    item = 2 * p + x
                    alone = first and x == 0
                    if not alone:
                        pe.wait_ge(s_atr, item)
                    turn_gates(item)
                    if x == 0:
                        pe.wait_ge(s_xte, p * 2 + 2)
                    expert(x, item)
                    if not alone:
                        for o in range(2):
                            combine(item - 1, o, 1 - x, first and x == 1)
                    if x == 1:
                        rows(p + 1, BLK if last else P)
                    turn_act(item, item * 2 + 2)
                    if not alone:
                        for o in range(2, 6):
                            combine(item - 1, o, 1 - x, False)
                    down(x, item, alone)

            rows(0, P)
            pe.wait_ge(s_bsplit, 1)
            pair(0, True, False)
            with pe.Fori(1, NPAIR - 1) as p:
                pair(p, False, False)
            pair(NPAIR - 1, False, True)
            pe.wait_ge(s_tabs, 1)
            n_extra = pe.value_load(tab[0:1, NX:NX + 1], min_val=0, max_val=NX)
            with pe.Fori(0, NX_OUTER) as g:
                with pe.If(g * NX_INNER < n_extra):
                    with pe.Fori(0, NX_INNER) as i0:
                        i = g * NX_INNER + i0
                        with pe.If(i < n_extra):
                            pe.wait_ge(s_xte, i * 2 + (NPAIR * 2 + 2))
                            expert(0, i + NE)
                            pe.wait_ge(s_gtc, i * 2 + 2 * NE)
                            for o in range(2):
                                combine(i + (NE - 1), o, 1, False)
                            turn_act(i + NE, i * 2 + 2 * NE)
                            for o in range(2, 6):
                                combine(i + (NE - 1), o, 1, False)
                            down(0, i + NE, False)
                            turn_gates(i + NE)
                            with pe.If(i + 1 < n_extra):
                                rows(i + (NPAIR + 1), BLK)
            pe.wait_ge(s_gtc, n_extra * 2 + 2 * NE)
            for o in range(6):
                combine(n_extra + (NE - 1), o, 1, False)



INPUTS = ["xT", "x_prompt", "x_sample", "state_gdn", "hist_q", "hist_u", "params", "consts", "w_in", "w_out", "g_ffn",
          "g_final", "w_router", "w_gate_up", "b_gate_up", "w_down", "b_down"]
OUTPUTS = {"y": (T, D), "sp": (H, P, P), "ss": (NB, H, P, P), "q_state": (P, QC * 9 * 3), "u_state": (P, CC * 9 * 30)}


def shape_constants():
    j, i = np.arange(P)[:, None], np.arange(P)[None, :]
    same = (j // TS) == (i // TS)
    mats = {"ident": j == i, "ones": (j >= 0) & (i >= 0), "incl_p": i >= j, "incl_s": (i >= j) & same, "later_p": j > i,
            "later_s": (j > i) & same, "strict": j < i}
    for l in range(LEVELS):
        s = 1 << l
        mats[f"level{l}"] = (i // (2 * s) == j // (2 * s)) & (i // s % 2 == 1) & (j // s % 2 == 0)
    cols = np.zeros((P, NXC), np.float32)
    cols[:, X_IOTA:X_IOTA + BLK] = np.arange(BLK)
    cols[:, X_BLK:X_BLK + NB] = (np.arange(P)[:, None] // TS) == np.arange(NB)
    cols[:, X_SEL:X_SEL + NE] = (np.arange(P)[:, None] % NE) == np.arange(NE)
    cols[:, X_SEL + NE] = np.arange(P)
    return np.concatenate([mats[m].astype(np.float32) for m in MATS] + [cols], axis=1)


def kernel(x_prompt, x_sample, state_gdn, state_qkv_conv, state_dwconv, norm_mix_g, w_in, w_conv_qkv, a_log, dt_bias,
           w_onorm, b_glu, w_dw, b_dw, ln_g, ln_b, w_out, norm_ffn_g, w_router, b_router, w_gate_up, b_gate_up, w_down,
           b_down, norm_final_g):
    from concourse import bacc
    from concourse.bass_utils import run_bass_kernel_spmd

    xp = np.asarray(x_prompt).reshape(TP, D)
    xs = np.asarray(x_sample).reshape(NB * TS, D)

    def channels(a, rows):
        return np.asarray(a).reshape(rows, -1, P).transpose(2, 0, 1).reshape(P, -1)

    def rows(a):
        return np.broadcast_to(np.asarray(a).reshape(1, -1), (P, np.asarray(a).size))

    params = np.concatenate([channels(norm_mix_g, 1), channels(w_conv_qkv, QW), channels(w_dw, DW), channels(b_glu, 1),
                             channels(b_dw, 1), channels(ln_g, 1), channels(ln_b, 1), channels(w_onorm, 1), rows(a_log),
                             rows(dt_bias), rows(b_router)], axis=1)

    def history(a, w):
        return np.asarray(a)[0].reshape(NB, w, -1, P).transpose(3, 2, 0, 1).reshape(P, -1)

    arrays = {
        "xT": np.concatenate([xp, xs]).T, "x_prompt": xp, "x_sample": xs, "state_gdn": np.asarray(state_gdn)[0],
        "hist_q": history(state_qkv_conv, QW - 1), "hist_u": history(state_dwconv, DW - 1), "params": params,
        "consts": shape_constants(), "w_in": np.asarray(w_in)[0], "w_out": np.asarray(w_out)[0],
        "g_ffn": np.asarray(norm_ffn_g)[0], "g_final": np.asarray(norm_final_g), "w_router": np.asarray(w_router)[0],
        "w_gate_up": np.asarray(w_gate_up)[0], "b_gate_up": np.asarray(b_gate_up)[0], "w_down": np.asarray(w_down)[0],
        "b_down": np.asarray(b_down)[0],
    }
    arrays = {n: np.ascontiguousarray(a) for n, a in arrays.items()}
    nc = bacc.Bacc("TRN2", target_bir_lowering=False, num_devices=1)
    ins = [nc.dram_tensor(f"in_{n}", arrays[n].shape, F32, kind="ExternalInput").ap() for n in INPUTS]
    outs = [nc.dram_tensor(f"out_{n}", s, F32, kind="ExternalOutput").ap() for n, s in OUTPUTS.items()]
    stream_step(nc, *ins, *outs)
    got = run_bass_kernel_spmd(nc, [{f"in_{n}": arrays[n] for n in INPUTS}], core_ids=[0]).results[0]

    y = np.asarray(got["out_y"])

    def states(a, tiles, w):
        return np.asarray(a).reshape(P, tiles, 9, w).transpose(2, 3, 1, 0).reshape(9, w, tiles * P)

    q, u = states(got["out_q_state"], QC, QW - 1), states(got["out_u_state"], CC, DW - 1)
    return (y[:TP].reshape(1, TP, D), y[TP:].reshape(NB, TS, D), np.asarray(got["out_sp"])[None, None], q[None, 0:1],
            u[None, 0:1], np.asarray(got["out_ss"])[None], q[None, 1:], u[None, 1:])
```
